# Optimizing a Trainium2 kernel written in Bass

```python
import jax
import jax.numpy as jnp
from jax import lax
import numpy as np

D_MODEL = 1024
BATCH = 1
SEQ = 256
DEPTH = 2
DEC_BATCH = 8
DEC_SEQ = 8
PAST_LEN = 2048
PAGE_SIZE = 128

POOL_GROUPS = 4
POOL_GROUP_DIM = 128
POOL_WIDTH = POOL_GROUPS * POOL_GROUP_DIM
POOL_WINDOWS = (2, 4, 8, 16)
POOL_BUF = max(POOL_WINDOWS) - 1
POOL_OUT_GROUP = D_MODEL // POOL_GROUPS
CONV_WIDTH = 512
CONV_KERNEL = 31
CONV_BUF = CONV_KERNEL - 1
DN_HEADS = 4
DN_DK = 128
DN_DV = 128
DN_QK = DN_HEADS * DN_DK
DN_V = DN_HEADS * DN_DV
QKV_WIDTH = 2 * DN_QK + DN_V
SHORT_KERNEL = 4
SHORT_BUF = SHORT_KERNEL - 1
CHUNK = 64
N_BRANCH = 3
POOL_OFF = 0
CONV_A_OFF = POOL_OFF + POOL_WIDTH
CONV_B_OFF = CONV_A_OFF + CONV_WIDTH
QKV_OFF = CONV_B_OFF + CONV_WIDTH
Z_OFF = QKV_OFF + QKV_WIDTH
DNA_OFF = Z_OFF + DN_V
DNB_OFF = DNA_OFF + DN_HEADS
GATE_OFF = DNB_OFF + DN_HEADS
IN_COLS = GATE_OFF + N_BRANCH * D_MODEL
D_FF = 2816
N_EXPERTS = 8
TOP_K = 2
D_FF_EXPERT = 1408
N_DENSE = (DEPTH + 1) // 2
N_MOE = DEPTH // 2
DEEPNORM_ALPHA = (2 * DEPTH) ** 0.25
DEEPNORM_BETA = (8 * DEPTH) ** -0.25
LN_EPS = 1e-5
RMS_EPS = 1e-6
L2_EPS = 1e-6

kernel_name = 'hybrid_pool_conformer_gdn_decoder_step'

def layer_norm(x, g, b):
    xf = x.astype(jnp.float32)
    mu = jnp.mean(xf, -1, keepdims=True)
    var = jnp.mean(jnp.square(xf - mu), -1, keepdims=True)
    return ((xf - mu) * lax.rsqrt(var + LN_EPS) * g.astype(jnp.float32) + b.astype(jnp.float32)).astype(x.dtype)

def l2norm(x):
    xf = x.astype(jnp.float32)
    return (xf * lax.rsqrt(jnp.sum(xf * xf, -1, keepdims=True) + L2_EPS)).astype(x.dtype)

def gated_rmsnorm(o, z, g):
    of = o.astype(jnp.float32)
    of = of * lax.rsqrt(jnp.mean(of * of, -1, keepdims=True) + RMS_EPS) * g.astype(jnp.float32)
    return (of * jax.nn.silu(z.astype(jnp.float32))).astype(o.dtype)

def causal_depthwise(x, buf, w):
    ext = jnp.concatenate([buf.astype(x.dtype), x], axis=1)
    y = lax.conv_general_dilated(ext, w[:, None, :].astype(x.dtype), window_strides=(1,), padding='VALID',
                                 dimension_numbers=('NWC', 'WIO', 'NWC'), feature_group_count=x.shape[-1])
    return y, ext[:, -(w.shape[0] - 1):]

def pool_mixer(u, buf, p0, w_pool, pool_scale):
    B, T, _ = u.shape
    ext = jnp.concatenate([buf.astype(u.dtype), u], axis=1)
    cs = jnp.cumsum(ext.astype(jnp.float32), axis=1)
    cs = jnp.concatenate([jnp.zeros_like(cs[:, :1]), cs], axis=1)
    end = cs[:, POOL_BUF + 1:]
    pos = p0 + jnp.arange(T)
    groups = []
    for gi, w in enumerate(POOL_WINDOWS):
        sl = slice(gi * POOL_GROUP_DIM, (gi + 1) * POOL_GROUP_DIM)
        start = cs[:, POOL_BUF + 1 - w:POOL_BUF + 1 - w + T, sl]
        cnt = jnp.minimum(pos + 1, w).astype(jnp.float32)[None, :, None]
        groups.append((end[..., sl] - start) / cnt)
    pooled = jnp.concatenate(groups, axis=-1)
    d = (pooled - u.astype(jnp.float32)).astype(u.dtype).reshape(B, T, POOL_GROUPS, POOL_GROUP_DIM)
    y = jnp.einsum('btgc,gcd->btgd', d, w_pool).reshape(B, T, D_MODEL) * pool_scale
    return y, ext[:, -POOL_BUF:]

def gated_delta_chunked(q, k, v, g, beta, S0):
    B, T, H, _ = q.shape
    L = min(CHUNK, T)
    n = -(-T // L)
    pad = n * L - T

    def prep(a):
        a = jnp.pad(a.astype(jnp.float32), [(0, 0), (0, pad)] + [(0, 0)] * (a.ndim - 2))
        a = a.reshape((B, n, L) + a.shape[2:])
        a = jnp.moveaxis(a, 3, 2)
        return jnp.moveaxis(a, 1, 0)

    qf, kf, vf, gf, bf = prep(q), prep(k), prep(v), prep(g), prep(beta)
    gc = jnp.cumsum(gf, axis=-1)
    idx = jnp.arange(L)
    causal = idx[:, None] >= idx[None, :]
    strict = (idx[:, None] > idx[None, :]).astype(jnp.float32)
    decay = jnp.exp(jnp.where(causal, gc[..., :, None] - gc[..., None, :], -jnp.inf))
    kb = kf * bf[..., None]
    N = jnp.einsum('...id,...jd->...ij', kb, kf) * decay * strict
    eye = jnp.eye(L, dtype=jnp.float32)
    Tm = lax.linalg.triangular_solve(eye + N, jnp.broadcast_to(eye, N.shape), left_side=True,
                                     lower=True, unit_diagonal=True)
    eg = jnp.exp(gc)
    u = Tm @ (vf * bf[..., None])
    w = Tm @ (kb * eg[..., None])
    attn = jnp.einsum('...id,...jd->...ij', qf, kf) * decay
    qg = qf * eg[..., None]
    kd = kf * jnp.exp(gc[..., -1:] - gc)[..., None]
    glast = eg[..., -1]

    def step(S, xs):
        u_c, w_c, a_c, qg_c, kd_c, gl_c = xs
        vnew = u_c - jnp.einsum('bhld,bhde->bhle', w_c, S)
        o = jnp.einsum('bhld,bhde->bhle', qg_c, S) + jnp.einsum('bhij,bhje->bhie', a_c, vnew)
        S = S * gl_c[..., None, None] + jnp.einsum('bhld,bhle->bhde', kd_c, vnew)
        return S, o

    S_fin, o = lax.scan(step, S0.astype(jnp.float32), (u, w, attn, qg, kd, glast))
    o = jnp.moveaxis(jnp.moveaxis(o, 0, 1), 2, 3).reshape(B, n * L, H, -1)[:, :T]
    return o.astype(q.dtype), S_fin

def token_mixers(h, buf_pool, buf_conv, buf_qkv, S0, p0, w_in, w_pool, pool_scale, w_dw, b_dw,
                 conv_ln_g, conv_ln_b, w_conv_out, w_short, a_log, dt_bias, dn_norm_g, w_dn_out, w_out):
    B, T, _ = h.shape
    p = h @ w_in
    y_pool, nb_pool = pool_mixer(p[..., POOL_OFF:POOL_OFF + POOL_WIDTH], buf_pool, p0, w_pool, pool_scale)
    glu = p[..., CONV_A_OFF:CONV_A_OFF + CONV_WIDTH] * jax.nn.sigmoid(p[..., CONV_B_OFF:CONV_B_OFF + CONV_WIDTH])
    c, nb_conv = causal_depthwise(glu, buf_conv, w_dw)
    c = jax.nn.silu(layer_norm(c + b_dw, conv_ln_g, conv_ln_b))
    y_conv = c @ w_conv_out
    qkv, nb_qkv = causal_depthwise(p[..., QKV_OFF:QKV_OFF + QKV_WIDTH], buf_qkv, w_short)
    qkv = jax.nn.silu(qkv)
    q = l2norm(qkv[..., :DN_QK].reshape(B, T, DN_HEADS, DN_DK)) * (DN_DK ** -0.5)
    k = l2norm(qkv[..., DN_QK:2 * DN_QK].reshape(B, T, DN_HEADS, DN_DK))
    v = qkv[..., 2 * DN_QK:].reshape(B, T, DN_HEADS, DN_DV)
    a_raw = p[..., DNA_OFF:DNA_OFF + DN_HEADS].astype(jnp.float32)
    g = -jnp.exp(a_log.astype(jnp.float32)) * jax.nn.softplus(a_raw + dt_bias.astype(jnp.float32))
    beta = jax.nn.sigmoid(p[..., DNB_OFF:DNB_OFF + DN_HEADS].astype(jnp.float32))
    o, S_new = gated_delta_chunked(q, k, v, g, beta, S0)
    z = p[..., Z_OFF:Z_OFF + DN_V].reshape(B, T, DN_HEADS, DN_DV)
    y_dn = gated_rmsnorm(o.astype(h.dtype), z, dn_norm_g).reshape(B, T, DN_V) @ w_dn_out
    gates = jax.nn.sigmoid(p[..., GATE_OFF:].reshape(B, T, N_BRANCH, D_MODEL))
    mixed = gates[..., 0, :] * y_pool + gates[..., 1, :] * y_conv + gates[..., 2, :] * y_dn
    return mixed @ w_out, nb_pool, nb_conv, nb_qkv, S_new.astype(h.dtype)

def swiglu(x, wg, wu, wd):
    return (jax.nn.silu(x @ wg) * (x @ wu)) @ wd

def moe_swiglu(x, w_router, b_router, wg, wu, wd):
    B, T, _ = x.shape
    xt = x.reshape(B * T, D_MODEL)
    logits = (xt @ w_router).astype(jnp.float32) + b_router.astype(jnp.float32)
    vals, idx = lax.top_k(logits, TOP_K)
    wts = jax.nn.softmax(vals, axis=-1)
    gate = jnp.sum(jax.nn.one_hot(idx, N_EXPERTS, dtype=jnp.float32) * wts[..., None], axis=1)
    out = jnp.zeros((B * T, D_MODEL), jnp.float32)
    for e in range(N_EXPERTS):
        out = out + gate[:, e:e + 1] * swiglu(xt, wg[e], wu[e], wd[e]).astype(jnp.float32)
    return out.astype(x.dtype).reshape(B, T, D_MODEL)

def trunk(x, st_pool, st_conv, st_qkv, st_delta, p0, weights):
    (w_in, w_pool, pool_scale, w_dw, b_dw, conv_ln_g, conv_ln_b, w_conv_out, w_short, a_log, dt_bias,
     dn_norm_g, w_dn_out, w_out, ln1_g, ln1_b, ffn_wg, ffn_wu, ffn_wd, w_router, b_router,
     moe_wg, moe_wu, moe_wd, ln2_g, ln2_b) = weights
    new_pool, new_conv, new_qkv, new_delta = [], [], [], []
    for l in range(DEPTH):
        m, nb_pool, nb_conv, nb_qkv, s_new = token_mixers(
            x, st_pool[l], st_conv[l], st_qkv[l], st_delta[l], p0, w_in[l], w_pool[l], pool_scale[l],
            w_dw[l], b_dw[l], conv_ln_g[l], conv_ln_b[l], w_conv_out[l], w_short[l], a_log[l], dt_bias[l],
            dn_norm_g[l], w_dn_out[l], w_out[l])
        new_pool.append(nb_pool)
        new_conv.append(nb_conv)
        new_qkv.append(nb_qkv)
        new_delta.append(s_new)
        x = layer_norm(DEEPNORM_ALPHA * x + m, ln1_g[l], ln1_b[l])
        j = l // 2
        if l % 2 == 0:
            f = swiglu(x, ffn_wg[j], ffn_wu[j], ffn_wd[j])
        else:
            f = moe_swiglu(x, w_router[j], b_router[j], moe_wg[j], moe_wu[j], moe_wd[j])
        x = layer_norm(DEEPNORM_ALPHA * x + f, ln2_g[l], ln2_b[l])
    return x, jnp.stack(new_pool), jnp.stack(new_conv), jnp.stack(new_qkv), jnp.stack(new_delta)

def setup_inputs(seed: int = 0) -> dict:
    key = jax.random.key(seed)
    ks = iter(jax.random.split(key, 64))

    def nrm(shape, scale):
        return jax.random.normal(next(ks), shape, jnp.float32) * scale

    def gain(shape):
        return 1.0 + nrm(shape, 0.02)

    dt = jnp.exp(jax.random.uniform(next(ks), (DEPTH, DN_HEADS), jnp.float32, np.log(1e-3), np.log(1e-1)))
    return {
        'x_prompt': nrm((BATCH, SEQ, D_MODEL), 1.0),
        'x_sample': nrm((DEC_BATCH, DEC_SEQ, D_MODEL), 1.0),
        'state_pool': nrm((DEPTH, DEC_BATCH, POOL_BUF, POOL_WIDTH), 1.0),
        'state_conv': nrm((DEPTH, DEC_BATCH, CONV_BUF, CONV_WIDTH), 0.5),
        'state_qkv_conv': nrm((DEPTH, DEC_BATCH, SHORT_BUF, QKV_WIDTH), 1.0),
        'state_delta': nrm((DEPTH, DEC_BATCH, DN_HEADS, DN_DK, DN_DV), 0.1),
        'w_in': nrm((DEPTH, D_MODEL, IN_COLS), D_MODEL ** -0.5),
        'w_pool': nrm((DEPTH, POOL_GROUPS, POOL_GROUP_DIM, POOL_OUT_GROUP), POOL_GROUP_DIM ** -0.5),
        'pool_scale': gain((DEPTH, D_MODEL)),
        'w_dw': nrm((DEPTH, CONV_KERNEL, CONV_WIDTH), CONV_KERNEL ** -0.5),
        'b_dw': nrm((DEPTH, CONV_WIDTH), 0.02),
        'conv_ln_g': gain((DEPTH, CONV_WIDTH)),
        'conv_ln_b': nrm((DEPTH, CONV_WIDTH), 0.02),
        'w_conv_out': nrm((DEPTH, CONV_WIDTH, D_MODEL), CONV_WIDTH ** -0.5),
        'w_short': nrm((DEPTH, SHORT_KERNEL, QKV_WIDTH), SHORT_KERNEL ** -0.5),
        'a_log': jnp.log(jax.random.uniform(next(ks), (DEPTH, DN_HEADS), jnp.float32, 1.0, 16.0)),
        'dt_bias': dt + jnp.log(-jnp.expm1(-dt)),
        'dn_norm_g': gain((DEPTH, DN_DV)),
        'w_dn_out': nrm((DEPTH, DN_V, D_MODEL), DN_V ** -0.5),
        'w_out': nrm((DEPTH, D_MODEL, D_MODEL), DEEPNORM_BETA * D_MODEL ** -0.5),
        'ln1_g': gain((DEPTH, D_MODEL)),
        'ln1_b': nrm((DEPTH, D_MODEL), 0.02),
        'ffn_wg': nrm((N_DENSE, D_MODEL, D_FF), D_MODEL ** -0.5),
        'ffn_wu': nrm((N_DENSE, D_MODEL, D_FF), D_MODEL ** -0.5),
        'ffn_wd': nrm((N_DENSE, D_FF, D_MODEL), DEEPNORM_BETA * D_FF ** -0.5),
        'w_router': nrm((N_MOE, D_MODEL, N_EXPERTS), D_MODEL ** -0.5),
        'b_router': nrm((N_MOE, N_EXPERTS), 0.01),
        'moe_wg': nrm((N_MOE, N_EXPERTS, D_MODEL, D_FF_EXPERT), D_MODEL ** -0.5),
        'moe_wu': nrm((N_MOE, N_EXPERTS, D_MODEL, D_FF_EXPERT), D_MODEL ** -0.5),
        'moe_wd': nrm((N_MOE, N_EXPERTS, D_FF_EXPERT, D_MODEL), DEEPNORM_BETA * D_FF_EXPERT ** -0.5),
        'ln2_g': gain((DEPTH, D_MODEL)),
        'ln2_b': nrm((DEPTH, D_MODEL), 0.02),
    }

def reference(x_prompt, x_sample, state_pool, state_conv, state_qkv_conv, state_delta,
              w_in, w_pool, pool_scale, w_dw, b_dw, conv_ln_g, conv_ln_b, w_conv_out,
              w_short, a_log, dt_bias, dn_norm_g, w_dn_out, w_out, ln1_g, ln1_b,
              ffn_wg, ffn_wu, ffn_wd, w_router, b_router, moe_wg, moe_wu, moe_wd, ln2_g, ln2_b):
    weights = (w_in, w_pool, pool_scale, w_dw, b_dw, conv_ln_g, conv_ln_b, w_conv_out, w_short, a_log,
               dt_bias, dn_norm_g, w_dn_out, w_out, ln1_g, ln1_b, ffn_wg, ffn_wu, ffn_wd, w_router,
               b_router, moe_wg, moe_wu, moe_wd, ln2_g, ln2_b)
    nb = x_prompt.shape[0]
    dt_ = x_prompt.dtype
    y_prompt, pool_p, conv_p, qkv_p, delta_p = trunk(
        x_prompt,
        jnp.zeros((DEPTH, nb, POOL_BUF, POOL_WIDTH), dt_),
        jnp.zeros((DEPTH, nb, CONV_BUF, CONV_WIDTH), dt_),
        jnp.zeros((DEPTH, nb, SHORT_BUF, QKV_WIDTH), dt_),
        jnp.zeros((DEPTH, nb, DN_HEADS, DN_DK, DN_DV), dt_),
        0, weights)
    y_sample, pool_s, conv_s, qkv_s, delta_s = trunk(
        x_sample, state_pool, state_conv, state_qkv_conv, state_delta, PAST_LEN, weights)
    return (y_prompt, y_sample, pool_p, conv_p, qkv_p, delta_p, pool_s, conv_s, qkv_s, delta_s)


_drawn_inputs = setup_inputs


def setup_inputs(seed=0):
    import zlib

    import numpy as np

    out = dict(_drawn_inputs(seed))
    spreads = {}
    factors = {'pool_scale': 5.736,
     'b_dw': 4.768,
     'conv_ln_g': 5.531,
     'conv_ln_b': 5.092,
     'dn_norm_g': 7.09,
     'b_router': 5.096}
    for name, (base, spread) in spreads.items():
        noise = np.random.default_rng([zlib.crc32(name.encode()), seed]).standard_normal(out[name].shape)
        drawn = base * np.exp(spread * noise) if base else spread * noise
        out[name] = jnp.asarray(drawn.astype(out[name].dtype))
    for name, factor in factors.items():
        out[name] = (out[name] * factor).astype(out[name].dtype)
    return out
```

```python
import numpy as np

DEPTH, D, SEQ, NSEQ, TS = 2, 1024, 256, 8, 8
T = SEQ + NSEQ * TS
KT = D // 128
H = 4
CK, SK_, PB = 31, 4, 15
CB, SB = CK - 1, SK_ - 1
FT = 11
NE = 8
ALPHA = (2 * DEPTH) ** 0.25
CHUNK = 64
WINDOWS = (2, 4, 8, 16)
GATE_OFF = 3592
UNIT = 1024
FUNIT = FT * 128
N_QKV, N_AB, N_POOL, N_Z, N_G, N_YP, N_YC, N_YD, N_WO = 12, 8, 4, 4, 24, 1, 4, 4, 8
U_AB = N_QKV
U_POOL = U_AB + N_AB
U_Z = U_POOL + N_POOL
U_G = U_Z + N_Z
U_YP = U_G + N_G
U_YC = U_YP + N_YP
U_YD = U_YC + N_YC
U_WO = U_YD + N_YD
NU = U_WO + N_WO
NB = (NU + 1) // 2
FU = 2 * FT + 8
FW = 2 * FT * UNIT + 8 * FUNIT

PAR = {}
_at = 0
for _n, _w in (("w_dw", 4 * CK), ("b_dw", 4), ("cg", 4), ("cb", 4), ("w_short", 12 * SK_), ("pscale", 8),
               ("dn_g", 1), ("ln1_g", 8), ("ln1_b", 8), ("ln2_g", 8), ("ln2_b", 8), ("a_log", 4), ("dt", 4)):
    PAR[_n] = (_at, _w)
    _at += _w
NPAR = _at

CON = {}
_at = 0
for _n, _w in (("ident", 128), ("ones", 128), ("cum_p", 128), ("blk_p", 128), ("strict_p", 128), ("cum_s", 64),
               ("blk_s", 64), ("strict_s", 64), ("ind_p", 8), ("ind_s", 8), ("lev", 6 * 128), ("lev0t", 128),
               ("invcnt", 64), ("before", 64)):
    CON[_n] = (_at, _w)
    _at += _w
NCON = _at


def build(nc, io):
    import concourse.bass as bass
    from concourse import mybir
    from contextlib import ExitStack

    f32, f32r = mybir.dt.float32, mybir.dt.float32r
    ALU, ACT, AX = mybir.AluOpType, mybir.ActivationFunctionType, mybir.AxisListType

    ctx = ExitStack()
    with ctx:
        base = (nc.sbuf_base + 31) // 32 * 32

        def size(shape):
            return (int(np.prod(shape[1:])) * 4 + 31) // 32 * 32

        def lay(at, *plan):
            out = []
            for name, shape, dt in plan:
                assert base + at + size(shape) <= nc.sbuf_usable_end, (name, base + at + size(shape))
                out.append(nc.alloc_sbuf_tensor_at(name, shape, dt, offset=base + at))
                at += size(shape)
            return out + [at]

        (con, par, X, Xh, Xl, raw, Wh, Wl, wab, wrt, brt, sq, std, rstd, ab, sc, gs, tmp3, TOP) = lay(
            0, ("con", [128, NCON], f32), ("par", [128, DEPTH, NPAR], f32),
            ("X", [128, KT, T], f32),
            ("Xh", [128, KT, T], f32r), ("Xl", [128, KT, T], f32r),
            ("raw", [128, 3, 2, UNIT], f32),
            ("Wh", [128, 3, UNIT], f32r), ("Wl", [128, 3, UNIT], f32r),
            ("wab", [128, KT, 8], f32), ("wrt", [128, KT, NE], f32), ("brt", [128, NE], f32),
            ("sq", [128, 2, T], f32), ("std", [128, T], f32), ("rstd", [128, T], f32),
            ("ab", [128, 3, 8], f32),
            ("sc", [128, 9, 3, 4], f32),
            ("gs", [128, 4, 8], f32),
            ("tmp3", [128, 3, 3, 4], f32))
        (G, EXT) = lay(TOP, ("G", [128, 24, T], f32))
        (cxp, cxs, pxp, pxs, E1) = lay(EXT, ("cxp", [128, H, CB + SEQ], f32), ("cxs", [128, H, NSEQ, CB + TS], f32),
                                       ("pxp", [128, H, PB + SEQ], f32), ("pxs", [128, H, NSEQ, PB + TS], f32))
        (Ss, E2) = lay(EXT, ("Ss", [128, H, NSEQ, 128], f32))
        (qxp, qxs, qh, qT, kT, vT, Z, S, oT, tp, ts, TEMP) = lay(
            max(E1, E2), ("qxp", [128, 2, SB + SEQ], f32), ("qxs", [128, 2, NSEQ, SB + TS], f32),
            ("qh", [128, 12, NSEQ, SB], f32),
            ("qT", [128, H, T], f32), ("kT", [128, H, T], f32), ("vT", [128, H, T], f32), ("Z", [128, H, T], f32),
            ("S", [128, H, 128], f32), ("oT", [128, H, T], f32),
            ("tp", [128, 12, SB], f32), ("ts", [128, 12, NSEQ, SB], f32))
        (gb, dec, decT, eg, NN, NT, XX, YY, T1, vb, kb, kd, uu, wT, aT, vn, E3) = lay(
            TEMP, *[(n, [128, H, 128], f32) for n in ("gb", "dec", "decT", "eg", "NN", "NT", "XX", "YY", "T1", "vb",
                                                      "kb", "kd", "uu", "wT", "aT", "vn")])
        (vblk, _) = lay(TEMP, ("vblk", [64, NSEQ, 128], f32))
        (cacc, _) = lay(TEMP - size([1, 12, SB]) - size([1, 12, NSEQ, SB]) - size([1, H, T]), ("cacc", [128, H, T], f32))
        (nrm, pw, dh, dl, yb, tt, E4) = lay(TEMP, ("nrm", [128, 8, T], f32), ("pw", [128, 2, PB + SEQ], f32),
                                            ("dh", [128, H, T], f32r), ("dl", [128, H, T], f32r),
                                            ("yb", [128, 2, T], f32), ("tt", [128, 2, T], f32))
        (Mh, Ml, E5) = lay(TEMP, ("Mh", [128, KT, T], f32r), ("Ml", [128, KT, T], f32r))
        (rmsr, _) = lay(TEMP, ("rmsr", [128, H, T], f32))
        (fh, fl, fraw, HT) = lay(TOP, ("fh", [128, 3, FUNIT], f32r), ("fl", [128, 3, FUNIT], f32r),
                                 ("fraw", [128, 5, FUNIT], f32))
        (Hh, Hl, acc, gbc, sg, hf, E6) = lay(HT, ("Hh", [128, FT, T], f32r), ("Hl", [128, FT, T], f32r),
                                             ("acc", [128, KT, T], f32), ("gbc", [128, NE, T], f32),
                                             ("sg", [128, 2, T], f32), ("hf", [128, 2, T], f32))
        (gexp, rk, rc, _) = lay(HT, ("gexp", [128, NE, 128], f32), ("rk", [128, 8, 3, NE], f32),
                                ("rc", [128, 2, 3, NE, NE], f32))

        PS = [ctx.enter_context(nc.psum_tensor(f"ps{i}", [128, 512], f32)) for i in range(8)]

        def sem(name):
            return ctx.enter_context(nc.semaphore(name))

        def C(name, rows=128):
            o, w = CON[name]
            return con[0:rows, o:o + w]

        def P(l, name, i=0):
            o, _ = PAR[name]
            return par[:, l, o + i:o + i + 1]

        def over(ap, n):
            return ap.unsqueeze(1).broadcast_to([ap.shape[0], n, ap.shape[1]])

        def along(ap, n):
            return ap.unsqueeze(2).broadcast_to([ap.shape[0], ap.shape[1], n])

        in_ready, state_in, ss_in, out_done = sem("in_ready"), sem("state_in"), sem("ss_in"), sem("out_done")
        raw_in = [sem(f"raw_in{i}") for i in range(3)]
        w_hi, w_lo, unit_done = sem("w_hi"), sem("w_lo"), sem("unit_done")
        evict_act, evict_dve = sem("evict_act"), sem("evict_dve")
        hist_zero, vch, ach = sem("hist_zero"), sem("vch"), sem("ach")
        qc_done, qt_done, qs_done, sqr_done = sem("qc_done"), sem("qt_done"), sem("qs_done"), sem("sqr_done")
        ssq_done, nrm_copied, nrm_root, qk_ready = sem("ssq_done"), sem("nrm_copied"), sem("nrm_root"), sem("qk_ready")
        tails_done = sem("tails_done")
        ab_done, ab_copied, ab_act, ab_dve = sem("ab_done"), sem("ab_copied"), sem("ab_act"), sem("ab_dve")
        glu_done, conv_done, z_done, d_made = sem("glu_done"), sem("conv_done"), sem("z_done"), sem("d_made")
        ln_sum, ln_cent, ln_sq, ln_sqs = sem("ln_sum"), sem("ln_cent"), sem("ln_sq"), sem("ln_sqs")
        ln_std, ln_norm, aff_done = sem("ln_std"), sem("ln_norm"), sem("aff_done")
        yp_seen = sem("yp_seen")
        csig, csilu = sem("csig"), sem("csilu")
        split_hi, split_lo = sem("split_hi"), sem("split_lo")
        yp_done, mix_done = sem("yp_done"), sem("mix_done")
        dmm, d_act, d_dve = sem("dmm"), sem("d_act"), sem("d_dve")
        gb_made, dif_made, kdec_made, eg_made = sem("gb_made"), sem("dif_made"), sem("kdec_made"), sem("eg_made")
        arg_made, dec_made, xy0_made = sem("arg_made"), sem("dec_made"), sem("xy0_made")
        s_zero, rms_sq, rms_sum, rms_root, o_made = sem("s_zero"), sem("rms_sq"), sem("rms_sum"), sem("rms_root"), sem("o_made")
        vblk_made = sem("vblk_made")
        fraw_in = [sem(f"fraw_in{i}") for i in range(5)]
        f_hi, f_lo, f_done = sem("f_hi"), sem("f_lo"), sem("f_done")
        f_silu, f_uev, f_dev, f_h = sem("f_silu"), sem("f_uev"), sem("f_dev"), sem("f_h")
        f_hhi, f_hlo, acc_init = sem("f_hhi"), sem("f_hlo"), sem("acc_init")
        rt_done, rt_top, rt_exp, gx_made, gb_done, gb_copied = (
            sem("rt_done"), sem("rt_top"), sem("rt_exp"), sem("gx_made"), sem("gb_done"), sem("gb_copied"))
        block = ctx.enter_context(nc.Block())

        def rows(t):
            return 128 if t < 2 else 64

        def cols(t):
            return slice(128 * t, 128 * t + rows(t))

        def groups_of(u):
            return ["act"] if u < U_YP else ["act"] * 8 if u < U_YC else ["dve"] * 2 if u < U_WO else ["dve"]

        GROUPS = [k for u in range(NU) for k in groups_of(u)]
        FIRST = [sum(len(groups_of(v)) for v in range(u)) for u in range(NU)]

        def evicted(l, g):
            k = GROUPS[g]
            return (evict_act if k == "act" else evict_dve), l * GROUPS.count(k) + GROUPS[:g + 1].count(k)

        def bank_free(eng, l, g):
            n = l * len(GROUPS) + g - 4
            if n >= 0:
                eng.wait_ge(*evicted(*divmod(n, len(GROUPS))))

        def gbank(l, g):
            return PS[(l * len(GROUPS) + g) % 4]

        def products(t):
            out = [("gc", "act"), ("R", "dve"), ("kt", "dve"), ("vt", "dve"), ("G", "dve"), ("A", "dve"), ("NT", "act")]
            top = 5 if t < 2 else 2
            for s in range(1, top + 1):
                out += [(f"t{s}", "dve")] + ([(f"x{s}", "dve")] if s < top else []) + [(f"y{s}", "dve")]
            if t < 2:
                out += [("u", "act"), ("w", "act")]
                for c in range(2):
                    out += [(f"p{c}", "dve"), (f"o{c}", "act"), (f"s{c}", "dve")]
            else:
                out += [("u", "act"), ("w", "act"), ("p", "dve"), ("v", "act"), ("o", "act")]
                out += [(f"s{h}{b}", "dve") for h in range(H) for b in range(2)]
            return out

        PROD = [(t, n, e) for t in range(3) for n, e in products(t)]
        KINDS = [e for _, _, e in PROD]

        def number(l, t, name):
            return l * len(PROD) + [(a, b) for a, b, _ in PROD].index((t, name))

        def consumed(j):
            l, i = divmod(j, len(PROD))
            return (d_act if KINDS[i] == "act" else d_dve), l * KINDS.count(KINDS[i]) + KINDS[:i + 1].count(KINDS[i])

        def read(l, t, name):
            return consumed(number(l, t, name))

        def dbank(j):
            return PS[4 + j % 4]

        SPL, NSPL = {"d": 0, "c": 4, "o": 8, "m": 12, "x1": 20, "x2": 28}, 36

        def split(l, name, i):
            return 8 + l * NSPL + SPL[name] + i + 1

        def x_split(l):
            return 8 if l == 0 else split(l - 1, "x2", 7)

        LNT = [4, 8, 8]

        def ln_at(l, w):
            return l * sum(LNT) + sum(LNT[:w])

        def e_range(l):
            return (0, 2) if l == 0 else (2, 2 + NE)

        STEPS = []
        for u in range(N_QKV):
            STEPS += [("unit", u), ("qconv", u)] + ([("qact", u - 1)] if u else []) + ([("ssq", u - 2)] if 2 <= u < 10 else [])
        STEPS += [("unit", U_AB), ("qact", 11), ("ab", 0)]
        for i in range(1, N_AB):
            STEPS += [("unit", U_AB + i)] + ([("glu", i // 2)] if i % 2 else [])
        STEPS += [("norms", 0)]
        STEPS += [("unit", U_POOL + i) for i in range(N_POOL)]
        STEPS += [("unit", U_Z + i) for i in range(N_Z)]
        STEPS += [("pool", i) for i in range(4)]
        STEPS += [("conv", i) for i in range(4)]
        STEPS += [("unit", U_G + i) for i in range(24)]
        STEPS += [("unit", U_YP), ("ln", 0)]
        STEPS += [("unit", U_YC + i) for i in range(4)]
        for t in range(3):
            STEPS += [("delta", (t, n)) for n, _ in products(t)]
        STEPS += [("rms", 0)]
        STEPS += [("unit", U_YD + i) for i in range(4)]
        STEPS += [("mix", i) for i in range(8)]
        STEPS += [("unit", U_WO + i) for i in range(8)]
        STEPS += [("ln", 1)]

        @block.sync
        def _(sp):
            for dst, src in ((X[:, :, :], io["x"]), (con[:, :], io["con"]), (wrt[:, :, :], io["w_router"]),
                             (par[:, :, :], io["par"]), (brt[:, :], io["b_router"])):
                sp.dma_start(dst, src).then_inc(in_ready, 16)

            def load_block(l, b):
                n = l * NB + b
                if n >= 3:
                    m, c = divmod(n - 3, NB)
                    sp.wait_ge(w_lo, m * NU + min(2 * c + 2, NU))
                w = min(2, NU - 2 * b)
                sp.dma_start(raw[:, n % 3, 0:w, :], io["w_mix"][l, :, 2 * b:2 * b + w, :]).then_inc(raw_in[n % 3], 16)

            for l in range(DEPTH):
                for b in range(2):
                    load_block(l, b)
                if l:
                    sp.wait_ge(split_lo, x_split(l))
                for dst, src in ((wab[:, :, :], io["w_ab"][l]), (qh[:, :, :, :], io["st_qkv"][l]),
                                 (cxs[:, :, :, :], io["st_conv"][l]), (pxs[:, :, :, :], io["st_pool"][l])):
                    sp.dma_start(dst, src).then_inc(state_in, 16)
                for b in range(2, NB):
                    load_block(l, b)
                    if b == (U_G + 20) // 2:
                        sp.wait_ge(glu_done, 4 * (l + 1))
                        sp.wait_ge(*evicted(l, U_Z))
                        sp.wait_ge(tails_done, 12 * (l + 1))
                        for dst, src in ((io["o_conv_p"][l], cxp[:, :, SEQ:]), (io["o_conv_s"][l], cxs[:, :, :, :]),
                                         (io["o_pool_p"][l], pxp[:, :, SEQ:]), (io["o_pool_s"][l], pxs[:, :, :, :]),
                                         (io["o_qkv_p"][l], tp[:, :, :]), (io["o_qkv_s"][l], ts[:, :, :, :])):
                            sp.dma_start(dst, src).then_inc(out_done, 16)
                    if b == (U_YP + 2) // 2:
                        sp.wait_ge(d_made, 4 * (l + 1))
                        sp.wait_ge(conv_done, 4 * (l + 1))
                        sp.wait_ge(out_done, (l * 8 + 6) * 16)
                        sp.dma_start(Ss[:, :, :, :], io["st_delta"][l]).then_inc(ss_in, 16)
                    if b == (U_WO + 0) // 2:
                        sp.wait_ge(*read(l, 1, "s1"))
                        sp.dma_start(io["o_delta_p"][l], S[:, :, :]).then_inc(out_done, 16)
                        sp.wait_ge(*read(l, 2, "s31"))
                        sp.dma_start(io["o_delta_s"][l], Ss[:, :, :, :]).then_inc(out_done, 16)
                sp.wait_ge(out_done, (l + 1) * 8 * 16)
                sp.wait_ge(split_lo, split(l, "m", 7))
                with sp.Fori(*e_range(l)) as e:
                    for i in range(FU):
                        sp.wait_ge(f_lo, e * FU + (i + 1))
                        o = i * UNIT if i < 2 * FT else 2 * FT * UNIT + (i - 2 * FT) * FUNIT
                        w = UNIT if i < 2 * FT else FUNIT
                        sp.dma_start(fraw[:, i % 5, 0:w],
                                     io["w_ffn"][bass.ds(e, 1), :, o:o + w].rearrange("e p n -> p (e n)"))\
                            .then_inc(fraw_in[i % 5], 16)
            sp.wait_ge(aff_done, DEPTH * sum(LNT))
            sp.dma_start(io["y"], X[:, :, :]).then_inc(out_done, 16)
            sp.wait_ge(out_done, (8 * DEPTH + 1) * 16)

        @block.gpsimd
        def _(pool):
            pool.sem_inc(f_lo, 5)
            for l in range(DEPTH):
                if l:
                    pool.wait_ge(split_lo, x_split(l))
                for z in (cxp[:, :, 0:CB], pxp[:, :, 0:PB], qxp[:, :, 0:SB], ab[:, :, :]):
                    pool.memset(z, 0.0).then_inc(hist_zero, 1)
                for u in range(NU):
                    n, b = l * NU + u, l * NB + u // 2
                    pool.wait_ge(w_hi, n + 1)
                    pool.tensor_tensor(Wl[:, n % 3, :], raw[:, b % 3, u % 2, :],
                                       Wh[:, n % 3, :].bitcast(f32), ALU.subtract).then_inc(w_lo, 1)
                with pool.Fori(*e_range(l)) as e:
                    for i in range(FU):
                        w = UNIT if i < 2 * FT else FUNIT
                        pool.wait_ge(f_hi, e * FU + (i + 1))
                        pool.tensor_tensor(fl[:, i % 3, 0:w], fraw[:, i % 5, 0:w],
                                           fh[:, i % 3, 0:w].bitcast(f32), ALU.subtract).then_inc(f_lo, 1)

        @block.scalar
        def _(act):
            steps = [0]

            def link(ins):
                steps[0] += 1
                ins.then_inc(ach, 1)
                act.wait_ge(ach, steps[0])

            def head(n):
                if n >= DEPTH * NU:
                    return
                l, u = divmod(n, NU)
                b = l * NB + u // 2
                act.wait_ge(raw_in[b % 3], (b // 3 + 1) * 16)
                if n >= 3:
                    act.wait_ge(unit_done, n - 2)
                act.activation(Wh[:, n % 3, :], raw[:, b % 3, u % 2, :], ACT.Copy).then_inc(w_hi, 1)

            def unit(l, u):
                n = l * NU + u
                if u < U_WO + 6:
                    head(n + 2)
                if u >= U_YP:
                    return
                act.wait_ge(unit_done, n + 1)
                bank = gbank(l, FIRST[u])
                pr, sa = bank[:, 0:SEQ], bank[:, SEQ:T].rearrange("p (b t) -> p b t", b=NSEQ)
                if u < U_AB:
                    if u >= 2:
                        act.wait_ge(qc_done, l * 12 + u - 1)
                    if u == 0:
                        act.wait_ge(hist_zero, 4 * (l + 1))
                        act.wait_ge(state_in, 64 * (l + 1))
                    act.activation(qxs[:, u % 2, :, 0:SB], qh[:, u, :, :], ACT.Copy)
                    act.activation(tp[:, u, :], bank[:, SEQ - SB:SEQ], ACT.Copy)
                    act.activation(ts[:, u, :, :], sa[:, :, TS - SB:TS], ACT.Copy).then_inc(tails_done, 1)
                    act.activation(qxp[:, u % 2, SB:], pr, ACT.Copy)
                    act.activation(qxs[:, u % 2, :, SB:], sa, ACT.Copy).then_inc(evict_act, 1)
                elif u < U_POOL:
                    i = (u - U_AB) // 2
                    if (u - U_AB) % 2 == 0:
                        act.activation(cxp[:, i, CB:], pr, ACT.Copy, scale=0.5)
                        act.activation(cxs[:, i, :, CB:], sa, ACT.Copy, scale=0.5).then_inc(evict_act, 1)
                    else:
                        if i:
                            act.wait_ge(glu_done, l * 4 + i)
                        act.activation(std[:, :], bank[:, 0:T], ACT.Tanh, scale=0.5).then_inc(evict_act, 1)
                elif u < U_Z:
                    act.activation(pxp[:, u - U_POOL, PB:], pr, ACT.Copy)
                    act.activation(pxs[:, u - U_POOL, :, PB:], sa, ACT.Copy).then_inc(evict_act, 1)
                elif u < U_G:
                    i = u - U_Z
                    if i >= 2:
                        act.wait_ge(z_done, l * 4 + i - 1)
                    act.activation(Z[:, i, :], bank[:, 0:T], ACT.Copy)
                    act.activation(sq[:, i % 2, :], bank[:, 0:T], ACT.Tanh, scale=0.5).then_inc(evict_act, 1)
                else:
                    act.activation(G[:, u - U_G, :], bank[:, 0:T], ACT.Tanh, scale=0.5).then_inc(evict_act, 1)

            def pooled_out(l):
                for m in range(8):
                    g = FIRST[U_YP] + m
                    act.wait_ge(yp_seen, l * 8 + m + 1)
                    if m >= 2:
                        act.wait_ge(yp_done, l * 8 + m - 1)
                    act.activation(yb[:, m % 2, :], gbank(l, g)[:, 0:T], ACT.Copy, scale=P(l, "pscale", m))\
                        .then_inc(evict_act, 1)

            def qact(l, i):
                dst = (qT, kT, vT)[i // 4][:, i % 4, :]
                act.wait_ge(qc_done, l * 12 + i + 1)
                if i >= 2:
                    act.wait_ge(qs_done, l * 12 + i - 1)
                act.activation(yb[:, i % 2, :], dst, ACT.Tanh, scale=0.5).then_inc(qt_done, 1)
                if i < 8:
                    act.wait_ge(qs_done, l * 12 + i + 1)
                    if i >= 2:
                        act.wait_ge(ssq_done, l * 8 + i - 1)
                    act.activation(sq[:, i % 2, :], dst, ACT.Square).then_inc(sqr_done, 1)

            def ssq(l, i):
                act.wait_ge(ssq_done, l * 8 + i + 1)
                act.activation(nrm[:, i, :], PS[4 + i % 2][:, 0:T], ACT.Copy).then_inc(nrm_copied, 1)

            def norms(l):
                act.wait_ge(nrm_copied, 8 * (l + 1))
                act.activation(nrm[:, :, :], nrm[:, :, :], ACT.Sqrt, bias=4e-6).then_inc(nrm_root, 1)

            def ab_part(l):
                act.wait_ge(ab_done, l + 1)
                for t in range(3):
                    ins = act.activation(ab[0:rows(t), t, :], PS[6][0:rows(t), 8 * t:8 * t + 8], ACT.Copy)
                ins.then_inc(ab_copied, 1)
                act.wait_ge(ab_dve, 2 * l + 1)
                link(act.activation(tmp3[:, 1, :, :], tmp3[:, 0, :, :], ACT.Abs))
                link(act.activation(tmp3[:, 1, :, :], tmp3[:, 1, :, :], ACT.Exp, scale=-1.0))
                act.activation(tmp3[:, 1, :, :], tmp3[:, 1, :, :], ACT.Ln, bias=1.0).then_inc(ab_act, 1)
                act.activation(tmp3[:, 2, 0, :], par[:, l, PAR["a_log"][0]:PAR["a_log"][0] + 4], ACT.Exp).then_inc(ab_act, 1)
                act.activation(sc[:, 1, :, :], ab[:, :, 4:8], ACT.Tanh, scale=0.5).then_inc(ab_act, 1)

            def ln(l, w):
                k, n0, n = LNT[w], ln_at(l, w), 3 * l + w
                src = (cacc, X, acc)[w]
                for m in range(k):
                    act.wait_ge(ln_cent, n0 + m + 1)
                    if m >= 2:
                        act.wait_ge(ln_sqs, n0 + m - 1)
                    act.activation(sq[:, m % 2, :], src[:, m, :], ACT.Square).then_inc(ln_sq, 1)
                act.wait_ge(ln_sqs, n0 + k)
                act.activation(std[:, :], PS[7][:, 0:T], ACT.Sqrt, scale=1.0 / (128 * k),
                               bias=(1e-5, 4e-5, 1e-5)[w]).then_inc(ln_std, 1)
                gname, bname = (("cg", "cb"), ("ln1_g", "ln1_b"), ("ln2_g", "ln2_b"))[w]
                dst = (cacc, X, X)[w]
                for m in range(k):
                    act.wait_ge(ln_norm, n0 + m + 1)
                    act.activation(dst[:, m, :], dst[:, m, :], ACT.Identity, scale=P(l, gname, m), bias=P(l, bname, m))\
                        .then_inc(aff_done, 1)
                if w == 0:
                    for m in range(k):
                        act.wait_ge(aff_done, n0 + m + 1)
                        if m >= 2:
                            act.wait_ge(csilu, l * 4 + m - 1)
                        act.activation(sq[:, m % 2, :], cacc[:, m, :], ACT.Tanh, scale=0.5).then_inc(csig, 1)
                    for m in range(k):
                        act.wait_ge(csilu, l * 4 + m + 1)
                        act.activation(Xh[:, m, :], cacc[:, m, :], ACT.Copy, scale=0.5).then_inc(split_hi, 1)
                elif (l, w) != (DEPTH - 1, 2):
                    act.wait_ge(aff_done, n0 + k)
                    for m in range(k):
                        act.activation(Xh[:, m, :], X[:, m, :], ACT.Copy).then_inc(split_hi, 1)

            def pool_head(l, i):
                act.wait_ge(d_made, l * 4 + i + 1)
                act.activation(dh[:, i, :], tt[:, i % 2, :], ACT.Copy).then_inc(split_hi, 1)

            def delta(l, t, name):
                j, r = number(l, t, name), rows(t)
                b = dbank(j)
                b4 = b[:, 0:4 * r].rearrange("p (h n) -> p h n", h=H)
                if dict(products(t)).get(name) == "act" or name == "R":
                    act.wait_ge(dmm, j + 1)
                inc = consumed(j)[0]
                if name == "gc":
                    act.activation(sc[0:r, 3:5, t, :], b[0:r, 0:8].rearrange("p (a h) -> p a h", a=2), ACT.Copy)
                    act.activation(sc[0:r, 5, t, :], b[0:r, 0:4], ACT.Exp)
                    act.activation(gs[:, :, :], b[:, 16:48].rearrange("p (h n) -> p h n", h=H), ACT.Exp).then_inc(inc, 1)
                    act.wait_ge(dif_made, l * 3 + t + 1)
                    act.activation(sc[0:r, 7, t, :], sc[0:r, 7, t, :], ACT.Exp).then_inc(kdec_made, 1)
                elif name == "R":
                    act.activation(eg[:, :, 0:r], b4, ACT.Exp).then_inc(eg_made, 1)
                    act.wait_ge(arg_made, l * 3 + t + 1)
                    act.activation(dec[0:r, :, 0:r], dec[0:r, :, 0:r], ACT.Exp, scale=-1.0)
                    act.activation(decT[0:r, :, 0:r], decT[0:r, :, 0:r], ACT.Exp).then_inc(dec_made, 1)
                elif name == "NT":
                    act.activation(NT[0:r, :, 0:r], b4[0:r], ACT.Copy).then_inc(inc, 1)
                elif name == "u":
                    if t < 2:
                        act.activation(uu[:, :, :], b4, ACT.Copy).then_inc(inc, 1)
                    else:
                        act.activation(uu[:, :, 0:r], b4, ACT.Copy).then_inc(inc, 1)
                elif name == "w":
                    act.activation(wT[:, :, 0:r], b4, ACT.Copy).then_inc(inc, 1)
                elif name == "v":
                    act.activation(vn[0:r, :, :], b[0:r, :].rearrange("p (h n) -> p h n", h=H), ACT.Copy).then_inc(inc, 1)
                elif name in ("o0", "o1", "o"):
                    c0 = 128 * t + (64 if name == "o1" else 0)
                    act.activation(oT[:, :, c0:c0 + 64], b[:, 0:256].rearrange("p (h n) -> p h n", h=H), ACT.Copy)\
                        .then_inc(inc, 1)

            def rms(l):
                act.wait_ge(*read(l, 2, "o"))
                for h in range(H):
                    if h >= 2:
                        act.wait_ge(rms_sum, l * 4 + h - 1)
                    act.activation(sq[:, h % 2, :], oT[:, h, :], ACT.Square).then_inc(rms_sq, 1)
                for h in range(H):
                    act.wait_ge(rms_sum, l * 4 + h + 1)
                    act.activation(rmsr[:, h, :], PS[4 + h][:, 0:T], ACT.Sqrt, scale=1.0 / 128, bias=1e-6)\
                        .then_inc(rms_root, 1)
                for h in range(H):
                    act.wait_ge(o_made, l * 4 + h + 1)
                    act.activation(Xh[:, 4 + h, :], oT[:, h, :], ACT.Copy).then_inc(split_hi, 1)

            def mix(l, m):
                act.wait_ge(mix_done, l * 8 + m + 1)
                act.activation(Mh[:, m, :], G[:, m, :], ACT.Copy).then_inc(split_hi, 1)

            def ffn(l):
                lo, hi = e_range(l)

                def fhead(e, i):
                    w = UNIT if i < 2 * FT else FUNIT
                    act.wait_ge(fraw_in[i % 5], e * (FU // 5 * 16) + (i // 5 + 1) * 16)
                    act.wait_ge(f_done, e * FU + (i + 1))
                    act.activation(fh[:, i % 3, 0:w], fraw[:, i % 5, 0:w], ACT.Copy).then_inc(f_hi, 1)

                def hhead(e, j):
                    if l == 0:
                        act.wait_ge(f_uev, e * FT + (2 + j + 1))
                    else:
                        act.wait_ge(f_h, (e - lo) * FT + (j + 1))
                    act.activation(Hh[:, j, :], hf[:, j % 2, :], ACT.Copy).then_inc(f_hhi, 1)

                with act.Fori(lo, hi) as e:
                    fhead(e, 0)
                    fhead(e, 1)
                    for j in range(FT):
                        fhead(e, 2 * j + 2)
                        if 2 * j + 3 < 2 * FT:
                            fhead(e, 2 * j + 3)
                        act.wait_ge(f_done, e * FU + (3 + 2 * j + 1))
                        act.wait_ge(f_uev, e * FT + (j + 1))
                        act.activation(sg[:, j % 2, :], PS[2 * j % 6][:, 0:T], ACT.Silu).then_inc(f_silu, 1)
                        if j:
                            hhead(e, j - 1)
                    hhead(e, FT - 1)
                    for i in range(2 * FT + 1, FU):
                        fhead(e, i)

            def router(l):
                act.wait_ge(rt_top, 1)
                act.activation(rk[:, 2], rk[:, 2], ACT.Exp).then_inc(rt_exp, 1)
                for t in range(3):
                    for half in range(2):
                        act.wait_ge(gb_done, 2 * t + half + 1)
                        act.activation(gbc[:, 4 * half:4 * half + 4, cols(t)],
                                       PS[6 + half][:, :].rearrange("p (e n) -> p e n", e=4)[:, :, 0:rows(t)], ACT.Copy)\
                            .then_inc(gb_copied, 1)

            act.wait_ge(in_ready, 80)
            for m in range(KT):
                act.activation(Xh[:, m, :], X[:, m, :], ACT.Copy).then_inc(split_hi, 1)
            head(0)
            head(1)
            for l in range(DEPTH):
                for kind, x in STEPS:
                    if kind == "unit":
                        unit(l, x)
                        if x == U_YP:
                            pooled_out(l)
                    elif kind == "qact":
                        qact(l, x)
                    elif kind == "ssq":
                        ssq(l, x)
                    elif kind == "norms":
                        norms(l)
                    elif kind == "ab":
                        ab_part(l)
                    elif kind == "pool":
                        pool_head(l, x)
                    elif kind == "ln":
                        ln(l, x)
                    elif kind == "delta":
                        delta(l, *x)
                    elif kind == "rms":
                        rms(l)
                    elif kind == "mix":
                        mix(l, x)
                act.wait_ge(aff_done, ln_at(l, 2))
                act.activation(acc[:, :, :], X[:, :, :], ACT.Copy, scale=ALPHA).then_inc(acc_init, 1)
                if l % 2:
                    router(l)
                ffn(l)
                ln(l, 2)
                head((l + 1) * NU)
                head((l + 1) * NU + 1)

        @block.tensor
        def _(pe):
            def mm3(out, wh, wl, xh, xl, start, stop):
                pe.matmul(out, wl, xh, start=start, stop=False)
                pe.matmul(out, wh, xl, start=False, stop=False)
                return pe.matmul(out, wh, xh, start=False, stop=stop)

            def unit(l, u):
                n = l * NU + u
                g = FIRST[u]
                hi, lo = Wh[:, n % 3, :], Wl[:, n % 3, :]
                if u == 0:
                    pe.wait_ge(split_lo, x_split(l))
                pe.wait_ge(w_lo, n + 1)
                if u < U_YP or u >= U_WO:
                    xh, xl = (Xh, Xl) if u < U_YP else (Mh, Ml)
                    if u == U_WO:
                        pe.wait_ge(split_lo, split(l, "m", 7))
                    bank_free(pe, l, g)
                    for k in range(KT):
                        c = slice(128 * k, 128 * k + 128)
                        ins = mm3(gbank(l, g)[:, 0:T], hi[:, c], lo[:, c], xh[:, k, :], xl[:, k, :], k == 0, k == KT - 1)
                elif u == U_YP:
                    pe.wait_ge(split_lo, split(l, "d", 3))
                    for m in range(8):
                        bank_free(pe, l, g + m)
                        c = slice(128 * m, 128 * m + 128)
                        ins = mm3(gbank(l, g + m)[:, 0:T], hi[:, c], lo[:, c], dh[:, m // 2, :], dl[:, m // 2, :], True, True)
                        ins.then_inc(yp_seen, 1)
                    pe.wait_ge(yp_seen, (l + 1) * 8)
                    pe.sem_inc(unit_done, 1)
                    return
                else:
                    k0 = 0 if u < U_YD else 4
                    if u in (U_YC, U_YD):
                        pe.wait_ge(split_lo, split(l, "c" if u < U_YD else "o", 3))
                    for m in range(2):
                        bank_free(pe, l, g + m)
                        for k in range(4):
                            c = slice(512 * m + 128 * k, 512 * m + 128 * k + 128)
                            ins = mm3(gbank(l, g + m)[:, 0:T], hi[:, c], lo[:, c], Xh[:, k0 + k, :], Xl[:, k0 + k, :],
                                      k == 0, k == 3)
                ins.then_inc(unit_done, 1)

            def ssq(l, i):
                pe.wait_ge(sqr_done, l * 8 + i + 1)
                if i >= 2:
                    pe.wait_ge(nrm_copied, l * 8 + i - 1)
                pe.matmul(PS[4 + i % 2][:, 0:T], C("ones"), sq[:, i % 2, :], start=True, stop=True).then_inc(ssq_done, 1)

            def ab_part(l):
                for t in range(3):
                    for k in range(KT):
                        ins = pe.matmul(PS[6][0:rows(t), 8 * t:8 * t + 8], X[:, k, cols(t)], wab[:, k, :],
                                        start=(k == 0), stop=(k == KT - 1))
                ins.then_inc(ab_done, 1)

            def ln(l, w):
                k, n0 = LNT[w], ln_at(l, w)
                src = (cacc, X, acc)[w]
                for m in range(k):
                    if w == 0:
                        pe.wait_ge(conv_done, l * 4 + m + 1)
                    elif w == 1:
                        pe.wait_ge(*evicted(l, FIRST[U_WO + m]))
                    else:
                        pe.wait_ge(f_dev, 8 + 8 * (e_range(l)[1] - 1) + m + 1)
                    ins = pe.matmul(PS[6][:, 0:T], C("ones"), src[:, m, :], start=(m == 0), stop=(m == k - 1))
                ins.then_inc(ln_sum, 1)
                for m in range(k):
                    pe.wait_ge(ln_sq, n0 + m + 1)
                    pe.matmul(PS[7][:, 0:T], C("ones"), sq[:, m % 2, :], start=(m == 0), stop=(m == k - 1))\
                        .then_inc(ln_sqs, 1)

            def delta(l, t, name):
                j, r = number(l, t, name), rows(t)
                if j % len(PROD) >= 4:
                    pe.wait_ge(*consumed(j - 4))
                b = dbank(j)
                p = "s" if t == 2 else "p"
                cum = C("cum_" + p, r)
                heads = range(H)
                cs = cols(t)

                def out4(h, m, n):
                    return b[0:m, n * h:n * h + n]

                if name == "gc":
                    pe.wait_ge(gb_made, l * 3 + t + 1)
                    pe.matmul(b[0:r, 0:4], cum, sc[0:r, 0, t, :], start=True, stop=True)
                    pe.matmul(b[0:r, 4:8], C("blk_" + p, r), sc[0:r, 0, t, :], start=True, stop=True)
                    ni = 2 if t < 2 else 8
                    for h in heads:
                        ins = pe.matmul(b[:, 16 + 8 * h:24 + 8 * h], gb[0:r, h, :], C("ind_" + p, r), start=True, stop=True)
                elif name == "R":
                    for h in heads:
                        ins = pe.matmul(out4(h, 128, r), gb[0:r, h, :], cum, start=True, stop=True)
                elif name in ("kt", "vt"):
                    if name == "kt":
                        pe.wait_ge(qk_ready, l + 1)
                        pe.wait_ge(qs_done, (l + 1) * 12)
                    src = kT if name == "kt" else vT
                    for h in heads:
                        ins = pe.transpose(out4(h, r, 128), src[:, h, cs], C("ident"))
                elif name == "G":
                    for h in heads:
                        ins = pe.matmul(out4(h, r, r), kT[:, h, cs], kT[:, h, cs], start=True, stop=True)
                elif name == "A":
                    for h in heads:
                        ins = pe.matmul(out4(h, r, r), kT[:, h, cs], qT[:, h, cs], start=True, stop=True)
                elif name == "NT":
                    pe.wait_ge(*read(l, t, "G"))
                    for h in heads:
                        ins = pe.transpose(out4(h, r, r), NN[0:r, h, 0:r], C("ident", r)[:, 0:r])
                elif name[0] == "t" :
                    s = int(name[1])
                    if s == 1:
                        pe.wait_ge(xy0_made, l * 3 + t + 1)
                    else:
                        pe.wait_ge(*read(l, t, f"y{s - 1}"))
                    for h in heads:
                        ins = pe.matmul(out4(h, r, r), NT[0:r, h, 0:r], XX[0:r, h, 0:r], start=True, stop=True)
                elif name[0] in "xy":
                    pe.wait_ge(*read(l, t, "t" + name[1]))
                    for h in heads:
                        a, c = (YY, T1) if name[0] == "x" else (T1, YY)
                        ins = pe.matmul(out4(h, r, r), a[0:r, h, 0:r], c[0:r, h, 0:r], start=True, stop=True)
                elif name == "u":
                    pe.wait_ge(*read(l, t, "y5" if t < 2 else "y2"))
                    for h in heads:
                        if t < 2:
                            ins = pe.matmul(out4(h, r, 128), YY[0:r, h, 0:r], vb[0:r, h, :], start=True, stop=True)
                        else:
                            ins = pe.matmul(out4(h, 128, r), vb[0:r, h, :], YY[0:r, h, 0:r], start=True, stop=True)
                elif name == "w":
                    for h in heads:
                        ins = pe.matmul(out4(h, 128, r), kb[0:r, h, :], YY[0:r, h, 0:r], start=True, stop=True)
                elif name in ("p0", "p1"):
                    c = int(name[1])
                    pe.wait_ge(*read(l, t, "w"))
                    if (t, c) == (0, 0):
                        pe.wait_ge(s_zero, l + 1)
                    else:
                        pe.wait_ge(*(read(l, t, "s0") if c else read(l, t - 1, "s1")))
                    for h in heads:
                        ins = pe.matmul(out4(h, 128, 128), wT[:, h, :], S[:, h, :], start=True, stop=True)
                elif name in ("o0", "o1"):
                    c = int(name[1])
                    q = slice(64 * c, 64 * c + 64)
                    for h in heads:
                        pe.matmul(out4(h, 128, 64), S[:, h, :], eg[:, h, q], start=(h == 0), stop=False, skip_group_check=True)
                    pe.wait_ge(*read(l, t, f"p{c}"))
                    for h in heads:
                        ins = pe.matmul(out4(h, 128, 64), vn[q, h, :], aT[q, h, q], start=False, stop=(h == H - 1),
                                        skip_group_check=True)
                elif name in ("s0", "s1"):
                    q = slice(64 * int(name[1]), 64 * int(name[1]) + 64)
                    for h in heads:
                        ins = pe.matmul(out4(h, 128, 128), kd[q, h, :], vn[q, h, :], start=True, stop=True)
                elif name == "p":
                    pe.wait_ge(*read(l, t, "w"))
                    pe.wait_ge(ss_in, 16 * (l + 1))
                    for h in heads:
                        for i in range(NSEQ):
                            ins = pe.matmul(b[:, 64 * h + 8 * i:64 * h + 8 * i + 8], Ss[:, h, i, :], wT[:, h, 8 * i:8 * i + 8],
                                            start=True, stop=True)
                elif name == "v":
                    pe.wait_ge(*read(l, t, "p"))
                    for h in heads:
                        ins = pe.transpose(out4(h, r, 128), uu[:, h, 0:r], C("ident"))
                elif name == "o":
                    for h in heads:
                        for i in range(NSEQ):
                            q = slice(8 * i, 8 * i + 8)
                            pe.matmul(b[:, 64 * h + 8 * i:64 * h + 8 * i + 8], Ss[:, h, i, :], eg[:, h, q],
                                      start=(h == 0 and i == 0), stop=False, skip_group_check=True)
                    pe.wait_ge(*read(l, t, "v"))
                    for h in heads:
                        ins = pe.matmul(out4(h, 128, 64), vn[0:64, h, :], aT[0:64, h, 0:64], start=False,
                                        stop=(h == H - 1), skip_group_check=True)
                else:
                    h, half = int(name[1]), int(name[2])
                    if half == 0:
                        pe.wait_ge(vblk_made, l * 4 + h + 1)
                    ins = pe.matmul(b[:, :], kd[0:64, h, :], vblk[:, 4 * half:4 * half + 4, :], start=True, stop=True)
                ins.then_inc(dmm, 1)

            def rms(l):
                for h in range(H):
                    pe.wait_ge(rms_sq, l * 4 + h + 1)
                    if h == 0:
                        pe.wait_ge(*read(l, 2, "s31"))
                    pe.matmul(PS[4 + h][:, 0:T], C("ones"), sq[:, h % 2, :], start=True, stop=True).then_inc(rms_sum, 1)

            def router(l):
                for t in range(3):
                    for k in range(KT):
                        ins = pe.matmul(PS[7][0:rows(t), 8 * t:8 * t + 8], X[:, k, cols(t)], wrt[:, k, :],
                                        start=(k == 0), stop=(k == KT - 1))
                ins.then_inc(rt_done, 1)
                for t in range(3):
                    pe.wait_ge(gx_made, t + 1)
                    for e in range(NE):
                        if e % 4 == 0 and (t or e):
                            pe.wait_ge(gb_copied, 2 * t + e // 4 - 1) if 2 * t + e // 4 >= 2 else None
                        ins = pe.matmul(PS[6 + e // 4][:, 128 * (e % 4):128 * (e % 4) + rows(t)], gexp[0:rows(t), e, :],
                                        C("ident", rows(t))[:, 0:rows(t)], start=True, stop=True)
                        if e % 4 == 3:
                            ins.then_inc(gb_done, 1)

            def ffn(l):
                lo, hi = e_range(l)
                with pe.Fori(lo, hi) as e:
                    for i in range(FU):
                        p = i - 6
                        if p < 0:
                            pe.wait_ge(f_dev, e * 8 + (i + 3))
                        elif p < 2 * FT and p % 2 == 0:
                            pe.wait_ge(f_silu, e * FT + (p // 2 + 1))
                        elif p < 2 * FT:
                            pe.wait_ge(f_uev, e * FT + (2 + p // 2 + 1))
                        else:
                            pe.wait_ge(f_dev, e * 8 + (8 + p - 2 * FT + 1))
                        pe.wait_ge(f_lo, e * FU + (5 + i + 1))
                        if i == 2 * FT:
                            pe.wait_ge(f_hlo, e * FT + (2 + FT))
                        n, xh, xl = (KT, Xh, Xl) if i < 2 * FT else (FT, Hh, Hl)
                        for k in range(n):
                            c = slice(128 * k, 128 * k + 128)
                            ins = mm3(PS[i % 6][:, 0:T], fh[:, i % 3, c], fl[:, i % 3, c], xh[:, k, :], xl[:, k, :],
                                      k == 0, k == n - 1)
                        ins.then_inc(f_done, 1)

            pe.sem_inc(f_done, 3)
            pe.sem_inc(f_uev, 2)
            pe.sem_inc(f_hlo, 2)
            pe.sem_inc(f_dev, 8)
            pe.wait_ge(in_ready, 80)
            for l in range(DEPTH):
                for kind, x in STEPS:
                    if kind == "unit":
                        unit(l, x)
                    elif kind == "ssq":
                        ssq(l, x)
                    elif kind == "ab":
                        pe.wait_ge(state_in, 64 * (l + 1))
                        ab_part(l)
                    elif kind == "ln":
                        ln(l, x)
                    elif kind == "delta":
                        delta(l, *x)
                    elif kind == "rms":
                        rms(l)
                pe.wait_ge(split_lo, split(l, "x1", 7))
                if l % 2:
                    router(l)
                ffn(l)
                ln(l, 2)

        @block.vector
        def _(dve):
            steps = [0]

            def step(ins):
                steps[0] += 1
                ins.then_inc(vch, 1)
                return steps[0]

            def link(ins):
                dve.wait_ge(vch, step(ins))

            def seqs(ap):
                return ap.rearrange("p (b t) -> p b t", b=NSEQ)

            def qconv(l, i):
                dst = (qT, kT, vT)[i // 4][:, i % 4, :]
                dve.wait_ge(*evicted(l, i))
                s = i % 2
                last = {}
                for k in range(SK_):
                    w = P(l, "w_short", SK_ * i + k)
                    for part in (0, 1):
                        src = qxp[:, s, k:k + SEQ] if part == 0 else qxs[:, s, :, k:k + TS]
                        out = dst[:, 0:SEQ] if part == 0 else seqs(dst[:, SEQ:T])
                        if k:
                            dve.wait_ge(vch, last[part])
                            ins = dve.scalar_tensor_tensor(out=out, in0=src, scalar=w, in1=out, op0=ALU.mult, op1=ALU.add)
                        else:
                            ins = dve.tensor_scalar(out, src, w, None, ALU.mult)
                        if k == SK_ - 1 and part:
                            ins.then_inc(qc_done, 1)
                        else:
                            last[part] = step(ins)
                dve.wait_ge(vch, last[0])

            def qact(l, i):
                dst = (qT, kT, vT)[i // 4][:, i % 4, :]
                dve.wait_ge(qt_done, l * 12 + i + 1)
                dve.wait_ge(qc_done, l * 12 + i + 1)
                dve.scalar_tensor_tensor(out=dst, in0=yb[:, i % 2, :], scalar=1.0, in1=dst, op0=ALU.add, op1=ALU.mult)\
                    .then_inc(qs_done, 1)

            def glu(l, i):
                dve.wait_ge(*evicted(l, U_AB + 2 * i + 1))
                link(dve.scalar_tensor_tensor(out=cxp[:, i, CB:], in0=std[:, 0:SEQ], scalar=1.0, in1=cxp[:, i, CB:],
                                              op0=ALU.add, op1=ALU.mult))
                dve.scalar_tensor_tensor(out=cxs[:, i, :, CB:], in0=seqs(std[:, SEQ:T]), scalar=1.0,
                                         in1=cxs[:, i, :, CB:], op0=ALU.add, op1=ALU.mult).then_inc(glu_done, 1)

            def z_silu(l, i):
                dve.wait_ge(*evicted(l, U_Z + i))
                dve.scalar_tensor_tensor(out=Z[:, i, :], in0=sq[:, i % 2, :], scalar=1.0, in1=Z[:, i, :],
                                         op0=ALU.add, op1=ALU.mult).then_inc(z_done, 1)

            def ab_part(l):
                a = PAR["dt"][0]
                dve.wait_ge(ab_copied, l + 1)
                dve.tensor_tensor(tmp3[:, 0, :, :], ab[:, :, 0:4], over(par[:, l, a:a + 4], 3), ALU.add).then_inc(ab_dve, 1)
                dve.wait_ge(ab_act, 3 * l + 3)
                dve.wait_ge(ab_dve, 2 * l + 1)
                link(dve.scalar_tensor_tensor(out=tmp3[:, 1, :, :], in0=tmp3[:, 0, :, :], scalar=0.0, in1=tmp3[:, 1, :, :],
                                              op0=ALU.max, op1=ALU.add))
                link(dve.scalar_tensor_tensor(out=sc[:, 0, :, :], in0=tmp3[:, 1, :, :], scalar=-1.0,
                                              in1=over(tmp3[:, 2, 0, :], 3), op0=ALU.mult, op1=ALU.mult))
                link(dve.tensor_scalar(sc[:, 1, :, :], sc[:, 1, :, :], 0.5, 0.5, ALU.mult, ALU.add))
                dve.tensor_scalar(sc[:, 2, :, :], sc[:, 1, :, :], 0.5, None, ALU.mult).then_inc(ab_dve, 1)

            def norms(l):
                dve.wait_ge(nrm_root, l + 1)
                dve.wait_ge(qs_done, l * 12 + 12)
                link(dve.reciprocal(nrm[:, :, :], nrm[:, :, :]))
                dve.scalar_tensor_tensor(out=qT[:, :, :], in0=qT[:, :, :], scalar=128 ** -0.5, in1=nrm[:, 0:4, :],
                                         op0=ALU.mult, op1=ALU.mult)
                dve.tensor_tensor(kT[:, :, :], kT[:, :, :], nrm[:, 4:8, :], ALU.mult).then_inc(qk_ready, 1)

            def pool(l, i):
                w = WINDOWS[i]
                dve.wait_ge(*evicted(l, U_POOL + i))
                d = tt[:, i % 2, :]
                for part in (1, 0):
                    src = pxp[:, i, :] if part == 0 else pxs[:, i, :, :]
                    n = PB + (SEQ if part == 0 else TS)

                    def at(ap, a, b):
                        return ap[:, a:b] if part == 0 else ap[:, :, a:b]

                    bufs = [pw[:, q, :] if part == 0 else pw[:, q, 0:NSEQ * n].rearrange("p (b t) -> p b t", b=NSEQ)
                            for q in (0, 1)]
                    cur, step_, q = src, 1, 0
                    while step_ < w:
                        lo = 2 * step_ - 1
                        link(dve.tensor_tensor(at(bufs[q], lo, n), at(cur, lo, n), at(cur, lo - step_, n - step_), ALU.add))
                        cur, step_, q = bufs[q], 2 * step_, 1 - q
                    out = d[:, 0:SEQ] if part == 0 else seqs(d[:, SEQ:T])
                    link(dve.scalar_tensor_tensor(out=out, in0=at(cur, PB, n), scalar=1.0 / w, in1=at(src, PB, n),
                                                  op0=ALU.mult, op1=ALU.subtract))
                    if part == 0:
                        o = CON["invcnt"][0] + 16 * i
                        link(dve.tensor_tensor(pw[:, q, 0:16], cur[:, PB:PB + 16], con[:, o:o + 16], ALU.mult))
                        dve.tensor_tensor(d[:, 0:16], pw[:, q, 0:16], src[:, PB:PB + 16], ALU.subtract).then_inc(d_made, 1)
                dve.wait_ge(d_made, l * 4 + i + 1)
                dve.wait_ge(split_hi, split(l, "d", i))
                dve.tensor_tensor(dl[:, i, :], d, dh[:, i, :].bitcast(f32), ALU.subtract).then_inc(split_lo, 1)

            def conv(l, i):
                last = {}
                for k in range(CK):
                    w = P(l, "w_dw", CK * i + k)
                    for part in (0, 1):
                        src = cxp[:, i, k:k + SEQ] if part == 0 else cxs[:, i, :, k:k + TS]
                        out = cacc[:, i, 0:SEQ] if part == 0 else seqs(cacc[:, i, SEQ:T])
                        if k == 0:
                            if part == 0:
                                dve.wait_ge(glu_done, l * 4 + i + 1)
                            ins = dve.tensor_scalar(out, src, w, P(l, "b_dw", i), ALU.mult, ALU.add)
                        else:
                            dve.wait_ge(vch, last[part])
                            ins = dve.scalar_tensor_tensor(out=out, in0=src, scalar=w, in1=out, op0=ALU.mult, op1=ALU.add)
                        if k == CK - 1 and part:
                            ins.then_inc(conv_done, 1)
                        else:
                            last[part] = step(ins)

            def ln(l, w):
                k, n0 = LNT[w], ln_at(l, w)
                src, dst = (cacc, X, acc)[w], (cacc, X, X)[w]
                dve.wait_ge(ln_sum, 3 * l + w + 1)
                for m in range(k):
                    if w == 0:
                        dve.wait_ge(conv_done, l * 4 + m + 1)
                    elif w == 1:
                        dve.wait_ge(*evicted(l, FIRST[U_WO + m]))
                    else:
                        dve.wait_ge(f_dev, 8 + 8 * (e_range(l)[1] - 1) + m + 1)
                    dve.scalar_tensor_tensor(out=src[:, m, :], in0=PS[6][:, 0:T], scalar=-1.0 / (128 * k), in1=src[:, m, :],
                                             op0=ALU.mult, op1=ALU.add).then_inc(ln_cent, 1)
                dve.wait_ge(ln_std, 3 * l + w + 1)
                dve.wait_ge(ln_cent, n0 + k)
                link(dve.reciprocal(rstd[:, :], std[:, :]))
                for m in range(k):
                    dve.tensor_tensor(dst[:, m, :], src[:, m, :], rstd[:, :], ALU.mult).then_inc(ln_norm, 1)
                if w == 0:
                    for m in range(k):
                        dve.wait_ge(csig, l * 4 + m + 1)
                        dve.scalar_tensor_tensor(out=cacc[:, m, :], in0=sq[:, m % 2, :], scalar=1.0, in1=cacc[:, m, :],
                                                 op0=ALU.add, op1=ALU.mult).then_inc(csilu, 1)
                    for m in range(k):
                        dve.wait_ge(split_hi, split(l, "c", m))
                        dve.scalar_tensor_tensor(out=Xl[:, m, :], in0=cacc[:, m, :], scalar=0.5,
                                                 in1=Xh[:, m, :].bitcast(f32), op0=ALU.mult, op1=ALU.subtract)\
                            .then_inc(split_lo, 1)
                elif (l, w) != (DEPTH - 1, 2):
                    for m in range(k):
                        dve.wait_ge(split_hi, split(l, "x1" if w == 1 else "x2", m))
                        dve.tensor_tensor(Xl[:, m, :], X[:, m, :], Xh[:, m, :].bitcast(f32), ALU.subtract)\
                            .then_inc(split_lo, 1)

            def delta(l, t, name):
                j, r = number(l, t, name), rows(t)
                b = dbank(j)
                n4 = {"kt": 128, "vt": 128, "p0": 128, "p1": 128, "s0": 128, "s1": 128}.get(name, r)
                b4 = b[:, 0:4 * n4].rearrange("p (h n) -> p h n", h=H)
                p = "s" if t == 2 else "p"
                inc = consumed(j)[0]
                if dict(products(t))[name] == "dve" and not (t == 2 and name[0] == "s"):
                    dve.wait_ge(dmm, j + 1)

                def scal(i):
                    return sc[0:r, i, t, :]

                def lev(s, n="lev"):
                    o = CON[n][0] + 128 * s
                    return over(con[0:r, o:o + r], H)

                if name == "gc":
                    dve.wait_ge(ab_dve, 2 * l + 2)
                    dve.tensor_copy(gb[0:r, :, :], along(scal(0), 128)).then_inc(gb_made, 1)
                    dve.wait_ge(*read(l, t, "gc"))
                    dve.tensor_tensor(scal(7), scal(4), scal(3), ALU.subtract).then_inc(dif_made, 1)
                    link(dve.tensor_tensor(scal(6), scal(1), scal(5), ALU.mult))
                elif name == "R":
                    dve.wait_ge(eg_made, l * 3 + t + 1)
                    link(dve.tensor_tensor(decT[0:r, :, 0:r], b4[0:r], along(scal(3), r), ALU.subtract))
                    dve.tensor_scalar(dec[0:r, :, 0:r], decT[0:r, :, 0:r], 0.0, None, ALU.max).then_inc(inc, 1)
                    dve.tensor_scalar(decT[0:r, :, 0:r], decT[0:r, :, 0:r], 0.0, None, ALU.min).then_inc(arg_made, 1)
                elif name == "kt":
                    dve.wait_ge(kdec_made, l * 3 + t + 1)
                    dve.tensor_tensor(kb[0:r, :, :], b4[0:r], along(scal(6), 128), ALU.mult)
                    dve.tensor_tensor(kd[0:r, :, :], b4[0:r], along(scal(7), 128), ALU.mult).then_inc(inc, 1)
                elif name == "vt":
                    dve.tensor_tensor(vb[0:r, :, :], b4[0:r], along(scal(2), 128), ALU.mult).then_inc(inc, 1)
                elif name == "G":
                    dve.wait_ge(dec_made, l * 3 + t + 1)
                    link(dve.scalar_tensor_tensor(out=dec[0:r, :, 0:r], in0=dec[0:r, :, 0:r], scalar=-1.0,
                                                  in1=over(C("strict_" + p, r), H), op0=ALU.mult, op1=ALU.mult))
                    link(dve.tensor_tensor(dec[0:r, :, 0:r], dec[0:r, :, 0:r], along(scal(1), r), ALU.mult))
                    dve.tensor_tensor(NN[0:r, :, 0:r], b4[0:r], dec[0:r, :, 0:r], ALU.mult).then_inc(inc, 1)
                elif name == "A":
                    link(dve.tensor_tensor(decT[0:r, :, 0:r], decT[0:r, :, 0:r], over(C("cum_" + p, r), H), ALU.mult))
                    dve.tensor_tensor(aT[0:r, :, 0:r], b4[0:r], decT[0:r, :, 0:r], ALU.mult).then_inc(inc, 1)
                    dve.wait_ge(*read(l, t, "G"))
                    link(dve.tensor_tensor(eg[:, :, 0:r], qT[:, :, cols(t)], eg[:, :, 0:r], ALU.mult))
                elif name == "NT":
                    link(dve.tensor_tensor(XX[0:r, :, 0:r], NN[0:r, :, 0:r], lev(0), ALU.mult))
                    link(dve.tensor_tensor(XX[0:r, :, 0:r], XX[0:r, :, 0:r], over(C("ident", r)[:, 0:r], H), ALU.add))
                    dve.wait_ge(*read(l, t, "NT"))
                    link(dve.tensor_tensor(YY[0:r, :, 0:r], NT[0:r, :, 0:r], lev(0, "lev0t"), ALU.mult))
                    dve.tensor_tensor(YY[0:r, :, 0:r], YY[0:r, :, 0:r], over(C("ident", r)[:, 0:r], H), ALU.add)\
                        .then_inc(xy0_made, 1)
                elif name[0] == "t":
                    dve.tensor_tensor(T1[0:r, :, 0:r], b4[0:r], lev(int(name[1])), ALU.mult).then_inc(inc, 1)
                elif name[0] in "xy":
                    m = XX if name[0] == "x" else YY
                    s = int(name[1])
                    if s == 1:
                        dve.wait_ge(xy0_made, l * 3 + t + 1)
                    elif name[0] == "y":
                        dve.wait_ge(*read(l, t, f"y{s - 1}"))
                    dve.tensor_tensor(m[0:r, :, 0:r], m[0:r, :, 0:r], b4[0:r], ALU.add).then_inc(inc, 1)
                elif name in ("p0", "p1"):
                    q = slice(64 * int(name[1]), 64 * int(name[1]) + 64)
                    dve.wait_ge(*read(l, t, "u"))
                    dve.tensor_tensor(vn[q, :, :], uu[q, :, :], b4[q], ALU.subtract).then_inc(inc, 1)
                elif name in ("s0", "s1"):
                    c = int(name[1])
                    for h in range(H):
                        ins = dve.scalar_tensor_tensor(out=S[:, h, :], in0=S[:, h, :], scalar=gs[:, h, c:c + 1],
                                                       in1=b4[:, h, :], op0=ALU.mult, op1=ALU.add)
                    ins.then_inc(inc, 1)
                    dve.wait_ge(*read(l, t, name))
                elif name == "p":
                    dve.wait_ge(*read(l, t, "u"))
                    dve.tensor_tensor(uu[:, :, 0:r], uu[:, :, 0:r], b4, ALU.subtract).then_inc(inc, 1)
                elif name == "v":
                    dve.wait_ge(*read(l, t, "v"))
                elif name[0] == "s":
                    h, half = int(name[1]), int(name[2])
                    q = slice(4 * half, 4 * half + 4)
                    if half == 0:
                        dve.wait_ge(dmm, j)
                        dve.tensor_tensor(vblk[:, :, :], over(vn[0:64, h, :], NSEQ), along(C("ind_s", 64), 128), ALU.mult)\
                            .then_inc(vblk_made, 1)
                        link(dve.tensor_tensor(Ss[:, h, :, :], Ss[:, h, :, :], along(gs[:, h, :], 128), ALU.mult))
                    dve.wait_ge(dmm, j + 1)
                    dve.tensor_tensor(Ss[:, h, q, :], Ss[:, h, q, :], b[:, :].rearrange("p (n d) -> p n d", n=4), ALU.add)\
                        .then_inc(inc, 1)

            def rms(l):
                for h in range(H):
                    dve.wait_ge(rms_root, l * 4 + h + 1)
                    link(dve.reciprocal(rmsr[:, h, :], rmsr[:, h, :]))
                    link(dve.scalar_tensor_tensor(out=oT[:, h, :], in0=oT[:, h, :], scalar=P(l, "dn_g"), in1=rmsr[:, h, :],
                                                  op0=ALU.mult, op1=ALU.mult))
                    dve.scalar_tensor_tensor(out=oT[:, h, :], in0=oT[:, h, :], scalar=0.5, in1=Z[:, h, :],
                                             op0=ALU.mult, op1=ALU.mult).then_inc(o_made, 1)
                for h in range(H):
                    dve.wait_ge(split_hi, split(l, "o", h))
                    dve.tensor_tensor(Xl[:, 4 + h, :], oT[:, h, :], Xh[:, 4 + h, :].bitcast(f32), ALU.subtract)\
                        .then_inc(split_lo, 1)

            def pooled_in(l):
                for m in range(8):
                    dve.wait_ge(*evicted(l, FIRST[U_YP] + m))
                    dve.scalar_tensor_tensor(out=G[:, m, :], in0=G[:, m, :], scalar=1.0, in1=yb[:, m % 2, :],
                                             op0=ALU.add, op1=ALU.mult).then_inc(yp_done, 1)

            def branch(l, u, gate0, last_branch):
                dve.wait_ge(unit_done, l * NU + u + 1)
                for i in range(2):
                    g = FIRST[u] + i
                    m = 2 * (u - (U_YD if last_branch else U_YC)) + i
                    dve.scalar_tensor_tensor(out=tt[:, i, :], in0=G[:, gate0 + m, :], scalar=1.0, in1=gbank(l, g)[:, 0:T],
                                             op0=ALU.add, op1=ALU.mult).then_inc(evict_dve, 1)
                    dve.wait_ge(*evicted(l, g))
                    ins = dve.tensor_tensor(G[:, m, :], G[:, m, :], tt[:, i, :], ALU.add)
                    if last_branch:
                        ins.then_inc(mix_done, 1)
                    else:
                        link(ins)

            def mix(l, m):
                dve.wait_ge(split_hi, split(l, "m", m))
                dve.tensor_tensor(Ml[:, m, :], G[:, m, :], Mh[:, m, :].bitcast(f32), ALU.subtract).then_inc(split_lo, 1)

            def unit(l, u):
                if U_Z <= u < U_G:
                    z_silu(l, u - U_Z)
                elif u == U_YP:
                    pooled_in(l)
                elif U_YC <= u < U_YD:
                    branch(l, u, 8, False)
                elif U_YD <= u < U_WO:
                    branch(l, u, 16, True)
                elif u >= U_WO:
                    m = u - U_WO
                    dve.wait_ge(unit_done, l * NU + u + 1)
                    dve.scalar_tensor_tensor(out=X[:, m, :], in0=X[:, m, :], scalar=2 * ALPHA, in1=gbank(l, FIRST[u])[:, 0:T],
                                             op0=ALU.mult, op1=ALU.add).then_inc(evict_dve, 1)

            def ffn(l):
                lo, hi = e_range(l)

                def rest(e, j):
                    dve.wait_ge(f_hhi, e * FT + (j + 1))
                    dve.tensor_tensor(Hl[:, j, :], hf[:, j % 2, :], Hh[:, j, :].bitcast(f32), ALU.subtract).then_inc(f_hlo, 1)

                dve.wait_ge(acc_init, l + 1)
                with dve.Fori(lo, hi) as e:
                    for j in range(FT):
                        dve.wait_ge(f_silu, e * FT + (j + 1))
                        dve.wait_ge(f_done, e * FU + (3 + 2 * j + 2))
                        dve.wait_ge(f_hlo, e * FT + (j + 1))
                        dve.tensor_tensor(hf[:, j % 2, :], sg[:, j % 2, :], PS[(2 * j + 1) % 6][:, 0:T], ALU.mult)\
                            .then_inc(f_uev, 1)
                        if l % 2:
                            dve.wait_ge(f_uev, e * FT + (2 + j + 1))
                            dve.tensor_tensor(hf[:, j % 2, :], hf[:, j % 2, :],
                                              gbc[:, bass.ds(e - lo, 1), :].rearrange("p e t -> p (e t)"), ALU.mult)\
                                .then_inc(f_h, 1)
                        if j:
                            rest(e, j - 1)
                    rest(e, FT - 1)
                    for m in range(8):
                        dve.wait_ge(f_done, e * FU + (3 + 2 * FT + m + 1))
                        dve.wait_ge(f_dev, e * 8 + (m + 1))
                        dve.tensor_tensor(acc[:, m, :], acc[:, m, :], PS[(2 * FT + m) % 6][:, 0:T], ALU.add).then_inc(f_dev, 1)

            def router(l):
                lg, mx, ex, cnt, den = rk[:, 0], rk[:, 1, :, 0:1], rk[:, 2], rk[:, 3], rk[:, 4, :, 0:1]
                link(dve.memset(rk[:, :, :, :], 0.0))
                dve.wait_ge(rt_done, 1)
                for t in range(3):
                    ins = dve.tensor_tensor(lg[0:rows(t), t, :], PS[7][0:rows(t), 8 * t:8 * t + 8], brt[0:rows(t), :], ALU.add)
                link(ins)
                for t in range(3):
                    le = along(lg[:, t, :], NE)
                    lj = over(lg[:, t, :], NE)
                    link(dve.tensor_tensor(rc[:, 0, t], lj, le, ALU.is_gt))
                    link(dve.tensor_tensor(rc[:, 1, t], lj, le, ALU.is_equal))
                    link(dve.tensor_tensor(rc[:, 1, t], rc[:, 1, t],
                                           C("before").rearrange("p (e j) -> p e j", e=NE), ALU.mult))
                    link(dve.tensor_tensor(rc[:, 0, t], rc[:, 0, t], rc[:, 1, t], ALU.add))
                    link(dve.tensor_reduce(cnt[:, t, :], rc[:, 0, t], AX.X, ALU.add))
                link(dve.tensor_reduce(mx, lg, AX.X, ALU.max))
                dve.tensor_tensor(ex, lg, mx.broadcast_to([128, 3, NE]), ALU.subtract).then_inc(rt_top, 1)
                dve.wait_ge(rt_exp, 1)
                link(dve.scalar_tensor_tensor(out=ex, in0=cnt, scalar=1.5, in1=ex, op0=ALU.is_lt, op1=ALU.mult))
                link(dve.tensor_reduce(den, ex, AX.X, ALU.add))
                link(dve.reciprocal(den, den))
                link(dve.tensor_tensor(ex, ex, den.broadcast_to([128, 3, NE]), ALU.mult))
                for t in range(3):
                    if t:
                        dve.wait_ge(gb_done, 2 * t)
                    dve.tensor_copy(gexp[:, :, :], along(ex[:, t, :], 128)).then_inc(gx_made, 1)

            dve.wait_ge(in_ready, 80)
            for m in range(KT):
                dve.wait_ge(split_hi, m + 1)
                dve.tensor_tensor(Xl[:, m, :], X[:, m, :], Xh[:, m, :].bitcast(f32), ALU.subtract).then_inc(split_lo, 1)
            for l in range(DEPTH):
                for kind, x in STEPS:
                    if kind == "unit":
                        unit(l, x)
                    elif kind == "qconv":
                        qconv(l, x)
                    elif kind == "qact":
                        qact(l, x)
                    elif kind == "glu":
                        glu(l, x)
                    elif kind == "ab":
                        ab_part(l)
                    elif kind == "norms":
                        norms(l)
                    elif kind == "pool":
                        pool(l, x)
                    elif kind == "conv":
                        conv(l, x)
                    elif kind == "ln":
                        ln(l, x)
                    elif kind == "delta":
                        if x == (0, "gc"):
                            if l:
                                dve.wait_ge(out_done, l * 8 * 16)
                            dve.memset(S[:, :, :], 0.0).then_inc(s_zero, 1)
                        delta(l, *x)
                    elif kind == "rms":
                        rms(l)
                    elif kind == "mix":
                        mix(l, x)
                if l % 2:
                    router(l)
                ffn(l)
                ln(l, 2)


def _constants():
    i, j = np.arange(128)[:, None], np.arange(128)[None, :]
    out = np.zeros((128, NCON), np.float32)

    def put(name, a):
        o, w = CON[name]
        out[:a.shape[0], o:o + w] = a.reshape(a.shape[0], w)

    put("ident", (i == j).astype(np.float32))
    put("ones", np.ones((128, 128), np.float32))
    for p, n, c in (("p", 128, CHUNK), ("s", 64, TS)):
        a, b = i[:n], j[:, :n]
        same = a // c == b // c
        put("cum_" + p, (same & (a <= b)).astype(np.float32))
        put("blk_" + p, same.astype(np.float32))
        put("strict_" + p, (same & (a > b)).astype(np.float32))
        put("ind_" + p, (a // c == np.arange(8)[None]).astype(np.float32))
    lev = [((i >> (s + 1)) == (j >> (s + 1))) & ((i >> s) & 1 == 1) & ((j >> s) & 1 == 0) for s in range(6)]
    put("lev", np.stack(lev, 1).astype(np.float32))
    put("lev0t", lev[0].T.astype(np.float32))
    put("invcnt", np.tile(np.concatenate([1.0 / np.minimum(np.arange(16) + 1, w) for w in WINDOWS]).astype(np.float32), (128, 1)))
    put("before", np.tile((np.arange(NE)[None, :] < np.arange(NE)[:, None]).astype(np.float32).ravel(), (128, 1)))
    return out


def _tiles(a):
    return np.moveaxis(a.reshape(a.shape[:-1] + (-1, 128)), -1, 0)


def kernel(**inputs):
    import concourse.bacc as bacc
    from concourse import mybir
    from concourse.bass_utils import run_bass_kernel_spmd

    a = {k: np.asarray(v) for k, v in inputs.items()}
    L = range(DEPTH)

    def units(w):
        k, n = w.shape[0] // 128, w.shape[1] // 128
        return w.reshape(k, 128, n, 128).transpose(1, 2, 0, 3).reshape(128, n, k * 128)

    x = np.concatenate([a["x_prompt"][0], a["x_sample"].reshape(-1, D)], 0)
    mix, wab = [], []
    for l in L:
        w = a["w_in"][l]
        pool, ca, cb, qkv, z = w[:, 0:512], w[:, 512:1024], w[:, 1024:1536], w[:, 1536:3072], w[:, 3072:3584]
        ab = np.stack([units(ca), units(cb)], 2).reshape(128, 8, UNIT)
        mix.append(np.concatenate([
            units(qkv), ab, units(pool), units(z), units(w[:, GATE_OFF:]),
            a["w_pool"][l].transpose(1, 0, 2).reshape(128, 1, UNIT),
            units(a["w_conv_out"][l]).reshape(128, 4, UNIT), units(a["w_dn_out"][l]).reshape(128, 4, UNIT),
            units(a["w_out"][l])], 1))
        wab.append(w[:, 3584:3592].reshape(KT, 128, 8).transpose(1, 0, 2))

    def expert(wg, wu, wd):
        gu = np.stack([units(wg), units(wu)], 2).reshape(128, 2 * FT * UNIT)
        return np.concatenate([gu, units(wd).reshape(128, 8 * FUNIT)], 1)

    hf = FT * 128
    g, u, d = a["ffn_wg"][0], a["ffn_wu"][0], a["ffn_wd"][0]
    ffn = [expert(g[:, i * hf:(i + 1) * hf], u[:, i * hf:(i + 1) * hf], d[i * hf:(i + 1) * hf]) for i in range(2)]
    ffn += [expert(a["moe_wg"][0, e], a["moe_wu"][0, e], a["moe_wd"][0, e]) for e in range(NE)]

    par = np.zeros((128, DEPTH, NPAR), np.float32)
    for l in L:
        for name, v in (("w_dw", _tiles(a["w_dw"][l]).transpose(0, 2, 1)), ("b_dw", _tiles(a["b_dw"][l])),
                        ("cg", _tiles(a["conv_ln_g"][l])), ("cb", _tiles(a["conv_ln_b"][l])),
                        ("w_short", _tiles(a["w_short"][l]).transpose(0, 2, 1)), ("pscale", _tiles(a["pool_scale"][l])),
                        ("dn_g", _tiles(a["dn_norm_g"][l])), ("ln1_g", _tiles(a["ln1_g"][l])), ("ln1_b", _tiles(a["ln1_b"][l])),
                        ("ln2_g", _tiles(a["ln2_g"][l])), ("ln2_b", _tiles(a["ln2_b"][l])),
                        ("a_log", np.tile(a["a_log"][l], (128, 1))), ("dt", np.tile(a["dt_bias"][l], (128, 1)))):
            o, w = PAR[name]
            par[:, l, o:o + w] = v.reshape(128, w)

    def history(s, room):
        n, b, r, c = s.shape
        s = s.reshape(n, b, r, c // 128, 128).transpose(0, 4, 3, 1, 2)
        return np.pad(s, [(0, 0)] * 4 + [(0, room)])

    arrays = {
        "x": x.reshape(T, KT, 128).transpose(2, 1, 0), "con": _constants(), "par": par,
        "w_router": a["w_router"][0].reshape(KT, 128, NE).transpose(1, 0, 2), "b_router": np.tile(a["b_router"][0], (128, 1)),
        "w_mix": np.stack(mix), "w_ab": np.stack(wab), "w_ffn": np.stack(ffn),
        "st_qkv": history(a["state_qkv_conv"], 0), "st_conv": history(a["state_conv"], TS),
        "st_pool": history(a["state_pool"], TS), "st_delta": a["state_delta"].transpose(0, 3, 2, 1, 4),
    }
    arrays = {k: np.ascontiguousarray(v) for k, v in arrays.items()}
    outs = {
        "y": (128, KT, T), "o_conv_p": (DEPTH, 128, H, CB), "o_conv_s": (DEPTH, 128, H, NSEQ, CB + TS),
        "o_pool_p": (DEPTH, 128, H, PB), "o_pool_s": (DEPTH, 128, H, NSEQ, PB + TS),
        "o_qkv_p": (DEPTH, 128, 12, SB), "o_qkv_s": (DEPTH, 128, 12, NSEQ, SB),
        "o_delta_p": (DEPTH, 128, H, 128), "o_delta_s": (DEPTH, 128, H, NSEQ, 128),
    }
    nc = bacc.Bacc("TRN2", target_bir_lowering=False, num_devices=1)
    io = {k: nc.dram_tensor(k, v.shape, mybir.dt.from_np(v.dtype), kind="ExternalInput").ap() for k, v in arrays.items()}
    io |= {k: nc.dram_tensor(k, s, mybir.dt.float32, kind="ExternalOutput").ap() for k, s in outs.items()}
    build(nc, io)
    r = run_bass_kernel_spmd(nc, [arrays], core_ids=[0]).results[0]

    y = r["y"].transpose(2, 1, 0).reshape(T, D)

    def rows_p(s):
        return s.transpose(0, 3, 2, 1).reshape(DEPTH, 1, s.shape[3], -1)

    def rows_s(s, keep):
        return s[..., -keep:].transpose(0, 3, 4, 2, 1).reshape(DEPTH, NSEQ, keep, -1)

    return (y[:SEQ].reshape(1, SEQ, D), y[SEQ:].reshape(NSEQ, TS, D),
            rows_p(r["o_pool_p"]), rows_p(r["o_conv_p"]), rows_p(r["o_qkv_p"]),
            r["o_delta_p"].transpose(0, 2, 1, 3)[:, None],
            rows_s(r["o_pool_s"], PB), rows_s(r["o_conv_s"], CB), rows_s(r["o_qkv_s"], SB),
            r["o_delta_s"].transpose(0, 3, 2, 1, 4))
```

```python
import numpy as np

DEPTH, D, SEQ, NSEQ, TS = 2, 1024, 256, 8, 8
T = SEQ + NSEQ * TS
KT = D // 128
H = 4
CK, SK_, PB = 31, 4, 15
CB, SB = CK - 1, SK_ - 1
FT = 11
NE = 8
CAP = 128
ALPHA = (2 * DEPTH) ** 0.25
CHUNK = 64
WINDOWS = (2, 4, 8, 16)
GATE_OFF = 3592
UNIT = 1024
FUNIT = FT * 128
N_QKV, N_AB, N_POOL, N_Z, N_G, N_YP, N_YC, N_YD, N_WO = 12, 8, 4, 4, 24, 1, 4, 4, 8
U_AB = N_QKV
U_POOL = U_AB + N_AB
U_Z = U_POOL + N_POOL
U_G = U_Z + N_Z
U_YP = U_G + N_G
U_YC = U_YP + N_YP
U_YD = U_YC + N_YC
U_WO = U_YD + N_YD
NU = U_WO + N_WO
NB = (NU + 1) // 2
FU = 2 * FT + 8
MG, MU, MD = 8, 8, FT
MN = MG + MU + MD
MW = (MG + MU) * FUNIT + MD * D
MP = MN + 1
MRAW, MS = 7, 4
SCAT = 2
MPOOL = [i for i in range(MN) if i % 4 == 3]

PAR = {}
_at = 0
for _n, _w in (("w_dw", 4 * CK), ("b_dw", 4), ("cg", 4), ("cb", 4), ("w_short", 12 * SK_), ("pscale", 8),
               ("dn_g", 1), ("ln1_g", 8), ("ln1_b", 8), ("ln2_g", 8), ("ln2_b", 8), ("a_log", 4), ("dt", 4)):
    PAR[_n] = (_at, _w)
    _at += _w
NPAR = _at

CON = {}
_at = 0
for _n, _w in (("ident", 128), ("ones", 128), ("cum_p", 128), ("blk_p", 128), ("strict_p", 128), ("cum_s", 64),
               ("blk_s", 64), ("strict_s", 64), ("ind_p", 8), ("ind_s", 8), ("lev", 6 * 128), ("lev0t", 128),
               ("invcnt", 64), ("before", 64),
               ("upto", 128), ("slot", 128)):
    CON[_n] = (_at, _w)
    _at += _w
NCON = _at


def build(nc, io):
    import concourse.bass as bass
    from concourse import mybir
    from contextlib import ExitStack

    f32, f32r = mybir.dt.float32, mybir.dt.float32r
    ALU, ACT, AX = mybir.AluOpType, mybir.ActivationFunctionType, mybir.AxisListType

    ctx = ExitStack()
    with ctx:
        base = (nc.sbuf_base + 31) // 32 * 32

        def size(shape):
            return (int(np.prod(shape[1:])) * 4 + 31) // 32 * 32

        def lay(at, *plan):
            out = []
            for name, shape, dt in plan:
                assert base + at + size(shape) <= nc.sbuf_usable_end, (name, base + at + size(shape))
                out.append(nc.alloc_sbuf_tensor_at(name, shape, dt, offset=base + at))
                at += size(shape)
            return out + [at]

        (con, par, X, Xh, Xl, raw, Wh, Wl, wab, wrt, brt, sq, std, rstd, ab, sc, gs, tmp3, gate, posm,
         gcol, gslot, flag, TOP) = lay(
            0, ("con", [128, NCON], f32), ("par", [128, DEPTH, NPAR], f32),
            ("X", [128, KT, T], f32),
            ("Xh", [128, KT, T], f32r), ("Xl", [128, KT, T], f32r),
            ("raw", [128, 3, 2, UNIT], f32),
            ("Wh", [128, 3, UNIT], f32r), ("Wl", [128, 3, UNIT], f32r),
            ("wab", [128, KT, 8], f32), ("wrt", [128, KT, NE], f32), ("brt", [128, NE], f32),
            ("sq", [128, 2, T], f32), ("std", [128, T], f32), ("rstd", [128, T], f32),
            ("ab", [128, 3, 8], f32),
            ("sc", [128, 9, 3, 4], f32),
            ("gs", [128, 4, 8], f32),
            ("tmp3", [128, 3, 3, 4], f32),
            ("gate", [128, 3, NE + 1], f32), ("posm", [128, 3, NE + 1], f32),
            ("gcol", [128, 3], f32), ("gslot", [128, 1], f32), ("flag", [128, 1], mybir.dt.int32))
        (G, EXT) = lay(TOP, ("G", [128, 24, T], f32))
        (cxp, cxs, pxp, pxs, E1) = lay(EXT, ("cxp", [128, H, CB + SEQ], f32), ("cxs", [128, H, NSEQ, CB + TS], f32),
                                       ("pxp", [128, H, PB + SEQ], f32), ("pxs", [128, H, NSEQ, PB + TS], f32))
        (Ss, E2) = lay(EXT, ("Ss", [128, H, NSEQ, 128], f32))
        (qxp, qxs, qh, qT, kT, vT, Z, S, oT, tp, ts, TEMP) = lay(
            max(E1, E2), ("qxp", [128, 2, SB + SEQ], f32), ("qxs", [128, 2, NSEQ, SB + TS], f32),
            ("qh", [128, 12, NSEQ, SB], f32),
            ("qT", [128, H, T], f32), ("kT", [128, H, T], f32), ("vT", [128, H, T], f32), ("Z", [128, H, T], f32),
            ("S", [128, H, 128], f32), ("oT", [128, H, T], f32),
            ("tp", [128, 12, SB], f32), ("ts", [128, 12, NSEQ, SB], f32))
        (gb, dec, decT, eg, NN, NT, XX, YY, T1, vb, kb, kd, uu, wT, aT, vn, E3) = lay(
            TEMP, *[(n, [128, H, 128], f32) for n in ("gb", "dec", "decT", "eg", "NN", "NT", "XX", "YY", "T1", "vb",
                                                      "kb", "kd", "uu", "wT", "aT", "vn")])
        (vblk, _) = lay(TEMP, ("vblk", [64, NSEQ, 128], f32))
        (cacc, _) = lay(TEMP - size([1, 12, SB]) - size([1, 12, NSEQ, SB]) - size([1, H, T]), ("cacc", [128, H, T], f32))
        (nrm, pw, dh, dl, yb, tt, E4) = lay(TEMP, ("nrm", [128, 8, T], f32), ("pw", [128, 2, PB + SEQ], f32),
                                            ("dh", [128, H, T], f32r), ("dl", [128, H, T], f32r),
                                            ("yb", [128, 2, T], f32), ("tt", [128, 2, T], f32))
        (Mh, Ml, E5) = lay(TEMP, ("Mh", [128, KT, T], f32r), ("Ml", [128, KT, T], f32r))
        (rmsr, _) = lay(TEMP, ("rmsr", [128, H, T], f32))
        (fh, fl, fraw, HT) = lay(TOP, ("fh", [128, 3, FUNIT], f32r), ("fl", [128, 3, FUNIT], f32r),
                                 ("fraw", [128, 5, FUNIT], f32))
        (Hh, Hl, acc, gbc, sg, hf, E6) = lay(HT, ("Hh", [128, FT, T], f32r), ("Hl", [128, FT, T], f32r),
                                             ("acc", [128, KT, T], f32), ("gbc", [128, NE, T], f32),
                                             ("sg", [128, 2, T], f32), ("hf", [128, 2, T], f32))
        (gexp, _) = lay(HT, ("gexp", [128, NE, 128], f32))
        (mraw, mh, ml, sg1, ACC) = lay(TOP, ("mraw", [128, MRAW, FUNIT], f32), ("mh", [128, MS, FUNIT], f32r),
                                       ("ml", [128, MS, FUNIT], f32r), ("sg1", [128, FUNIT], f32))
        assert ACC == HT + 2 * size([128, FT, T])
        (yf, yh, yl, rk, rc, _) = lay(ACC + size([128, KT, T]), ("yf", [128, D], f32), ("yh", [128, D], f32r),
                                      ("yl", [128, D], f32r), ("rk", [128, 5, 3, NE], f32), ("rc", [128, 2, 3, NE, NE], f32))
        RING = sum(size(s) for s in ([1, NCON], [1, DEPTH, NPAR])) + 3 * size([1, KT, T])
        (xth, xtl, hTh, hTl, xeh, xel, PT, Pm, E7) = lay(
            RING, ("xth", [128, 3, D], f32r), ("xtl", [128, 3, D], f32r), ("hTh", [128, FT, CAP], f32r),
            ("hTl", [128, FT, CAP], f32r), ("xeh", [128, KT, CAP], f32r), ("xel", [128, KT, CAP], f32r),
            ("PT", [CAP, T], f32r), ("Pm", [128, 3, CAP], f32r))
        assert E7 <= RING + 12 * UNIT * 4

        PS = [ctx.enter_context(nc.psum_tensor(f"ps{i}", [128, 512], f32)) for i in range(8)]

        def sem(name):
            return ctx.enter_context(nc.semaphore(name))

        def C(name, rows=128):
            o, w = CON[name]
            return con[0:rows, o:o + w]

        def P(l, name, i=0):
            o, _ = PAR[name]
            return par[:, l, o + i:o + i + 1]

        def over(ap, n):
            return ap.unsqueeze(1).broadcast_to([ap.shape[0], n, ap.shape[1]])

        def along(ap, n):
            return ap.unsqueeze(2).broadcast_to([ap.shape[0], ap.shape[1], n])

        in_ready, state_in, ss_in, out_done = sem("in_ready"), sem("state_in"), sem("ss_in"), sem("out_done")
        raw_in = [sem(f"raw_in{i}") for i in range(3)]
        w_hi, w_lo, unit_done = sem("w_hi"), sem("w_lo"), sem("unit_done")
        evict_act, evict_dve = sem("evict_act"), sem("evict_dve")
        hist_zero, vch, ach = sem("hist_zero"), sem("vch"), sem("ach")
        qc_done, qt_done, qs_done, sqr_done = sem("qc_done"), sem("qt_done"), sem("qs_done"), sem("sqr_done")
        ssq_done, nrm_copied, nrm_root, qk_ready = sem("ssq_done"), sem("nrm_copied"), sem("nrm_root"), sem("qk_ready")
        tails_done = sem("tails_done")
        ab_done, ab_copied, ab_act, ab_dve = sem("ab_done"), sem("ab_copied"), sem("ab_act"), sem("ab_dve")
        glu_done, conv_done, z_done, d_made = sem("glu_done"), sem("conv_done"), sem("z_done"), sem("d_made")
        ln_sum, ln_cent, ln_sq, ln_sqs = sem("ln_sum"), sem("ln_cent"), sem("ln_sq"), sem("ln_sqs")
        ln_std, ln_norm, aff_done = sem("ln_std"), sem("ln_norm"), sem("aff_done")
        yp_seen = sem("yp_seen")
        csig, csilu = sem("csig"), sem("csilu")
        split_hi, split_lo = sem("split_hi"), sem("split_lo")
        yp_done, mix_done = sem("yp_done"), sem("mix_done")
        dmm, d_act, d_dve = sem("dmm"), sem("d_act"), sem("d_dve")
        gb_made, dif_made, kdec_made, eg_made = sem("gb_made"), sem("dif_made"), sem("kdec_made"), sem("eg_made")
        arg_made, dec_made, xy0_made = sem("arg_made"), sem("dec_made"), sem("xy0_made")
        s_zero, rms_sq, rms_sum, rms_root, o_made = sem("s_zero"), sem("rms_sq"), sem("rms_sum"), sem("rms_root"), sem("o_made")
        vblk_made = sem("vblk_made")
        fraw_in = [sem(f"fraw_in{i}") for i in range(5)]
        f_hi, f_lo, f_done = sem("f_hi"), sem("f_lo"), sem("f_done")
        f_silu, f_uev, f_dev, f_h = sem("f_silu"), sem("f_uev"), sem("f_dev"), sem("f_h")
        f_hhi, f_hlo, acc_init = sem("f_hhi"), sem("f_hlo"), sem("acc_init")
        rt_done, rt_top, rt_exp, gx_made, gb_done, gb_copied = (
            sem("rt_done"), sem("rt_top"), sem("rt_exp"), sem("gx_made"), sem("gb_done"), sem("gb_copied"))
        pos_done, pos_made, flag_made = sem("pos_done"), sem("pos_made"), sem("flag_made")
        xt_mm, xt_act, xt_dve = sem("xt_mm"), sem("xt_act"), sem("xt_dve")
        m_raw = [sem(f"m_raw{i}") for i in range(MRAW)]
        m_hi, m_lop, m_lod, m_done = sem("m_hi"), sem("m_lop"), sem("m_lod"), sem("m_done")
        m_p, m_pt, m_ptc = sem("m_p"), sem("m_pt"), sem("m_ptc")
        m_g, m_xea, m_xev = sem("m_g"), sem("m_xea"), sem("m_xev")
        m_silu, m_h, m_t, m_thi, m_tlo = sem("m_silu"), sem("m_h"), sem("m_t"), sem("m_thi"), sem("m_tlo")
        m_yf, m_yhi, m_ylo, m_sc, m_acc = sem("m_yf"), sem("m_yhi"), sem("m_ylo"), sem("m_sc"), sem("m_acc")
        acc_ready = sem("acc_ready")
        block = ctx.enter_context(nc.Block())

        def rows(t):
            return 128 if t < 2 else 64

        def cols(t):
            return slice(128 * t, 128 * t + rows(t))

        def groups_of(u):
            return ["act"] if u < U_YP else ["act"] * 8 if u < U_YC else ["dve"] * 2 if u < U_WO else ["dve"]

        GROUPS = [k for u in range(NU) for k in groups_of(u)]
        FIRST = [sum(len(groups_of(v)) for v in range(u)) for u in range(NU)]

        def evicted(l, g):
            k = GROUPS[g]
            return (evict_act if k == "act" else evict_dve), l * GROUPS.count(k) + GROUPS[:g + 1].count(k)

        def bank_free(eng, l, g):
            n = l * len(GROUPS) + g - 4
            if n >= 0:
                eng.wait_ge(*evicted(*divmod(n, len(GROUPS))))

        def gbank(l, g):
            return PS[(l * len(GROUPS) + g) % 4]

        def products(t):
            out = [("gc", "act"), ("R", "dve"), ("kt", "dve"), ("vt", "dve"), ("G", "dve"), ("A", "dve"), ("NT", "act")]
            top = 5 if t < 2 else 2
            for s in range(1, top + 1):
                out += [(f"t{s}", "dve")] + ([(f"x{s}", "dve")] if s < top else []) + [(f"y{s}", "dve")]
            if t < 2:
                out += [("u", "act"), ("w", "act")]
                for c in range(2):
                    out += [(f"p{c}", "dve"), (f"o{c}", "act"), (f"s{c}", "dve")]
            else:
                out += [("u", "act"), ("w", "act"), ("p", "dve"), ("v", "act"), ("o", "act")]
                out += [(f"s{h}{b}", "dve") for h in range(H) for b in range(2)]
            return out

        PROD = [(t, n, e) for t in range(3) for n, e in products(t)]
        KINDS = [e for _, _, e in PROD]

        def number(l, t, name):
            return l * len(PROD) + [(a, b) for a, b, _ in PROD].index((t, name))

        def consumed(j):
            l, i = divmod(j, len(PROD))
            return (d_act if KINDS[i] == "act" else d_dve), l * KINDS.count(KINDS[i]) + KINDS[:i + 1].count(KINDS[i])

        def read(l, t, name):
            return consumed(number(l, t, name))

        def dbank(j):
            return PS[4 + j % 4]

        SPL, NSPL = {"d": 0, "c": 4, "o": 8, "m": 12, "x1": 20, "x2": 28}, 36

        def split(l, name, i):
            return 8 + l * NSPL + SPL[name] + i + 1

        def x_split(l):
            return 8 if l == 0 else split(l - 1, "x2", 7)

        LNT = [4, 8, 8]

        def ln_at(l, w):
            return l * sum(LNT) + sum(LNT[:w])

        def e_range(l):
            return (0, 2) if l == 0 else (2, 2 + NE)

        def mwidth(i):
            return FUNIT if i < MG + MU else D

        def m_rest(e, i):
            mine = i in MPOOL
            k = sum((v in MPOOL) == mine for v in range(i + 1))
            n = len(MPOOL) if mine else MN - len(MPOOL)
            return (m_lop if mine else m_lod), e * n + (n + k)

        def m_rest_before(e, i):
            i -= MRAW
            if i >= 0:
                return m_rest(e, i)
            i += MP
            if i == MN:
                i -= MRAW
            mine = i in MPOOL
            return (m_lop if mine else m_lod), e * (len(MPOOL) if mine else MN - len(MPOOL)) + sum(
                (v in MPOOL) == mine for v in range(i + 1))

        def m_before(e, i):
            i -= MS
            if i >= 0:
                return m_done, e * MN + (MN + i + 1)
            i += MP
            if i == MN:
                i -= MS
            return m_done, e * MN + (i + 1)

        def m_loaded(e, i):
            n = len(range(i % MRAW, MN, MRAW))
            return m_raw[i % MRAW], e * (n * 16) + (i // MRAW + 1) * 16

        def overflow(eng):
            eng.wait_ge(flag_made, 1)
            return eng.value_load(flag[0:1, 0:1], min_val=0, max_val=1) > 0

        STEPS = []
        for u in range(N_QKV):
            STEPS += [("unit", u), ("qconv", u)] + ([("qact", u - 1)] if u else []) + ([("ssq", u - 2)] if 2 <= u < 10 else [])
        STEPS += [("unit", U_AB), ("qact", 11), ("ab", 0)]
        for i in range(1, N_AB):
            STEPS += [("unit", U_AB + i)] + ([("glu", i // 2)] if i % 2 else [])
        STEPS += [("norms", 0)]
        STEPS += [("unit", U_POOL + i) for i in range(N_POOL)]
        STEPS += [("unit", U_Z + i) for i in range(N_Z)]
        STEPS += [("pool", i) for i in range(4)]
        STEPS += [("conv", i) for i in range(4)]
        STEPS += [("unit", U_G + i) for i in range(24)]
        STEPS += [("unit", U_YP), ("ln", 0)]
        STEPS += [("unit", U_YC + i) for i in range(4)]
        for t in range(3):
            STEPS += [("delta", (t, n)) for n, _ in products(t)]
        STEPS += [("rms", 0)]
        STEPS += [("unit", U_YD + i) for i in range(4)]
        STEPS += [("mix", i) for i in range(8)]
        STEPS += [("unit", U_WO + i) for i in range(8)]
        STEPS += [("ln", 1)]

        @block.sync
        def _(sp):
            for dst, src in ((X[:, :, :], io["x"]), (con[:, :], io["con"]), (wrt[:, :, :], io["w_router"]),
                             (par[:, :, :], io["par"]), (brt[:, :], io["b_router"])):
                sp.dma_start(dst, src).then_inc(in_ready, 16)

            def load_block(l, b):
                n = l * NB + b
                if n >= 3:
                    m, c = divmod(n - 3, NB)
                    sp.wait_ge(w_lo, m * NU + min(2 * c + 2, NU))
                w = min(2, NU - 2 * b)
                sp.dma_start(raw[:, n % 3, 0:w, :], io["w_mix"][l, :, 2 * b:2 * b + w, :]).then_inc(raw_in[n % 3], 16)

            def load_experts(l):
                lo, hi = e_range(l)
                with sp.Fori(lo, hi) as e:
                    for i in range(FU):
                        sp.wait_ge(f_lo, e * FU + (i + 1))
                        k = KT if i < 2 * FT else FT
                        if l == 0:
                            o = i * UNIT if i < 2 * FT else 2 * FT * UNIT + (i - 2 * FT) * FUNIT
                            src = io["w_ffn"][bass.ds(e, 1), :, o:o + k * 128].rearrange("e p n -> p (e n)")
                            dst = fraw[:, i % 5, 0:k * 128]
                        else:
                            w = io["w_moe"][bass.ds(e - lo, 1)].rearrange("e p n -> p (e n)")
                            if i < 2 * FT:
                                o, n, c = (i % 2) * MG * FUNIT, FUNIT, i // 2
                            else:
                                o, n, c = (MG + MU) * FUNIT, D, i - 2 * FT
                            src = w[:, o:o + k * n].rearrange("p (k n) -> p k n", n=n)[:, :, 128 * c:128 * c + 128]
                            dst = fraw[:, i % 5, 0:k * 128].rearrange("p (k n) -> p k n", n=128)
                        sp.dma_start(dst, src).then_inc(fraw_in[i % 5], 16)

            for l in range(DEPTH):
                for b in range(2):
                    load_block(l, b)
                if l:
                    sp.wait_ge(split_lo, x_split(l))
                for dst, src in ((wab[:, :, :], io["w_ab"][l]), (qh[:, :, :, :], io["st_qkv"][l]),
                                 (cxs[:, :, :, :], io["st_conv"][l]), (pxs[:, :, :, :], io["st_pool"][l])):
                    sp.dma_start(dst, src).then_inc(state_in, 16)
                for b in range(2, NB):
                    load_block(l, b)
                    if b == (U_G + 20) // 2:
                        sp.wait_ge(glu_done, 4 * (l + 1))
                        sp.wait_ge(*evicted(l, U_Z))
                        sp.wait_ge(tails_done, 12 * (l + 1))
                        for dst, src in ((io["o_conv_p"][l], cxp[:, :, SEQ:]), (io["o_conv_s"][l], cxs[:, :, :, :]),
                                         (io["o_pool_p"][l], pxp[:, :, SEQ:]), (io["o_pool_s"][l], pxs[:, :, :, :]),
                                         (io["o_qkv_p"][l], tp[:, :, :]), (io["o_qkv_s"][l], ts[:, :, :, :])):
                            sp.dma_start(dst, src).then_inc(out_done, 16)
                    if b == (U_YP + 2) // 2:
                        sp.wait_ge(d_made, 4 * (l + 1))
                        sp.wait_ge(conv_done, 4 * (l + 1))
                        sp.wait_ge(out_done, (l * 8 + 6) * 16)
                        sp.dma_start(Ss[:, :, :, :], io["st_delta"][l]).then_inc(ss_in, 16)
                    if b == (U_WO + 0) // 2:
                        sp.wait_ge(*read(l, 1, "s1"))
                        sp.dma_start(io["o_delta_p"][l], S[:, :, :]).then_inc(out_done, 16)
                        sp.wait_ge(*read(l, 2, "s31"))
                        sp.dma_start(io["o_delta_s"][l], Ss[:, :, :, :]).then_inc(out_done, 16)
                sp.wait_ge(out_done, (l + 1) * 8 * 16)
                sp.wait_ge(split_lo, split(l, "m", 7))
                if l == 0:
                    load_experts(l)
                else:
                    with sp.Fori(0, NE) as e:
                        for i in range(MN):
                            sp.wait_ge(*m_rest_before(e, i))
                            o = min(i, MG + MU) * FUNIT + max(i - MG - MU, 0) * D
                            sp.dma_start(mraw[:, i % MRAW, 0:mwidth(i)],
                                         io["w_moe"][bass.ds(e, 1), :, o:o + mwidth(i)].rearrange("e p n -> p (e n)"))\
                                .then_inc(m_raw[i % MRAW], 16)
                    with sp.If(overflow(sp)):
                        sp.wait_ge(m_acc, 2 + 8 * (NE + 1))
                        load_experts(l)
            sp.wait_ge(aff_done, DEPTH * sum(LNT))
            sp.dma_start(io["y"], X[:, :, :]).then_inc(out_done, 16)
            sp.wait_ge(out_done, (8 * DEPTH + 1) * 16)

        @block.gpsimd
        def _(pool):
            def expert_rests(l):
                with pool.Fori(*e_range(l)) as e:
                    for i in range(FU):
                        w = UNIT if i < 2 * FT else FUNIT
                        pool.wait_ge(f_hi, e * FU + (i + 1))
                        pool.tensor_tensor(fl[:, i % 3, 0:w], fraw[:, i % 5, 0:w],
                                           fh[:, i % 3, 0:w].bitcast(f32), ALU.subtract).then_inc(f_lo, 1)

            pool.sem_inc(f_lo, 5)
            pool.sem_inc(m_lop, len(MPOOL))
            pool.sem_inc(m_lod, MN - len(MPOOL))
            for l in range(DEPTH):
                if l:
                    pool.wait_ge(split_lo, x_split(l))
                for z in (cxp[:, :, 0:CB], pxp[:, :, 0:PB], qxp[:, :, 0:SB], ab[:, :, :]):
                    pool.memset(z, 0.0).then_inc(hist_zero, 1)
                for u in range(NU):
                    n, b = l * NU + u, l * NB + u // 2
                    pool.wait_ge(w_hi, n + 1)
                    pool.tensor_tensor(Wl[:, n % 3, :], raw[:, b % 3, u % 2, :],
                                       Wh[:, n % 3, :].bitcast(f32), ALU.subtract).then_inc(w_lo, 1)
                if l == 0:
                    expert_rests(l)
                else:
                    with pool.Fori(0, NE) as e:
                        for i in MPOOL:
                            w = mwidth(i)
                            pool.wait_ge(m_hi, e * MN + (i + 1))
                            pool.tensor_tensor(ml[:, i % MS, 0:w], mraw[:, i % MRAW, 0:w],
                                               mh[:, i % MS, 0:w].bitcast(f32), ALU.subtract).then_inc(m_lop, 1)
                    with pool.If(overflow(pool)):
                        expert_rests(l)

        @block.scalar
        def _(act):
            steps = [0]

            def link(ins):
                steps[0] += 1
                ins.then_inc(ach, 1)
                act.wait_ge(ach, steps[0])

            def head(n):
                if n >= DEPTH * NU:
                    return
                l, u = divmod(n, NU)
                b = l * NB + u // 2
                act.wait_ge(raw_in[b % 3], (b // 3 + 1) * 16)
                if n >= 3:
                    act.wait_ge(unit_done, n - 2)
                act.activation(Wh[:, n % 3, :], raw[:, b % 3, u % 2, :], ACT.Copy).then_inc(w_hi, 1)

            def unit(l, u):
                n = l * NU + u
                if u < U_WO + 6:
                    head(n + 2)
                if u >= U_YP:
                    return
                act.wait_ge(unit_done, n + 1)
                bank = gbank(l, FIRST[u])
                pr, sa = bank[:, 0:SEQ], bank[:, SEQ:T].rearrange("p (b t) -> p b t", b=NSEQ)
                if u < U_AB:
                    if u >= 2:
                        act.wait_ge(qc_done, l * 12 + u - 1)
                    if u == 0:
                        act.wait_ge(hist_zero, 4 * (l + 1))
                        act.wait_ge(state_in, 64 * (l + 1))
                    act.activation(qxs[:, u % 2, :, 0:SB], qh[:, u, :, :], ACT.Copy)
                    act.activation(tp[:, u, :], bank[:, SEQ - SB:SEQ], ACT.Copy)
                    act.activation(ts[:, u, :, :], sa[:, :, TS - SB:TS], ACT.Copy).then_inc(tails_done, 1)
                    act.activation(qxp[:, u % 2, SB:], pr, ACT.Copy)
                    act.activation(qxs[:, u % 2, :, SB:], sa, ACT.Copy).then_inc(evict_act, 1)
                elif u < U_POOL:
                    i = (u - U_AB) // 2
                    if (u - U_AB) % 2 == 0:
                        act.activation(cxp[:, i, CB:], pr, ACT.Copy, scale=0.5)
                        act.activation(cxs[:, i, :, CB:], sa, ACT.Copy, scale=0.5).then_inc(evict_act, 1)
                    else:
                        if i:
                            act.wait_ge(glu_done, l * 4 + i)
                        act.activation(std[:, :], bank[:, 0:T], ACT.Tanh, scale=0.5).then_inc(evict_act, 1)
                elif u < U_Z:
                    act.activation(pxp[:, u - U_POOL, PB:], pr, ACT.Copy)
                    act.activation(pxs[:, u - U_POOL, :, PB:], sa, ACT.Copy).then_inc(evict_act, 1)
                elif u < U_G:
                    i = u - U_Z
                    if i >= 2:
                        act.wait_ge(z_done, l * 4 + i - 1)
                    act.activation(Z[:, i, :], bank[:, 0:T], ACT.Copy)
                    act.activation(sq[:, i % 2, :], bank[:, 0:T], ACT.Tanh, scale=0.5).then_inc(evict_act, 1)
                else:
                    act.activation(G[:, u - U_G, :], bank[:, 0:T], ACT.Tanh, scale=0.5).then_inc(evict_act, 1)

            def pooled_out(l):
                for m in range(8):
                    g = FIRST[U_YP] + m
                    act.wait_ge(yp_seen, l * 8 + m + 1)
                    if m >= 2:
                        act.wait_ge(yp_done, l * 8 + m - 1)
                    act.activation(yb[:, m % 2, :], gbank(l, g)[:, 0:T], ACT.Copy, scale=P(l, "pscale", m))\
                        .then_inc(evict_act, 1)

            def qact(l, i):
                dst = (qT, kT, vT)[i // 4][:, i % 4, :]
                act.wait_ge(qc_done, l * 12 + i + 1)
                if i >= 2:
                    act.wait_ge(qs_done, l * 12 + i - 1)
                act.activation(yb[:, i % 2, :], dst, ACT.Tanh, scale=0.5).then_inc(qt_done, 1)
                if i < 8:
                    act.wait_ge(qs_done, l * 12 + i + 1)
                    if i >= 2:
                        act.wait_ge(ssq_done, l * 8 + i - 1)
                    act.activation(sq[:, i % 2, :], dst, ACT.Square).then_inc(sqr_done, 1)

            def ssq(l, i):
                act.wait_ge(ssq_done, l * 8 + i + 1)
                act.activation(nrm[:, i, :], PS[4 + i % 2][:, 0:T], ACT.Copy).then_inc(nrm_copied, 1)

            def norms(l):
                act.wait_ge(nrm_copied, 8 * (l + 1))
                act.activation(nrm[:, :, :], nrm[:, :, :], ACT.Sqrt, bias=4e-6).then_inc(nrm_root, 1)

            def ab_part(l):
                act.wait_ge(ab_done, l + 1)
                for t in range(3):
                    ins = act.activation(ab[0:rows(t), t, :], PS[6][0:rows(t), 8 * t:8 * t + 8], ACT.Copy)
                ins.then_inc(ab_copied, 1)
                act.wait_ge(ab_dve, 2 * l + 1)
                link(act.activation(tmp3[:, 1, :, :], tmp3[:, 0, :, :], ACT.Abs))
                link(act.activation(tmp3[:, 1, :, :], tmp3[:, 1, :, :], ACT.Exp, scale=-1.0))
                act.activation(tmp3[:, 1, :, :], tmp3[:, 1, :, :], ACT.Ln, bias=1.0).then_inc(ab_act, 1)
                act.activation(tmp3[:, 2, 0, :], par[:, l, PAR["a_log"][0]:PAR["a_log"][0] + 4], ACT.Exp).then_inc(ab_act, 1)
                act.activation(sc[:, 1, :, :], ab[:, :, 4:8], ACT.Tanh, scale=0.5).then_inc(ab_act, 1)

            def ln(l, w):
                k, n0, n = LNT[w], ln_at(l, w), 3 * l + w
                src = (cacc, X, acc)[w]
                for m in range(k):
                    act.wait_ge(ln_cent, n0 + m + 1)
                    if m >= 2:
                        act.wait_ge(ln_sqs, n0 + m - 1)
                    act.activation(sq[:, m % 2, :], src[:, m, :], ACT.Square).then_inc(ln_sq, 1)
                act.wait_ge(ln_sqs, n0 + k)
                act.activation(std[:, :], PS[7][:, 0:T], ACT.Sqrt, scale=1.0 / (128 * k),
                               bias=(1e-5, 4e-5, 1e-5)[w]).then_inc(ln_std, 1)
                gname, bname = (("cg", "cb"), ("ln1_g", "ln1_b"), ("ln2_g", "ln2_b"))[w]
                dst = (cacc, X, X)[w]
                for m in range(k):
                    act.wait_ge(ln_norm, n0 + m + 1)
                    act.activation(dst[:, m, :], dst[:, m, :], ACT.Identity, scale=P(l, gname, m), bias=P(l, bname, m))\
                        .then_inc(aff_done, 1)
                if w == 0:
                    for m in range(k):
                        act.wait_ge(aff_done, n0 + m + 1)
                        if m >= 2:
                            act.wait_ge(csilu, l * 4 + m - 1)
                        act.activation(sq[:, m % 2, :], cacc[:, m, :], ACT.Tanh, scale=0.5).then_inc(csig, 1)
                    for m in range(k):
                        act.wait_ge(csilu, l * 4 + m + 1)
                        act.activation(Xh[:, m, :], cacc[:, m, :], ACT.Copy, scale=0.5).then_inc(split_hi, 1)
                elif (l, w) != (DEPTH - 1, 2):
                    act.wait_ge(aff_done, n0 + k)
                    for m in range(k):
                        act.activation(Xh[:, m, :], X[:, m, :], ACT.Copy).then_inc(split_hi, 1)

            def pool_head(l, i):
                act.wait_ge(d_made, l * 4 + i + 1)
                act.activation(dh[:, i, :], tt[:, i % 2, :], ACT.Copy).then_inc(split_hi, 1)

            def delta(l, t, name):
                j, r = number(l, t, name), rows(t)
                b = dbank(j)
                b4 = b[:, 0:4 * r].rearrange("p (h n) -> p h n", h=H)
                if dict(products(t)).get(name) == "act" or name == "R":
                    act.wait_ge(dmm, j + 1)
                inc = consumed(j)[0]
                if name == "gc":
                    act.activation(sc[0:r, 3:5, t, :], b[0:r, 0:8].rearrange("p (a h) -> p a h", a=2), ACT.Copy)
                    act.activation(sc[0:r, 5, t, :], b[0:r, 0:4], ACT.Exp)
                    act.activation(gs[:, :, :], b[:, 16:48].rearrange("p (h n) -> p h n", h=H), ACT.Exp).then_inc(inc, 1)
                    act.wait_ge(dif_made, l * 3 + t + 1)
                    act.activation(sc[0:r, 7, t, :], sc[0:r, 7, t, :], ACT.Exp).then_inc(kdec_made, 1)
                elif name == "R":
                    act.activation(eg[:, :, 0:r], b4, ACT.Exp).then_inc(eg_made, 1)
                    act.wait_ge(arg_made, l * 3 + t + 1)
                    act.activation(dec[0:r, :, 0:r], dec[0:r, :, 0:r], ACT.Exp, scale=-1.0)
                    act.activation(decT[0:r, :, 0:r], decT[0:r, :, 0:r], ACT.Exp).then_inc(dec_made, 1)
                elif name == "NT":
                    act.activation(NT[0:r, :, 0:r], b4[0:r], ACT.Copy).then_inc(inc, 1)
                elif name == "u":
                    if t < 2:
                        act.activation(uu[:, :, :], b4, ACT.Copy).then_inc(inc, 1)
                    else:
                        act.activation(uu[:, :, 0:r], b4, ACT.Copy).then_inc(inc, 1)
                elif name == "w":
                    act.activation(wT[:, :, 0:r], b4, ACT.Copy).then_inc(inc, 1)
                elif name == "v":
                    act.activation(vn[0:r, :, :], b[0:r, :].rearrange("p (h n) -> p h n", h=H), ACT.Copy).then_inc(inc, 1)
                elif name in ("o0", "o1", "o"):
                    c0 = 128 * t + (64 if name == "o1" else 0)
                    act.activation(oT[:, :, c0:c0 + 64], b[:, 0:256].rearrange("p (h n) -> p h n", h=H), ACT.Copy)\
                        .then_inc(inc, 1)

            def rms(l):
                act.wait_ge(*read(l, 2, "o"))
                for h in range(H):
                    if h >= 2:
                        act.wait_ge(rms_sum, l * 4 + h - 1)
                    act.activation(sq[:, h % 2, :], oT[:, h, :], ACT.Square).then_inc(rms_sq, 1)
                for h in range(H):
                    act.wait_ge(rms_sum, l * 4 + h + 1)
                    act.activation(rmsr[:, h, :], PS[4 + h][:, 0:T], ACT.Sqrt, scale=1.0 / 128, bias=1e-6)\
                        .then_inc(rms_root, 1)
                for h in range(H):
                    act.wait_ge(o_made, l * 4 + h + 1)
                    act.activation(Xh[:, 4 + h, :], oT[:, h, :], ACT.Copy).then_inc(split_hi, 1)

            def mix(l, m):
                act.wait_ge(mix_done, l * 8 + m + 1)
                act.activation(Mh[:, m, :], G[:, m, :], ACT.Copy).then_inc(split_hi, 1)

            def ffn(l):
                lo, hi = e_range(l)

                def fhead(e, i):
                    w = UNIT if i < 2 * FT else FUNIT
                    act.wait_ge(fraw_in[i % 5], e * (FU // 5 * 16) + (i // 5 + 1) * 16)
                    act.wait_ge(f_done, e * FU + (i + 1))
                    act.activation(fh[:, i % 3, 0:w], fraw[:, i % 5, 0:w], ACT.Copy).then_inc(f_hi, 1)

                def hhead(e, j):
                    if l == 0:
                        act.wait_ge(f_uev, e * FT + (2 + j + 1))
                    else:
                        act.wait_ge(f_h, (e - lo) * FT + (j + 1))
                    act.activation(Hh[:, j, :], hf[:, j % 2, :], ACT.Copy).then_inc(f_hhi, 1)

                with act.Fori(lo, hi) as e:
                    fhead(e, 0)
                    fhead(e, 1)
                    for j in range(FT):
                        fhead(e, 2 * j + 2)
                        if 2 * j + 3 < 2 * FT:
                            fhead(e, 2 * j + 3)
                        act.wait_ge(f_done, e * FU + (3 + 2 * j + 1))
                        act.wait_ge(f_uev, e * FT + (j + 1))
                        act.activation(sg[:, j % 2, :], PS[2 * j % 6][:, 0:T], ACT.Silu).then_inc(f_silu, 1)
                        if j:
                            hhead(e, j - 1)
                    hhead(e, FT - 1)
                    for i in range(2 * FT + 1, FU):
                        fhead(e, i)

            def router(l):
                act.wait_ge(rt_top, 1)
                act.activation(rk[:, 2], rk[:, 2], ACT.Exp).then_inc(rt_exp, 1)

            def gates_everywhere():
                for t in range(3):
                    for half in range(2):
                        act.wait_ge(gb_done, 2 * t + half + 1)
                        act.activation(gbc[:, 4 * half:4 * half + 4, cols(t)],
                                       PS[6 + half][:, :].rearrange("p (e n) -> p e n", e=4)[:, :, 0:rows(t)], ACT.Copy)\
                            .then_inc(gb_copied, 1)

            def experts():
                for q in range(0, 12, 2):
                    t, half, lo = q // 4, q // 2 % 2, q % 2
                    act.wait_ge(xt_mm, q + 1)
                    act.activation(xth[0:rows(t), t, 512 * half:512 * half + 512], PS[q % 6][0:rows(t), :], ACT.Copy)\
                        .then_inc(xt_act, 1)

                def mhead(e, i):
                    act.wait_ge(*m_loaded(e, i))
                    act.wait_ge(*m_before(e, i))
                    act.activation(mh[:, i % MS, 0:mwidth(i)], mraw[:, i % MRAW, 0:mwidth(i)], ACT.Copy).then_inc(m_hi, 1)

                def gathered(e, n):
                    act.wait_ge(m_g, e * 4 + (n + 1))
                    dst = (xeh if n == 0 else xel)[:, 0:4, :]
                    act.activation(dst, PS[(7, 6, 0, 1)[n]][:, :].rearrange("p (k n) -> p k n", k=4), ACT.Copy)\
                        .then_inc(m_xea, 1)

                def y_head(e):
                    act.wait_ge(m_yf, e + 1)
                    act.activation(yh[:, :], yf[:, :], ACT.Copy).then_inc(m_yhi, 1)

                gathered(0, 0)
                gathered(0, 2)
                with act.Fori(0, NE) as e:
                    mhead(e, 0)
                    mhead(e, 1)
                    mhead(e, 2)
                    y_head(e)
                    for i in range(MN):
                        if i + 3 < MN:
                            mhead(e, i + 3)
                        if i == MG - 1:
                            act.wait_ge(m_done, e * MN + (MN + MG))
                            for c in range(3):
                                n = min(512, FUNIT - 512 * c)
                                act.activation(sg1[:, 512 * c:512 * c + n], PS[c][:, 0:n], ACT.Silu).then_inc(m_silu, 1)
                        if i == 7 + SCAT:
                            act.wait_ge(m_pt, e + 1)
                            act.activation(gslot[:, :], PS[6][:, T:T + 1], ACT.Copy)
                            act.activation(PT[:, :], PS[6][:, 0:T], ACT.Copy).then_inc(m_ptc, 1)
                        if i == MG + MU - 1:
                            gathered(e + 1, 0)
                            gathered(e + 1, 2)
                            for c in range(3):
                                k = min(4, FT - 4 * c)
                                act.wait_ge(m_t, e * 3 + (c + 1))
                                act.activation(hTh[:, 4 * c:4 * c + k, :],
                                               PS[3 + c][:, 0:128 * k].rearrange("p (k n) -> p k n", k=k), ACT.Copy)\
                                    .then_inc(m_thi, 1)
                y_head(NE)

            act.wait_ge(in_ready, 80)
            for m in range(KT):
                act.activation(Xh[:, m, :], X[:, m, :], ACT.Copy).then_inc(split_hi, 1)
            head(0)
            head(1)
            for l in range(DEPTH):
                for kind, x in STEPS:
                    if kind == "unit":
                        unit(l, x)
                        if x == U_YP:
                            pooled_out(l)
                    elif kind == "qact":
                        qact(l, x)
                    elif kind == "ssq":
                        ssq(l, x)
                    elif kind == "norms":
                        norms(l)
                    elif kind == "ab":
                        ab_part(l)
                    elif kind == "pool":
                        pool_head(l, x)
                    elif kind == "ln":
                        ln(l, x)
                    elif kind == "delta":
                        delta(l, *x)
                    elif kind == "rms":
                        rms(l)
                    elif kind == "mix":
                        mix(l, x)
                act.wait_ge(aff_done, ln_at(l, 2))
                act.activation(acc[:, :, :], X[:, :, :], ACT.Copy, scale=ALPHA).then_inc(acc_init, 1)
                if l == 0:
                    ffn(l)
                else:
                    router(l)
                    experts()
                    with act.If(overflow(act)):
                        act.wait_ge(m_acc, 2 + 8 * (NE + 1))
                        act.activation(acc[:, :, :], X[:, :, :], ACT.Copy, scale=ALPHA).then_inc(acc_init, 1)
                        gates_everywhere()
                        ffn(l)
                ln(l, 2)
                head((l + 1) * NU)
                head((l + 1) * NU + 1)

        @block.tensor
        def _(pe):
            def mm3(out, wh, wl, xh, xl, start, stop):
                pe.matmul(out, wl, xh, start=start, stop=False)
                pe.matmul(out, wh, xl, start=False, stop=False)
                return pe.matmul(out, wh, xh, start=False, stop=stop)

            def unit(l, u):
                n = l * NU + u
                g = FIRST[u]
                hi, lo = Wh[:, n % 3, :], Wl[:, n % 3, :]
                if u == 0:
                    pe.wait_ge(split_lo, x_split(l))
                pe.wait_ge(w_lo, n + 1)
                if u < U_YP or u >= U_WO:
                    xh, xl = (Xh, Xl) if u < U_YP else (Mh, Ml)
                    if u == U_WO:
                        pe.wait_ge(split_lo, split(l, "m", 7))
                    bank_free(pe, l, g)
                    for k in range(KT):
                        c = slice(128 * k, 128 * k + 128)
                        ins = mm3(gbank(l, g)[:, 0:T], hi[:, c], lo[:, c], xh[:, k, :], xl[:, k, :], k == 0, k == KT - 1)
                elif u == U_YP:
                    pe.wait_ge(split_lo, split(l, "d", 3))
                    for m in range(8):
                        bank_free(pe, l, g + m)
                        c = slice(128 * m, 128 * m + 128)
                        ins = mm3(gbank(l, g + m)[:, 0:T], hi[:, c], lo[:, c], dh[:, m // 2, :], dl[:, m // 2, :], True, True)
                        ins.then_inc(yp_seen, 1)
                    pe.wait_ge(yp_seen, (l + 1) * 8)
                    pe.sem_inc(unit_done, 1)
                    return
                else:
                    k0 = 0 if u < U_YD else 4
                    if u in (U_YC, U_YD):
                        pe.wait_ge(split_lo, split(l, "c" if u < U_YD else "o", 3))
                    for m in range(2):
                        bank_free(pe, l, g + m)
                        for k in range(4):
                            c = slice(512 * m + 128 * k, 512 * m + 128 * k + 128)
                            ins = mm3(gbank(l, g + m)[:, 0:T], hi[:, c], lo[:, c], Xh[:, k0 + k, :], Xl[:, k0 + k, :],
                                      k == 0, k == 3)
                ins.then_inc(unit_done, 1)

            def ssq(l, i):
                pe.wait_ge(sqr_done, l * 8 + i + 1)
                if i >= 2:
                    pe.wait_ge(nrm_copied, l * 8 + i - 1)
                pe.matmul(PS[4 + i % 2][:, 0:T], C("ones"), sq[:, i % 2, :], start=True, stop=True).then_inc(ssq_done, 1)

            def ab_part(l):
                for t in range(3):
                    for k in range(KT):
                        ins = pe.matmul(PS[6][0:rows(t), 8 * t:8 * t + 8], X[:, k, cols(t)], wab[:, k, :],
                                        start=(k == 0), stop=(k == KT - 1))
                ins.then_inc(ab_done, 1)

            def ln(l, w):
                k, n0 = LNT[w], ln_at(l, w)
                src = (cacc, X, acc)[w]
                for m in range(k):
                    if w == 0:
                        pe.wait_ge(conv_done, l * 4 + m + 1)
                    elif w == 1:
                        pe.wait_ge(*evicted(l, FIRST[U_WO + m]))
                    else:
                        pe.wait_ge(acc_ready, l + 1)
                    ins = pe.matmul(PS[6][:, 0:T], C("ones"), src[:, m, :], start=(m == 0), stop=(m == k - 1))
                ins.then_inc(ln_sum, 1)
                for m in range(k):
                    pe.wait_ge(ln_sq, n0 + m + 1)
                    pe.matmul(PS[7][:, 0:T], C("ones"), sq[:, m % 2, :], start=(m == 0), stop=(m == k - 1))\
                        .then_inc(ln_sqs, 1)

            def delta(l, t, name):
                j, r = number(l, t, name), rows(t)
                if j % len(PROD) >= 4:
                    pe.wait_ge(*consumed(j - 4))
                b = dbank(j)
                p = "s" if t == 2 else "p"
                cum = C("cum_" + p, r)
                heads = range(H)
                cs = cols(t)

                def out4(h, m, n):
                    return b[0:m, n * h:n * h + n]

                if name == "gc":
                    pe.wait_ge(gb_made, l * 3 + t + 1)
                    pe.matmul(b[0:r, 0:4], cum, sc[0:r, 0, t, :], start=True, stop=True)
                    pe.matmul(b[0:r, 4:8], C("blk_" + p, r), sc[0:r, 0, t, :], start=True, stop=True)
                    ni = 2 if t < 2 else 8
                    for h in heads:
                        ins = pe.matmul(b[:, 16 + 8 * h:24 + 8 * h], gb[0:r, h, :], C("ind_" + p, r), start=True, stop=True)
                elif name == "R":
                    for h in heads:
                        ins = pe.matmul(out4(h, 128, r), gb[0:r, h, :], cum, start=True, stop=True)
                elif name in ("kt", "vt"):
                    if name == "kt":
                        pe.wait_ge(qk_ready, l + 1)
                        pe.wait_ge(qs_done, (l + 1) * 12)
                    src = kT if name == "kt" else vT
                    for h in heads:
                        ins = pe.transpose(out4(h, r, 128), src[:, h, cs], C("ident"))
                elif name == "G":
                    for h in heads:
                        ins = pe.matmul(out4(h, r, r), kT[:, h, cs], kT[:, h, cs], start=True, stop=True)
                elif name == "A":
                    for h in heads:
                        ins = pe.matmul(out4(h, r, r), kT[:, h, cs], qT[:, h, cs], start=True, stop=True)
                elif name == "NT":
                    pe.wait_ge(*read(l, t, "G"))
                    for h in heads:
                        ins = pe.transpose(out4(h, r, r), NN[0:r, h, 0:r], C("ident", r)[:, 0:r])
                elif name[0] == "t" :
                    s = int(name[1])
                    if s == 1:
                        pe.wait_ge(xy0_made, l * 3 + t + 1)
                    else:
                        pe.wait_ge(*read(l, t, f"y{s - 1}"))
                    for h in heads:
                        ins = pe.matmul(out4(h, r, r), NT[0:r, h, 0:r], XX[0:r, h, 0:r], start=True, stop=True)
                elif name[0] in "xy":
                    pe.wait_ge(*read(l, t, "t" + name[1]))
                    for h in heads:
                        a, c = (YY, T1) if name[0] == "x" else (T1, YY)
                        ins = pe.matmul(out4(h, r, r), a[0:r, h, 0:r], c[0:r, h, 0:r], start=True, stop=True)
                elif name == "u":
                    pe.wait_ge(*read(l, t, "y5" if t < 2 else "y2"))
                    for h in heads:
                        if t < 2:
                            ins = pe.matmul(out4(h, r, 128), YY[0:r, h, 0:r], vb[0:r, h, :], start=True, stop=True)
                        else:
                            ins = pe.matmul(out4(h, 128, r), vb[0:r, h, :], YY[0:r, h, 0:r], start=True, stop=True)
                elif name == "w":
                    for h in heads:
                        ins = pe.matmul(out4(h, 128, r), kb[0:r, h, :], YY[0:r, h, 0:r], start=True, stop=True)
                elif name in ("p0", "p1"):
                    c = int(name[1])
                    pe.wait_ge(*read(l, t, "w"))
                    if (t, c) == (0, 0):
                        pe.wait_ge(s_zero, l + 1)
                    else:
                        pe.wait_ge(*(read(l, t, "s0") if c else read(l, t - 1, "s1")))
                    for h in heads:
                        ins = pe.matmul(out4(h, 128, 128), wT[:, h, :], S[:, h, :], start=True, stop=True)
                elif name in ("o0", "o1"):
                    c = int(name[1])
                    q = slice(64 * c, 64 * c + 64)
                    for h in heads:
                        pe.matmul(out4(h, 128, 64), S[:, h, :], eg[:, h, q], start=(h == 0), stop=False, skip_group_check=True)
                    pe.wait_ge(*read(l, t, f"p{c}"))
                    for h in heads:
                        ins = pe.matmul(out4(h, 128, 64), vn[q, h, :], aT[q, h, q], start=False, stop=(h == H - 1),
                                        skip_group_check=True)
                elif name in ("s0", "s1"):
                    q = slice(64 * int(name[1]), 64 * int(name[1]) + 64)
                    for h in heads:
                        ins = pe.matmul(out4(h, 128, 128), kd[q, h, :], vn[q, h, :], start=True, stop=True)
                elif name == "p":
                    pe.wait_ge(*read(l, t, "w"))
                    pe.wait_ge(ss_in, 16 * (l + 1))
                    for h in heads:
                        for i in range(NSEQ):
                            ins = pe.matmul(b[:, 64 * h + 8 * i:64 * h + 8 * i + 8], Ss[:, h, i, :], wT[:, h, 8 * i:8 * i + 8],
                                            start=True, stop=True)
                elif name == "v":
                    pe.wait_ge(*read(l, t, "p"))
                    for h in heads:
                        ins = pe.transpose(out4(h, r, 128), uu[:, h, 0:r], C("ident"))
                elif name == "o":
                    for h in heads:
                        for i in range(NSEQ):
                            q = slice(8 * i, 8 * i + 8)
                            pe.matmul(b[:, 64 * h + 8 * i:64 * h + 8 * i + 8], Ss[:, h, i, :], eg[:, h, q],
                                      start=(h == 0 and i == 0), stop=False, skip_group_check=True)
                    pe.wait_ge(*read(l, t, "v"))
                    for h in heads:
                        ins = pe.matmul(out4(h, 128, 64), vn[0:64, h, :], aT[0:64, h, 0:64], start=False,
                                        stop=(h == H - 1), skip_group_check=True)
                else:
                    h, half = int(name[1]), int(name[2])
                    if half == 0:
                        pe.wait_ge(vblk_made, l * 4 + h + 1)
                    ins = pe.matmul(b[:, :], kd[0:64, h, :], vblk[:, 4 * half:4 * half + 4, :], start=True, stop=True)
                ins.then_inc(dmm, 1)

            def rms(l):
                for h in range(H):
                    pe.wait_ge(rms_sq, l * 4 + h + 1)
                    if h == 0:
                        pe.wait_ge(*read(l, 2, "s31"))
                    pe.matmul(PS[4 + h][:, 0:T], C("ones"), sq[:, h % 2, :], start=True, stop=True).then_inc(rms_sum, 1)

            def router(l):
                for t in range(3):
                    for k in range(KT):
                        ins = pe.matmul(PS[7][0:rows(t), 8 * t:8 * t + 8], X[:, k, cols(t)], wrt[:, k, :],
                                        start=(k == 0), stop=(k == KT - 1))
                ins.then_inc(rt_done, 1)

            def gates_everywhere():
                for t in range(3):
                    pe.wait_ge(gx_made, t + 2)
                    for e in range(NE):
                        if e % 4 == 0 and t:
                            pe.wait_ge(gb_copied, 2 * t + e // 4 - 1)
                        ins = pe.matmul(PS[6 + e // 4][:, 128 * (e % 4):128 * (e % 4) + rows(t)], gexp[0:rows(t), e, :],
                                        C("ident", rows(t))[:, 0:rows(t)], start=True, stop=True)
                        if e % 4 == 3:
                            ins.then_inc(gb_done, 1)

            def experts():
                for q in range(12):
                    t, half, lo = q // 4, q // 2 % 2, q % 2
                    if q >= 6:
                        pe.wait_ge(*((xt_dve, (q - 6) // 2 + 1) if q % 2 else (xt_act, (q - 6) // 2 + 1)))
                    for k in range(4):
                        ins = pe.transpose(PS[q % 6][0:rows(t), 128 * k:128 * k + 128],
                                           (Xl if lo else Xh)[:, 4 * half + k, cols(t)].bitcast(f32), C("ident"))
                    ins.then_inc(xt_mm, 1)
                pe.wait_ge(gx_made, 1)
                for t in range(3):
                    for s in range(t + 1):
                        pe.matmul(PS[7][0:rows(t), 8 * t:8 * t + 8],
                                  (C("upto", rows(s)) if s == t else C("ones", rows(s)))[:, 0:rows(t)],
                                  rk[0:rows(s), 3, s, :], start=(s == 0), stop=(s == t))
                for s in range(3):
                    ins = pe.matmul(PS[7][:, 32:40], C("ones", rows(s)), rk[0:rows(s), 3, s, :], start=(s == 0), stop=(s == 2))
                ins.then_inc(pos_done, 1)

                def gather(e, n):
                    src, half = (xth if n < 2 else xtl), n % 2
                    for k in range(4):
                        f = 512 * half + 128 * k
                        for t in range(3):
                            ins = pe.matmul(PS[(7, 6, 0, 1)[n]][:, 128 * k:128 * k + 128], src[0:rows(t), t, f:f + 128],
                                            Pm[0:rows(t), t, :], start=(t == 0), stop=(t == 2))
                    ins.then_inc(m_g, 1)

                def scatter(e, m):
                    if m == 0:
                        pe.wait_ge(m_ylo, e + 2)
                    pe.wait_ge(m_acc, e * 8 + (m + 1))
                    c = slice(128 * m, 128 * m + 128)
                    pe.matmul(PS[6 + m % 2][:, 0:T], yl[:, c], PT[:, :], start=True, stop=False)
                    pe.matmul(PS[6 + m % 2][:, 0:T], yh[:, c], PT[:, :], start=False, stop=True).then_inc(m_sc, 1)

                def wide(e, i, banks, w, xh, xl, k, last):
                    pe.wait_ge(*m_rest(e, i))
                    for c in range(len(banks)):
                        n = min(512, w - 512 * c)
                        o = banks[c][:, 0:n]
                        s = slice(512 * c, 512 * c + n)
                        pe.matmul(o, xl[:, k, :], mh[:, i % MS, s], start=(k == 0), stop=False)
                        pe.matmul(o, xh[:, k, :], ml[:, i % MS, s], start=False, stop=False)
                        ins = pe.matmul(o, xh[:, k, :], mh[:, i % MS, s], start=False, stop=(k == last))
                    ins.then_inc(m_done, 1)

                pe.wait_ge(m_p, 1)
                pe.wait_ge(xt_act, 6)
                pe.wait_ge(xt_dve, 6)
                for n in range(4):
                    gather(0, n)
                with pe.Fori(0, NE) as e:
                    pe.wait_ge(m_xea, e * 2 + 2)
                    pe.wait_ge(m_xev, e * 2 + 2)
                    for k in range(8 + SCAT):
                        if k < MG:
                            wide(e, k, PS[0:3], FUNIT, xeh, xel, k, MG - 1)
                        else:
                            wide(e, k, PS[3:6], FUNIT, xeh, xel, k - MG, MU - 1)
                        if k >= SCAT:
                            scatter(e, k - SCAT)
                    pe.wait_ge(m_acc, e * 8 + (2 + 7))
                    for t in range(3):
                        pe.transpose(PS[6][:, cols(t)], Pm[0:rows(t), t, :].bitcast(f32), C("ident", rows(t))[:, 0:rows(t)])
                    for t in range(3):
                        ins = pe.matmul(PS[6][:, T:T + 1], Pm[0:rows(t), t, :].bitcast(f32), gcol[0:rows(t), t:t + 1],
                                        start=(t == 0), stop=(t == 2))
                    ins.then_inc(m_pt, 1)
                    for k in range(SCAT, MU):
                        wide(e, MG + k, PS[3:6], FUNIT, xeh, xel, k, MU - 1)
                    pe.wait_ge(m_p, e + 2)
                    pe.wait_ge(m_acc, e * 8 + (2 + 8))
                    gather(e + 1, 0)
                    pe.wait_ge(m_ptc, e + 1)
                    gather(e + 1, 1)
                    pe.wait_ge(m_silu, e * 3 + 3)
                    gather(e + 1, 2)
                    gather(e + 1, 3)
                    for c in range(3):
                        pe.wait_ge(m_h, e * 3 + (c + 1))
                        for k in range(4 * c, min(4 * c + 4, FT)):
                            ins = pe.transpose(PS[3 + c][:, 128 * (k % 4):128 * (k % 4) + 128], sg1[:, 128 * k:128 * k + 128],
                                               C("ident"))
                        ins.then_inc(m_t, 1)
                    pe.wait_ge(m_xea, e * 2 + 3)
                    pe.wait_ge(m_xev, e * 2 + 3)
                    for k in range(MD):
                        if k % 4 == 0:
                            pe.wait_ge(m_tlo, e * 3 + (k // 4 + 1))
                        wide(e, MG + MU + k, PS[6:8], D, hTh, hTl, k, MD - 1)
                for m in range(8):
                    scatter(NE, m)

            def ffn(l):
                lo, hi = e_range(l)
                with pe.Fori(lo, hi) as e:
                    for i in range(FU):
                        p = i - 6
                        if p < 0:
                            pe.wait_ge(f_dev, e * 8 + (i + 3))
                        elif p < 2 * FT and p % 2 == 0:
                            pe.wait_ge(f_silu, e * FT + (p // 2 + 1))
                        elif p < 2 * FT:
                            pe.wait_ge(f_uev, e * FT + (2 + p // 2 + 1))
                        else:
                            pe.wait_ge(f_dev, e * 8 + (8 + p - 2 * FT + 1))
                        pe.wait_ge(f_lo, e * FU + (5 + i + 1))
                        if i == 2 * FT:
                            pe.wait_ge(f_hlo, e * FT + (2 + FT))
                        n, xh, xl = (KT, Xh, Xl) if i < 2 * FT else (FT, Hh, Hl)
                        for k in range(n):
                            c = slice(128 * k, 128 * k + 128)
                            ins = mm3(PS[i % 6][:, 0:T], fh[:, i % 3, c], fl[:, i % 3, c], xh[:, k, :], xl[:, k, :],
                                      k == 0, k == n - 1)
                        ins.then_inc(f_done, 1)

            pe.sem_inc(m_done, MN)
            pe.sem_inc(m_ylo, 1)
            pe.sem_inc(m_acc, 2)
            pe.sem_inc(f_done, 3)
            pe.sem_inc(f_uev, 2)
            pe.sem_inc(f_hlo, 2)
            pe.sem_inc(f_dev, 8)
            pe.wait_ge(in_ready, 80)
            for l in range(DEPTH):
                for kind, x in STEPS:
                    if kind == "unit":
                        unit(l, x)
                    elif kind == "ssq":
                        ssq(l, x)
                    elif kind == "ab":
                        pe.wait_ge(state_in, 64 * (l + 1))
                        ab_part(l)
                    elif kind == "ln":
                        ln(l, x)
                    elif kind == "delta":
                        delta(l, *x)
                    elif kind == "rms":
                        rms(l)
                pe.wait_ge(split_lo, split(l, "x1", 7))
                if l == 0:
                    ffn(l)
                else:
                    router(l)
                    experts()
                    with pe.If(overflow(pe)):
                        gates_everywhere()
                        ffn(l)
                ln(l, 2)

        @block.vector
        def _(dve):
            steps = [0]

            def step(ins):
                steps[0] += 1
                ins.then_inc(vch, 1)
                return steps[0]

            def link(ins):
                dve.wait_ge(vch, step(ins))

            def seqs(ap):
                return ap.rearrange("p (b t) -> p b t", b=NSEQ)

            def qconv(l, i):
                dst = (qT, kT, vT)[i // 4][:, i % 4, :]
                dve.wait_ge(*evicted(l, i))
                s = i % 2
                last = {}
                for k in range(SK_):
                    w = P(l, "w_short", SK_ * i + k)
                    for part in (0, 1):
                        src = qxp[:, s, k:k + SEQ] if part == 0 else qxs[:, s, :, k:k + TS]
                        out = dst[:, 0:SEQ] if part == 0 else seqs(dst[:, SEQ:T])
                        if k:
                            dve.wait_ge(vch, last[part])
                            ins = dve.scalar_tensor_tensor(out=out, in0=src, scalar=w, in1=out, op0=ALU.mult, op1=ALU.add)
                        else:
                            ins = dve.tensor_scalar(out, src, w, None, ALU.mult)
                        if k == SK_ - 1 and part:
                            ins.then_inc(qc_done, 1)
                        else:
                            last[part] = step(ins)
                dve.wait_ge(vch, last[0])

            def qact(l, i):
                dst = (qT, kT, vT)[i // 4][:, i % 4, :]
                dve.wait_ge(qt_done, l * 12 + i + 1)
                dve.wait_ge(qc_done, l * 12 + i + 1)
                dve.scalar_tensor_tensor(out=dst, in0=yb[:, i % 2, :], scalar=1.0, in1=dst, op0=ALU.add, op1=ALU.mult)\
                    .then_inc(qs_done, 1)

            def glu(l, i):
                dve.wait_ge(*evicted(l, U_AB + 2 * i + 1))
                link(dve.scalar_tensor_tensor(out=cxp[:, i, CB:], in0=std[:, 0:SEQ], scalar=1.0, in1=cxp[:, i, CB:],
                                              op0=ALU.add, op1=ALU.mult))
                dve.scalar_tensor_tensor(out=cxs[:, i, :, CB:], in0=seqs(std[:, SEQ:T]), scalar=1.0,
                                         in1=cxs[:, i, :, CB:], op0=ALU.add, op1=ALU.mult).then_inc(glu_done, 1)

            def z_silu(l, i):
                dve.wait_ge(*evicted(l, U_Z + i))
                dve.scalar_tensor_tensor(out=Z[:, i, :], in0=sq[:, i % 2, :], scalar=1.0, in1=Z[:, i, :],
                                         op0=ALU.add, op1=ALU.mult).then_inc(z_done, 1)

            def ab_part(l):
                a = PAR["dt"][0]
                dve.wait_ge(ab_copied, l + 1)
                dve.tensor_tensor(tmp3[:, 0, :, :], ab[:, :, 0:4], over(par[:, l, a:a + 4], 3), ALU.add).then_inc(ab_dve, 1)
                dve.wait_ge(ab_act, 3 * l + 3)
                dve.wait_ge(ab_dve, 2 * l + 1)
                link(dve.scalar_tensor_tensor(out=tmp3[:, 1, :, :], in0=tmp3[:, 0, :, :], scalar=0.0, in1=tmp3[:, 1, :, :],
                                              op0=ALU.max, op1=ALU.add))
                link(dve.scalar_tensor_tensor(out=sc[:, 0, :, :], in0=tmp3[:, 1, :, :], scalar=-1.0,
                                              in1=over(tmp3[:, 2, 0, :], 3), op0=ALU.mult, op1=ALU.mult))
                link(dve.tensor_scalar(sc[:, 1, :, :], sc[:, 1, :, :], 0.5, 0.5, ALU.mult, ALU.add))
                dve.tensor_scalar(sc[:, 2, :, :], sc[:, 1, :, :], 0.5, None, ALU.mult).then_inc(ab_dve, 1)

            def norms(l):
                dve.wait_ge(nrm_root, l + 1)
                dve.wait_ge(qs_done, l * 12 + 12)
                link(dve.reciprocal(nrm[:, :, :], nrm[:, :, :]))
                dve.scalar_tensor_tensor(out=qT[:, :, :], in0=qT[:, :, :], scalar=128 ** -0.5, in1=nrm[:, 0:4, :],
                                         op0=ALU.mult, op1=ALU.mult)
                dve.tensor_tensor(kT[:, :, :], kT[:, :, :], nrm[:, 4:8, :], ALU.mult).then_inc(qk_ready, 1)

            def pool(l, i):
                w = WINDOWS[i]
                dve.wait_ge(*evicted(l, U_POOL + i))
                d = tt[:, i % 2, :]
                for part in (1, 0):
                    src = pxp[:, i, :] if part == 0 else pxs[:, i, :, :]
                    n = PB + (SEQ if part == 0 else TS)

                    def at(ap, a, b):
                        return ap[:, a:b] if part == 0 else ap[:, :, a:b]

                    bufs = [pw[:, q, :] if part == 0 else pw[:, q, 0:NSEQ * n].rearrange("p (b t) -> p b t", b=NSEQ)
                            for q in (0, 1)]
                    cur, step_, q = src, 1, 0
                    while step_ < w:
                        lo = 2 * step_ - 1
                        link(dve.tensor_tensor(at(bufs[q], lo, n), at(cur, lo, n), at(cur, lo - step_, n - step_), ALU.add))
                        cur, step_, q = bufs[q], 2 * step_, 1 - q
                    out = d[:, 0:SEQ] if part == 0 else seqs(d[:, SEQ:T])
                    link(dve.scalar_tensor_tensor(out=out, in0=at(cur, PB, n), scalar=1.0 / w, in1=at(src, PB, n),
                                                  op0=ALU.mult, op1=ALU.subtract))
                    if part == 0:
                        o = CON["invcnt"][0] + 16 * i
                        link(dve.tensor_tensor(pw[:, q, 0:16], cur[:, PB:PB + 16], con[:, o:o + 16], ALU.mult))
                        dve.tensor_tensor(d[:, 0:16], pw[:, q, 0:16], src[:, PB:PB + 16], ALU.subtract).then_inc(d_made, 1)
                dve.wait_ge(d_made, l * 4 + i + 1)
                dve.wait_ge(split_hi, split(l, "d", i))
                dve.tensor_tensor(dl[:, i, :], d, dh[:, i, :].bitcast(f32), ALU.subtract).then_inc(split_lo, 1)

            def conv(l, i):
                last = {}
                for k in range(CK):
                    w = P(l, "w_dw", CK * i + k)
                    for part in (0, 1):
                        src = cxp[:, i, k:k + SEQ] if part == 0 else cxs[:, i, :, k:k + TS]
                        out = cacc[:, i, 0:SEQ] if part == 0 else seqs(cacc[:, i, SEQ:T])
                        if k == 0:
                            if part == 0:
                                dve.wait_ge(glu_done, l * 4 + i + 1)
                            ins = dve.tensor_scalar(out, src, w, P(l, "b_dw", i), ALU.mult, ALU.add)
                        else:
                            dve.wait_ge(vch, last[part])
                            ins = dve.scalar_tensor_tensor(out=out, in0=src, scalar=w, in1=out, op0=ALU.mult, op1=ALU.add)
                        if k == CK - 1 and part:
                            ins.then_inc(conv_done, 1)
                        else:
                            last[part] = step(ins)

            def ln(l, w):
                k, n0 = LNT[w], ln_at(l, w)
                src, dst = (cacc, X, acc)[w], (cacc, X, X)[w]
                dve.wait_ge(ln_sum, 3 * l + w + 1)
                for m in range(k):
                    if w == 0:
                        dve.wait_ge(conv_done, l * 4 + m + 1)
                    elif w == 1:
                        dve.wait_ge(*evicted(l, FIRST[U_WO + m]))
                    else:
                        dve.wait_ge(acc_ready, l + 1)
                    dve.scalar_tensor_tensor(out=src[:, m, :], in0=PS[6][:, 0:T], scalar=-1.0 / (128 * k), in1=src[:, m, :],
                                             op0=ALU.mult, op1=ALU.add).then_inc(ln_cent, 1)
                dve.wait_ge(ln_std, 3 * l + w + 1)
                dve.wait_ge(ln_cent, n0 + k)
                link(dve.reciprocal(rstd[:, :], std[:, :]))
                for m in range(k):
                    dve.tensor_tensor(dst[:, m, :], src[:, m, :], rstd[:, :], ALU.mult).then_inc(ln_norm, 1)
                if w == 0:
                    for m in range(k):
                        dve.wait_ge(csig, l * 4 + m + 1)
                        dve.scalar_tensor_tensor(out=cacc[:, m, :], in0=sq[:, m % 2, :], scalar=1.0, in1=cacc[:, m, :],
                                                 op0=ALU.add, op1=ALU.mult).then_inc(csilu, 1)
                    for m in range(k):
                        dve.wait_ge(split_hi, split(l, "c", m))
                        dve.scalar_tensor_tensor(out=Xl[:, m, :], in0=cacc[:, m, :], scalar=0.5,
                                                 in1=Xh[:, m, :].bitcast(f32), op0=ALU.mult, op1=ALU.subtract)\
                            .then_inc(split_lo, 1)
                elif (l, w) != (DEPTH - 1, 2):
                    for m in range(k):
                        dve.wait_ge(split_hi, split(l, "x1" if w == 1 else "x2", m))
                        dve.tensor_tensor(Xl[:, m, :], X[:, m, :], Xh[:, m, :].bitcast(f32), ALU.subtract)\
                            .then_inc(split_lo, 1)

            def delta(l, t, name):
                j, r = number(l, t, name), rows(t)
                b = dbank(j)
                n4 = {"kt": 128, "vt": 128, "p0": 128, "p1": 128, "s0": 128, "s1": 128}.get(name, r)
                b4 = b[:, 0:4 * n4].rearrange("p (h n) -> p h n", h=H)
                p = "s" if t == 2 else "p"
                inc = consumed(j)[0]
                if dict(products(t))[name] == "dve" and not (t == 2 and name[0] == "s"):
                    dve.wait_ge(dmm, j + 1)

                def scal(i):
                    return sc[0:r, i, t, :]

                def lev(s, n="lev"):
                    o = CON[n][0] + 128 * s
                    return over(con[0:r, o:o + r], H)

                if name == "gc":
                    dve.wait_ge(ab_dve, 2 * l + 2)
                    dve.tensor_copy(gb[0:r, :, :], along(scal(0), 128)).then_inc(gb_made, 1)
                    dve.wait_ge(*read(l, t, "gc"))
                    dve.tensor_tensor(scal(7), scal(4), scal(3), ALU.subtract).then_inc(dif_made, 1)
                    link(dve.tensor_tensor(scal(6), scal(1), scal(5), ALU.mult))
                elif name == "R":
                    dve.wait_ge(eg_made, l * 3 + t + 1)
                    link(dve.tensor_tensor(decT[0:r, :, 0:r], b4[0:r], along(scal(3), r), ALU.subtract))
                    dve.tensor_scalar(dec[0:r, :, 0:r], decT[0:r, :, 0:r], 0.0, None, ALU.max).then_inc(inc, 1)
                    dve.tensor_scalar(decT[0:r, :, 0:r], decT[0:r, :, 0:r], 0.0, None, ALU.min).then_inc(arg_made, 1)
                elif name == "kt":
                    dve.wait_ge(kdec_made, l * 3 + t + 1)
                    dve.tensor_tensor(kb[0:r, :, :], b4[0:r], along(scal(6), 128), ALU.mult)
                    dve.tensor_tensor(kd[0:r, :, :], b4[0:r], along(scal(7), 128), ALU.mult).then_inc(inc, 1)
                elif name == "vt":
                    dve.tensor_tensor(vb[0:r, :, :], b4[0:r], along(scal(2), 128), ALU.mult).then_inc(inc, 1)
                elif name == "G":
                    dve.wait_ge(dec_made, l * 3 + t + 1)
                    link(dve.scalar_tensor_tensor(out=dec[0:r, :, 0:r], in0=dec[0:r, :, 0:r], scalar=-1.0,
                                                  in1=over(C("strict_" + p, r), H), op0=ALU.mult, op1=ALU.mult))
                    link(dve.tensor_tensor(dec[0:r, :, 0:r], dec[0:r, :, 0:r], along(scal(1), r), ALU.mult))
                    dve.tensor_tensor(NN[0:r, :, 0:r], b4[0:r], dec[0:r, :, 0:r], ALU.mult).then_inc(inc, 1)
                elif name == "A":
                    link(dve.tensor_tensor(decT[0:r, :, 0:r], decT[0:r, :, 0:r], over(C("cum_" + p, r), H), ALU.mult))
                    dve.tensor_tensor(aT[0:r, :, 0:r], b4[0:r], decT[0:r, :, 0:r], ALU.mult).then_inc(inc, 1)
                    dve.wait_ge(*read(l, t, "G"))
                    link(dve.tensor_tensor(eg[:, :, 0:r], qT[:, :, cols(t)], eg[:, :, 0:r], ALU.mult))
                elif name == "NT":
                    link(dve.tensor_tensor(XX[0:r, :, 0:r], NN[0:r, :, 0:r], lev(0), ALU.mult))
                    link(dve.tensor_tensor(XX[0:r, :, 0:r], XX[0:r, :, 0:r], over(C("ident", r)[:, 0:r], H), ALU.add))
                    dve.wait_ge(*read(l, t, "NT"))
                    link(dve.tensor_tensor(YY[0:r, :, 0:r], NT[0:r, :, 0:r], lev(0, "lev0t"), ALU.mult))
                    dve.tensor_tensor(YY[0:r, :, 0:r], YY[0:r, :, 0:r], over(C("ident", r)[:, 0:r], H), ALU.add)\
                        .then_inc(xy0_made, 1)
                elif name[0] == "t":
                    dve.tensor_tensor(T1[0:r, :, 0:r], b4[0:r], lev(int(name[1])), ALU.mult).then_inc(inc, 1)
                elif name[0] in "xy":
                    m = XX if name[0] == "x" else YY
                    s = int(name[1])
                    if s == 1:
                        dve.wait_ge(xy0_made, l * 3 + t + 1)
                    elif name[0] == "y":
                        dve.wait_ge(*read(l, t, f"y{s - 1}"))
                    dve.tensor_tensor(m[0:r, :, 0:r], m[0:r, :, 0:r], b4[0:r], ALU.add).then_inc(inc, 1)
                elif name in ("p0", "p1"):
                    q = slice(64 * int(name[1]), 64 * int(name[1]) + 64)
                    dve.wait_ge(*read(l, t, "u"))
                    dve.tensor_tensor(vn[q, :, :], uu[q, :, :], b4[q], ALU.subtract).then_inc(inc, 1)
                elif name in ("s0", "s1"):
                    c = int(name[1])
                    for h in range(H):
                        ins = dve.scalar_tensor_tensor(out=S[:, h, :], in0=S[:, h, :], scalar=gs[:, h, c:c + 1],
                                                       in1=b4[:, h, :], op0=ALU.mult, op1=ALU.add)
                    ins.then_inc(inc, 1)
                    dve.wait_ge(*read(l, t, name))
                elif name == "p":
                    dve.wait_ge(*read(l, t, "u"))
                    dve.tensor_tensor(uu[:, :, 0:r], uu[:, :, 0:r], b4, ALU.subtract).then_inc(inc, 1)
                elif name == "v":
                    dve.wait_ge(*read(l, t, "v"))
                elif name[0] == "s":
                    h, half = int(name[1]), int(name[2])
                    q = slice(4 * half, 4 * half + 4)
                    if half == 0:
                        dve.wait_ge(dmm, j)
                        dve.tensor_tensor(vblk[:, :, :], over(vn[0:64, h, :], NSEQ), along(C("ind_s", 64), 128), ALU.mult)\
                            .then_inc(vblk_made, 1)
                        link(dve.tensor_tensor(Ss[:, h, :, :], Ss[:, h, :, :], along(gs[:, h, :], 128), ALU.mult))
                    dve.wait_ge(dmm, j + 1)
                    dve.tensor_tensor(Ss[:, h, q, :], Ss[:, h, q, :], b[:, :].rearrange("p (n d) -> p n d", n=4), ALU.add)\
                        .then_inc(inc, 1)

            def rms(l):
                for h in range(H):
                    dve.wait_ge(rms_root, l * 4 + h + 1)
                    link(dve.reciprocal(rmsr[:, h, :], rmsr[:, h, :]))
                    link(dve.scalar_tensor_tensor(out=oT[:, h, :], in0=oT[:, h, :], scalar=P(l, "dn_g"), in1=rmsr[:, h, :],
                                                  op0=ALU.mult, op1=ALU.mult))
                    dve.scalar_tensor_tensor(out=oT[:, h, :], in0=oT[:, h, :], scalar=0.5, in1=Z[:, h, :],
                                             op0=ALU.mult, op1=ALU.mult).then_inc(o_made, 1)
                for h in range(H):
                    dve.wait_ge(split_hi, split(l, "o", h))
                    dve.tensor_tensor(Xl[:, 4 + h, :], oT[:, h, :], Xh[:, 4 + h, :].bitcast(f32), ALU.subtract)\
                        .then_inc(split_lo, 1)

            def pooled_in(l):
                for m in range(8):
                    dve.wait_ge(*evicted(l, FIRST[U_YP] + m))
                    dve.scalar_tensor_tensor(out=G[:, m, :], in0=G[:, m, :], scalar=1.0, in1=yb[:, m % 2, :],
                                             op0=ALU.add, op1=ALU.mult).then_inc(yp_done, 1)

            def branch(l, u, gate0, last_branch):
                dve.wait_ge(unit_done, l * NU + u + 1)
                for i in range(2):
                    g = FIRST[u] + i
                    m = 2 * (u - (U_YD if last_branch else U_YC)) + i
                    dve.scalar_tensor_tensor(out=tt[:, i, :], in0=G[:, gate0 + m, :], scalar=1.0, in1=gbank(l, g)[:, 0:T],
                                             op0=ALU.add, op1=ALU.mult).then_inc(evict_dve, 1)
                    dve.wait_ge(*evicted(l, g))
                    ins = dve.tensor_tensor(G[:, m, :], G[:, m, :], tt[:, i, :], ALU.add)
                    if last_branch:
                        ins.then_inc(mix_done, 1)
                    else:
                        link(ins)

            def mix(l, m):
                dve.wait_ge(split_hi, split(l, "m", m))
                dve.tensor_tensor(Ml[:, m, :], G[:, m, :], Mh[:, m, :].bitcast(f32), ALU.subtract).then_inc(split_lo, 1)

            def unit(l, u):
                if U_Z <= u < U_G:
                    z_silu(l, u - U_Z)
                elif u == U_YP:
                    pooled_in(l)
                elif U_YC <= u < U_YD:
                    branch(l, u, 8, False)
                elif U_YD <= u < U_WO:
                    branch(l, u, 16, True)
                elif u >= U_WO:
                    m = u - U_WO
                    dve.wait_ge(unit_done, l * NU + u + 1)
                    dve.scalar_tensor_tensor(out=X[:, m, :], in0=X[:, m, :], scalar=2 * ALPHA, in1=gbank(l, FIRST[u])[:, 0:T],
                                             op0=ALU.mult, op1=ALU.add).then_inc(evict_dve, 1)

            def ffn(l):
                lo, hi = e_range(l)

                def rest(e, j):
                    dve.wait_ge(f_hhi, e * FT + (j + 1))
                    dve.tensor_tensor(Hl[:, j, :], hf[:, j % 2, :], Hh[:, j, :].bitcast(f32), ALU.subtract).then_inc(f_hlo, 1)

                dve.wait_ge(acc_init, 1 if l == 0 else 3)
                with dve.Fori(lo, hi) as e:
                    for j in range(FT):
                        dve.wait_ge(f_silu, e * FT + (j + 1))
                        dve.wait_ge(f_done, e * FU + (3 + 2 * j + 2))
                        dve.wait_ge(f_hlo, e * FT + (j + 1))
                        dve.tensor_tensor(hf[:, j % 2, :], sg[:, j % 2, :], PS[(2 * j + 1) % 6][:, 0:T], ALU.mult)\
                            .then_inc(f_uev, 1)
                        if l % 2:
                            dve.wait_ge(f_uev, e * FT + (2 + j + 1))
                            dve.tensor_tensor(hf[:, j % 2, :], hf[:, j % 2, :],
                                              gbc[:, bass.ds(e - lo, 1), :].rearrange("p e t -> p (e t)"), ALU.mult)\
                                .then_inc(f_h, 1)
                        if j:
                            rest(e, j - 1)
                    rest(e, FT - 1)
                    for m in range(8):
                        dve.wait_ge(f_done, e * FU + (3 + 2 * FT + m + 1))
                        dve.wait_ge(f_dev, e * 8 + (m + 1))
                        dve.tensor_tensor(acc[:, m, :], acc[:, m, :], PS[(2 * FT + m) % 6][:, 0:T], ALU.add).then_inc(f_dev, 1)
                dve.wait_ge(f_dev, 8 + 8 * hi)

            def router(l):
                lg, mx, ex, cnt, den = rk[:, 0], rk[:, 1, :, 0:1], rk[:, 2], rk[:, 3], rk[:, 4, :, 0:1]
                link(dve.memset(rk[:, :, :, :], 0.0))
                dve.wait_ge(rt_done, 1)
                for t in range(3):
                    ins = dve.tensor_tensor(lg[0:rows(t), t, :], PS[7][0:rows(t), 8 * t:8 * t + 8], brt[0:rows(t), :], ALU.add)
                link(ins)
                for t in range(3):
                    le = along(lg[:, t, :], NE)
                    lj = over(lg[:, t, :], NE)
                    dve.tensor_tensor(rc[:, 0, t], lj, le, ALU.is_gt)
                    link(dve.tensor_tensor(rc[:, 1, t], lj, le, ALU.is_equal))
                    link(dve.tensor_tensor(rc[:, 1, t], rc[:, 1, t],
                                           C("before").rearrange("p (e j) -> p e j", e=NE), ALU.mult))
                    link(dve.tensor_tensor(rc[:, 0, t], rc[:, 0, t], rc[:, 1, t], ALU.add))
                    link(dve.tensor_reduce(cnt[:, t, :], rc[:, 0, t], AX.X, ALU.add))
                dve.tensor_scalar(cnt, cnt, 1.5, None, ALU.is_lt).then_inc(gx_made, 1)
                link(dve.tensor_reduce(mx, lg, AX.X, ALU.max))
                dve.tensor_tensor(ex, lg, mx.broadcast_to([128, 3, NE]), ALU.subtract).then_inc(rt_top, 1)
                dve.wait_ge(rt_exp, 1)
                dve.wait_ge(gx_made, 1)
                link(dve.tensor_tensor(ex, ex, cnt, ALU.mult))
                link(dve.tensor_reduce(den, ex, AX.X, ALU.add))
                link(dve.reciprocal(den, den))
                link(dve.tensor_tensor(gate[:, :, 0:NE], ex, den.broadcast_to([128, 3, NE]), ALU.mult))

            def gates_everywhere():
                for t in range(3):
                    if t:
                        dve.wait_ge(gb_done, 2 * t)
                    dve.tensor_copy(gexp[:, :, :], along(gate[:, t, 0:NE], 128)).then_inc(gx_made, 1)

            def experts():
                for q in range(1, 12, 2):
                    t, half = q // 4, q // 2 % 2
                    dve.wait_ge(xt_mm, q + 1)
                    dve.tensor_copy(xtl[0:rows(t), t, 512 * half:512 * half + 512], PS[q % 6][0:rows(t), :])\
                        .then_inc(xt_dve, 1)
                dve.wait_ge(pos_done, 1)
                dve.memset(gate[:, :, NE:], 0.0)
                link(dve.memset(posm[:, :, :], -1.0))
                for t in range(3):
                    r = rows(t)
                    link(dve.tensor_tensor(posm[0:r, t, 0:NE], PS[7][0:r, 8 * t:8 * t + 8], rk[0:r, 3, t, :], ALU.mult))
                    link(dve.tensor_scalar(posm[0:r, t, 0:NE], posm[0:r, t, 0:NE], 1.0, None, ALU.subtract))
                link(dve.tensor_reduce(rk[:, 1, 0, 0:1], PS[7][:, 32:40], AX.X, ALU.max))
                dve.tensor_scalar(flag[:, :], rk[:, 1, 0, 0:1], CAP + 0.5, None, ALU.is_gt).then_inc(flag_made, 1)

                def places(e, seen):
                    for t in range(3):
                        dve.tensor_scalar(Pm[:, t, :], C("slot"), seen(posm, t), None, ALU.is_equal)
                    dve.tensor_copy(gcol[:, :], seen(gate, None)).then_inc(m_p, 1)

                def column(e):
                    def seen(a, t):
                        ap = a[:, :, bass.ds(e, 1)] if t is None else a[:, t, bass.ds(e, 1)]
                        return ap.rearrange("p t e -> p (t e)") if t is None else ap
                    return seen

                def mlo(e, i):
                    if i in MPOOL:
                        return
                    w = mwidth(i)
                    dve.wait_ge(m_hi, e * MN + (i + 1))
                    dve.tensor_tensor(ml[:, i % MS, 0:w], mraw[:, i % MRAW, 0:w],
                                      mh[:, i % MS, 0:w].bitcast(f32), ALU.subtract).then_inc(m_lod, 1)

                def gathered(e, n):
                    dve.wait_ge(m_g, e * 4 + (n + 1))
                    dst = (xeh if n == 1 else xel)[:, 4:8, :]
                    dve.tensor_copy(dst, PS[(7, 6, 0, 1)[n]][:, :].rearrange("p (k n) -> p k n", k=4)).then_inc(m_xev, 1)

                def y_full(e):
                    dve.wait_ge(m_done, e * MN + MN)
                    dve.wait_ge(m_ylo, e + 1)
                    for c in range(2):
                        ins = dve.tensor_scalar(yf[:, 512 * c:512 * c + 512], PS[6 + c][:, :], gslot[:, 0:1], None, ALU.mult)
                    ins.then_inc(m_yf, 1)

                def y_rest(e):
                    dve.wait_ge(m_yhi, e + 1)
                    dve.wait_ge(m_yf, e + 1)
                    dve.tensor_tensor(yl[:, :], yf[:, :], yh[:, :].bitcast(f32), ALU.subtract).then_inc(m_ylo, 1)

                def add(e, m):
                    dve.wait_ge(m_sc, e * 8 + (m + 1))
                    dve.wait_ge(m_acc, e * 8 + (m + 1))
                    dve.tensor_tensor(acc[:, m, :], acc[:, m, :], PS[6 + m % 2][:, 0:T], ALU.add).then_inc(m_acc, 1)

                link(dve.memset(gslot[:, :], 0.0))
                link(dve.memset(PT[:, :].bitcast(f32), 0.0))
                for t in range(3):
                    dve.tensor_scalar(Pm[:, t, :], C("slot"), posm[:, t, 0:1], None, ALU.is_equal)
                dve.tensor_copy(gcol[:, :], gate[:, :, 0]).then_inc(m_p, 1)
                gathered(0, 1)
                gathered(0, 3)
                dve.wait_ge(m_xea, 2)
                dve.wait_ge(m_xev, 2)
                dve.wait_ge(acc_init, 2)
                with dve.Fori(0, NE) as e:
                    mlo(e, 0)
                    mlo(e, 1)
                    y_full(e)
                    mlo(e, 2)
                    for i in range(MN):
                        if i + 3 < MN:
                            mlo(e, i + 3)
                        if i == 0:
                            y_rest(e)
                        if SCAT <= i < SCAT + 8:
                            add(e, i - SCAT)
                        if i == 7 + SCAT:
                            dve.wait_ge(m_pt, e + 1)
                            places(e, column(e + 1))
                        if i == MG + MU - 1:
                            dve.wait_ge(m_silu, e * 3 + 3)
                            dve.wait_ge(m_done, e * MN + (MN + MG + MU))
                            for c in range(3):
                                n = min(512, FUNIT - 512 * c)
                                s = slice(512 * c, 512 * c + n)
                                dve.tensor_tensor(sg1[:, s], sg1[:, s], PS[3 + c][:, 0:n], ALU.mult).then_inc(m_h, 1)
                            gathered(e + 1, 1)
                            gathered(e + 1, 3)
                            for c in range(3):
                                k = min(4, FT - 4 * c)
                                dve.wait_ge(m_thi, e * 3 + (c + 1))
                                dve.tensor_tensor(hTl[:, 4 * c:4 * c + k, :],
                                                  PS[3 + c][:, 0:128 * k].rearrange("p (k n) -> p k n", k=k),
                                                  hTh[:, 4 * c:4 * c + k, :].bitcast(f32), ALU.subtract).then_inc(m_tlo, 1)
                y_full(NE)
                y_rest(NE)
                for m in range(8):
                    add(NE, m)
                dve.wait_ge(m_acc, 2 + 8 * (NE + 1))

            dve.wait_ge(in_ready, 80)
            for m in range(KT):
                dve.wait_ge(split_hi, m + 1)
                dve.tensor_tensor(Xl[:, m, :], X[:, m, :], Xh[:, m, :].bitcast(f32), ALU.subtract).then_inc(split_lo, 1)
            for l in range(DEPTH):
                for kind, x in STEPS:
                    if kind == "unit":
                        unit(l, x)
                    elif kind == "qconv":
                        qconv(l, x)
                    elif kind == "qact":
                        qact(l, x)
                    elif kind == "glu":
                        glu(l, x)
                    elif kind == "ab":
                        ab_part(l)
                    elif kind == "norms":
                        norms(l)
                    elif kind == "pool":
                        pool(l, x)
                    elif kind == "conv":
                        conv(l, x)
                    elif kind == "ln":
                        ln(l, x)
                    elif kind == "delta":
                        if x == (0, "gc"):
                            if l:
                                dve.wait_ge(out_done, l * 8 * 16)
                            dve.memset(S[:, :, :], 0.0).then_inc(s_zero, 1)
                        delta(l, *x)
                    elif kind == "rms":
                        rms(l)
                    elif kind == "mix":
                        mix(l, x)
                if l == 0:
                    ffn(l)
                else:
                    router(l)
                    experts()
                    with dve.If(overflow(dve)):
                        gates_everywhere()
                        ffn(l)
                dve.sem_inc(acc_ready, 1)
                ln(l, 2)


def _constants():
    i, j = np.arange(128)[:, None], np.arange(128)[None, :]
    out = np.zeros((128, NCON), np.float32)

    def put(name, a):
        o, w = CON[name]
        out[:a.shape[0], o:o + w] = a.reshape(a.shape[0], w)

    put("ident", (i == j).astype(np.float32))
    put("ones", np.ones((128, 128), np.float32))
    for p, n, c in (("p", 128, CHUNK), ("s", 64, TS)):
        a, b = i[:n], j[:, :n]
        same = a // c == b // c
        put("cum_" + p, (same & (a <= b)).astype(np.float32))
        put("blk_" + p, same.astype(np.float32))
        put("strict_" + p, (same & (a > b)).astype(np.float32))
        put("ind_" + p, (a // c == np.arange(8)[None]).astype(np.float32))
    lev = [((i >> (s + 1)) == (j >> (s + 1))) & ((i >> s) & 1 == 1) & ((j >> s) & 1 == 0) for s in range(6)]
    put("lev", np.stack(lev, 1).astype(np.float32))
    put("lev0t", lev[0].T.astype(np.float32))
    put("invcnt", np.tile(np.concatenate([1.0 / np.minimum(np.arange(16) + 1, w) for w in WINDOWS]).astype(np.float32), (128, 1)))
    put("upto", (i <= j).astype(np.float32))
    put("slot", np.tile(np.arange(128, dtype=np.float32), (128, 1)))
    put("before", np.tile((np.arange(NE)[None, :] < np.arange(NE)[:, None]).astype(np.float32).ravel(), (128, 1)))
    return out


def _tiles(a):
    return np.moveaxis(a.reshape(a.shape[:-1] + (-1, 128)), -1, 0)


def kernel(**inputs):
    import concourse.bacc as bacc
    from concourse import mybir
    from concourse.bass_utils import run_bass_kernel_spmd

    a = {k: np.asarray(v) for k, v in inputs.items()}
    L = range(DEPTH)

    def units(w):
        k, n = w.shape[0] // 128, w.shape[1] // 128
        return w.reshape(k, 128, n, 128).transpose(1, 2, 0, 3).reshape(128, n, k * 128)

    x = np.concatenate([a["x_prompt"][0], a["x_sample"].reshape(-1, D)], 0)
    mix, wab = [], []
    for l in L:
        w = a["w_in"][l]
        pool, ca, cb, qkv, z = w[:, 0:512], w[:, 512:1024], w[:, 1024:1536], w[:, 1536:3072], w[:, 3072:3584]
        ab = np.stack([units(ca), units(cb)], 2).reshape(128, 8, UNIT)
        mix.append(np.concatenate([
            units(qkv), ab, units(pool), units(z), units(w[:, GATE_OFF:]),
            a["w_pool"][l].transpose(1, 0, 2).reshape(128, 1, UNIT),
            units(a["w_conv_out"][l]).reshape(128, 4, UNIT), units(a["w_dn_out"][l]).reshape(128, 4, UNIT),
            units(a["w_out"][l])], 1))
        wab.append(w[:, 3584:3592].reshape(KT, 128, 8).transpose(1, 0, 2))

    def expert(wg, wu, wd):
        gu = np.stack([units(wg), units(wu)], 2).reshape(128, 2 * FT * UNIT)
        return np.concatenate([gu, units(wd).reshape(128, 8 * FUNIT)], 1)

    hf = FT * 128
    g, u, d = a["ffn_wg"][0], a["ffn_wu"][0], a["ffn_wd"][0]
    ffn = [expert(g[:, i * hf:(i + 1) * hf], u[:, i * hf:(i + 1) * hf], d[i * hf:(i + 1) * hf]) for i in range(2)]


    def matrix(w):
        e, k, n = w.shape
        return w.reshape(e, k // 128, 128, n).transpose(0, 2, 1, 3).reshape(e, 128, -1)

    moe = np.concatenate([matrix(a[k][0]) for k in ("moe_wg", "moe_wu", "moe_wd")], 2)

    par = np.zeros((128, DEPTH, NPAR), np.float32)
    for l in L:
        for name, v in (("w_dw", _tiles(a["w_dw"][l]).transpose(0, 2, 1)), ("b_dw", _tiles(a["b_dw"][l])),
                        ("cg", _tiles(a["conv_ln_g"][l])), ("cb", _tiles(a["conv_ln_b"][l])),
                        ("w_short", _tiles(a["w_short"][l]).transpose(0, 2, 1)), ("pscale", _tiles(a["pool_scale"][l])),
                        ("dn_g", _tiles(a["dn_norm_g"][l])), ("ln1_g", _tiles(a["ln1_g"][l])), ("ln1_b", _tiles(a["ln1_b"][l])),
                        ("ln2_g", _tiles(a["ln2_g"][l])), ("ln2_b", _tiles(a["ln2_b"][l])),
                        ("a_log", np.tile(a["a_log"][l], (128, 1))), ("dt", np.tile(a["dt_bias"][l], (128, 1)))):
            o, w = PAR[name]
            par[:, l, o:o + w] = v.reshape(128, w)

    def history(s, room):
        n, b, r, c = s.shape
        s = s.reshape(n, b, r, c // 128, 128).transpose(0, 4, 3, 1, 2)
        return np.pad(s, [(0, 0)] * 4 + [(0, room)])

    arrays = {
        "x": x.reshape(T, KT, 128).transpose(2, 1, 0), "con": _constants(), "par": par,
        "w_router": a["w_router"][0].reshape(KT, 128, NE).transpose(1, 0, 2), "b_router": np.tile(a["b_router"][0], (128, 1)),
        "w_mix": np.stack(mix), "w_ab": np.stack(wab), "w_ffn": np.stack(ffn), "w_moe": moe,
        "st_qkv": history(a["state_qkv_conv"], 0), "st_conv": history(a["state_conv"], TS),
        "st_pool": history(a["state_pool"], TS), "st_delta": a["state_delta"].transpose(0, 3, 2, 1, 4),
    }
    arrays = {k: np.ascontiguousarray(v) for k, v in arrays.items()}
    outs = {
        "y": (128, KT, T), "o_conv_p": (DEPTH, 128, H, CB), "o_conv_s": (DEPTH, 128, H, NSEQ, CB + TS),
        "o_pool_p": (DEPTH, 128, H, PB), "o_pool_s": (DEPTH, 128, H, NSEQ, PB + TS),
        "o_qkv_p": (DEPTH, 128, 12, SB), "o_qkv_s": (DEPTH, 128, 12, NSEQ, SB),
        "o_delta_p": (DEPTH, 128, H, 128), "o_delta_s": (DEPTH, 128, H, NSEQ, 128),
    }
    nc = bacc.Bacc("TRN2", target_bir_lowering=False, num_devices=1)
    io = {k: nc.dram_tensor(k, v.shape, mybir.dt.from_np(v.dtype), kind="ExternalInput").ap() for k, v in arrays.items()}
    io |= {k: nc.dram_tensor(k, s, mybir.dt.float32, kind="ExternalOutput").ap() for k, s in outs.items()}
    build(nc, io)
    r = run_bass_kernel_spmd(nc, [arrays], core_ids=[0]).results[0]

    y = r["y"].transpose(2, 1, 0).reshape(T, D)

    def rows_p(s):
        return s.transpose(0, 3, 2, 1).reshape(DEPTH, 1, s.shape[3], -1)

    def rows_s(s, keep):
        return s[..., -keep:].transpose(0, 3, 4, 2, 1).reshape(DEPTH, NSEQ, keep, -1)

    return (y[:SEQ].reshape(1, SEQ, D), y[SEQ:].reshape(NSEQ, TS, D),
            rows_p(r["o_pool_p"]), rows_p(r["o_conv_p"]), rows_p(r["o_qkv_p"]),
            r["o_delta_p"].transpose(0, 2, 1, 3)[:, None],
            rows_s(r["o_pool_s"], PB), rows_s(r["o_conv_s"], CB), rows_s(r["o_qkv_s"], SB),
            r["o_delta_s"].transpose(0, 3, 2, 1, 4))
```

```python
import numpy as np

DEPTH, D, SEQ, NSEQ, TS = 2, 1024, 256, 8, 8
T = SEQ + NSEQ * TS
KT = D // 128
H = 4
CK, SK_, PB = 31, 4, 15
CB, SB = CK - 1, SK_ - 1
FT = 11
NE = 8
CAP = 128
ALPHA = (2 * DEPTH) ** 0.25
CHUNK = 64
WINDOWS = (2, 4, 8, 16)
GATE_OFF = 3592
PTAP = 2
UNIT = 1024
FUNIT = FT * 128
N_QKV, N_AB, N_POOL, N_Z, N_G, N_YP, N_YC, N_YD, N_WO = 12, 8, 4, 4, 24, 1, 4, 4, 8
U_AB = N_QKV
U_POOL = U_AB + N_AB
U_Z = U_POOL + N_POOL
U_G = U_Z + N_Z
U_YP = U_G + N_G
U_YC = U_YP + N_YP
U_YD = U_YC + N_YC
U_WO = U_YD + N_YD
NU = U_WO + N_WO
NB = (NU + 1) // 2
NOUT = 6 + 1 + H
FU = 2 * FT + 8
MG, MU, MD = 8, 8, FT
MN = MG + MU + MD
MW = (MG + MU) * FUNIT + MD * D
MP = MN + 1
MRAW, MS = 7, 4
SCAT = 2
MPOOL = [i for i in range(MN) if i % 4 == 3]

PAR = {}
_at = 0
for _n, _w in (("w_dw", 4 * CK), ("b_dw", 4), ("cg", 4), ("cb", 4), ("w_short", 12 * SK_), ("pscale", 8),
               ("dn_g", 1), ("ln1_g", 8), ("ln1_b", 8), ("ln2_g", 8), ("ln2_b", 8), ("a_log", 4), ("dt", 4)):
    PAR[_n] = (_at, _w)
    _at += _w
NPAR = _at

CON = {}
_at = 0
for _n, _w in (("ident", 128), ("ones", 1), ("pick", 15), ("cum_p", 128), ("blk_p", 128), ("strict_p", 128), ("cum_s", 64),
               ("blk_s", 64), ("strict_s", 64), ("ind_p", 8), ("ind_s", 8), ("lev", 6 * 128), ("lev0t", 128),
               ("invcnt", 64), ("before", 64),
               ("upto", 128), ("slot", 128)):
    CON[_n] = (_at, _w)
    _at += _w
NCON = _at


def build(nc, io):
    import concourse.bass as bass
    from concourse import mybir
    from contextlib import ExitStack

    f32, f32r = mybir.dt.float32, mybir.dt.float32r
    ALU, ACT, AX = mybir.AluOpType, mybir.ActivationFunctionType, mybir.AxisListType

    ctx = ExitStack()
    with ctx:
        base = (nc.sbuf_base + 31) // 32 * 32

        def size(shape):
            return (int(np.prod(shape[1:])) * 4 + 31) // 32 * 32

        def lay(at, *plan):
            out = []
            for name, shape, dt in plan:
                assert base + at + size(shape) <= nc.sbuf_usable_end, (name, base + at + size(shape))
                out.append(nc.alloc_sbuf_tensor_at(name, shape, dt, offset=base + at))
                at += size(shape)
            return out + [at]

        (con, par, X, Xh, Xl, raw, Wh, Wl, wab, wrt, brt, sq, std, rstd, ab, sc, gs, tmp3, gate, posm,
         gcol, gslot, flag, TOP) = lay(
            0, ("con", [128, NCON], f32), ("par", [128, DEPTH, NPAR], f32),
            ("X", [128, KT, T], f32),
            ("Xh", [128, KT, T], f32r), ("Xl", [128, KT, T], f32r),
            ("raw", [128, 3, 2, UNIT], f32),
            ("Wh", [128, 3, UNIT], f32r), ("Wl", [128, 3, UNIT], f32r),
            ("wab", [128, KT, 8], f32), ("wrt", [128, KT, NE], f32), ("brt", [128, NE], f32),
            ("sq", [128, 2, T], f32), ("std", [128, T], f32), ("rstd", [128, T], f32),
            ("ab", [128, 3, 8], f32),
            ("sc", [128, 9, 3, 4], f32),
            ("gs", [128, 4, 8], f32),
            ("tmp3", [128, 3, 3, 4], f32),
            ("gate", [128, 3, NE + 1], f32), ("posm", [128, 3, NE + 1], f32),
            ("gcol", [128, 3], f32), ("gslot", [128, 1], f32), ("flag", [128, 1], mybir.dt.int32))
        (G, EXT) = lay(TOP, ("G", [128, 24, T], f32))
        (cxp, cxs, pxp, pxs, E1) = lay(EXT, ("cxp", [128, H, CB + SEQ], f32), ("cxs", [128, H, NSEQ, CB + TS], f32),
                                       ("pxp", [128, H, PB + SEQ], f32), ("pxs", [128, H, NSEQ, PB + TS], f32))
        (Ss, E2) = lay(EXT, ("Ss", [128, H, NSEQ, 128], f32))
        (qxp, qxs, qh, qT, kT, vT, Z, S, oT, tp, ts, TEMP) = lay(
            max(E1, E2), ("qxp", [128, 2, SB + SEQ], f32), ("qxs", [128, 2, NSEQ, SB + TS], f32),
            ("qh", [128, 12, NSEQ, SB], f32),
            ("qT", [128, H, T], f32), ("kT", [128, H, T], f32), ("vT", [128, H, T], f32), ("Z", [128, H, T], f32),
            ("S", [128, H, 128], f32), ("oT", [128, H, T], f32),
            ("tp", [128, 12, SB], f32), ("ts", [128, 12, NSEQ, SB], f32))
        (NT, YY, vb, kb, eg, aT, decT, dif, cacc, XX, T1, NN, kd, yb, E3) = lay(
            TEMP, *[(n, [128, H, 128], f32) for n in ("NT", "YY", "vb", "kb", "eg", "aT", "decT")],
            ("dif", [128, H, T], f32),
            ("cacc", [128, H, T], f32), *[(n, [128, H, 128], f32) for n in ("XX", "T1", "NN", "kd")],
            ("yb", [128, 2, T], f32))
        gb, dec, uu, wT, vn, tt = XX, YY, XX, T1, NN, yb
        (vblk, _) = lay(E3 - size([1, 2, T]) - 4 * size([1, H, 128]), ("vblk", [64, NSEQ, 128], f32))
        (pw, _) = lay(max(E1, E2), ("pw", [128, 2, PB + SEQ], f32))
        (Mh, Ml, E5) = lay(TEMP, ("Mh", [128, KT, T], f32r), ("Ml", [128, KT, T], f32r))
        (fh, fl, fraw, HT) = lay(TOP, ("fh", [128, 3, FUNIT], f32r), ("fl", [128, 3, FUNIT], f32r),
                                 ("fraw", [128, 5, FUNIT], f32))
        (Hh, Hl, acc, gbc, sg, hf, E6) = lay(HT, ("Hh", [128, FT, T], f32r), ("Hl", [128, FT, T], f32r),
                                             ("acc", [128, KT, T], f32), ("gbc", [128, NE, T], f32),
                                             ("sg", [128, 2, T], f32), ("hf", [128, 2, T], f32))
        (gexp, _) = lay(HT, ("gexp", [128, NE, 128], f32))
        (mraw, mh, ml, sg1, ACC) = lay(TOP, ("mraw", [128, MRAW, FUNIT], f32), ("mh", [128, MS, FUNIT], f32r),
                                       ("ml", [128, MS, FUNIT], f32r), ("sg1", [128, FUNIT], f32))
        assert ACC == HT + 2 * size([128, FT, T])
        (yf, yh, yl, rk, rc, _) = lay(ACC + size([128, KT, T]), ("yf", [128, D], f32), ("yh", [128, D], f32r),
                                      ("yl", [128, D], f32r), ("rk", [128, 5, 3, NE], f32), ("rc", [128, 2, 3, NE, NE], f32))
        RING = sum(size(s) for s in ([1, NCON], [1, DEPTH, NPAR])) + 3 * size([1, KT, T])
        (xth, xtl, hTh, hTl, xeh, xel, PT, Pm, E7) = lay(
            RING, ("xth", [128, 3, D], f32r), ("xtl", [128, 3, D], f32r), ("hTh", [128, FT, CAP], f32r),
            ("hTl", [128, FT, CAP], f32r), ("xeh", [128, KT, CAP], f32r), ("xel", [128, KT, CAP], f32r),
            ("PT", [CAP, T], f32r), ("Pm", [128, 3, CAP], f32r))
        assert E7 <= RING + 12 * UNIT * 4

        PS = [ctx.enter_context(nc.psum_tensor(f"ps{i}", [128, 512], f32)) for i in range(8)]

        def sem(name):
            return ctx.enter_context(nc.semaphore(name))

        def C(name, rows=128):
            o, w = CON[name]
            return con[0:rows, o:o + w]

        def ones(rows=128, n=128):
            return C("ones", rows).broadcast_to([rows, n])

        def picked(i):
            o, _ = CON["pick"]
            return con[:, o + 7 - i:o + 15 - i]

        def spread(i):
            return C("ident", 8)[:, i:i + 1].broadcast_to([8, 128])

        def P(l, name, i=0):
            o, _ = PAR[name]
            return par[:, l, o + i:o + i + 1]

        def over(ap, n):
            return ap.unsqueeze(1).broadcast_to([ap.shape[0], n, ap.shape[1]])

        def along(ap, n):
            return ap.unsqueeze(2).broadcast_to([ap.shape[0], ap.shape[1], n])

        xa_in, xb_in, par_in, con_in, qh_in = sem("xa_in"), sem("xb_in"), sem("par_in"), sem("con_in"), sem("qh_in")
        state_in, ss_in, out_done = sem("state_in"), sem("ss_in"), sem("out_done")
        raw_in = [sem(f"raw_in{i}") for i in range(3)]
        w_hi, w_lo, unit_done = sem("w_hi"), sem("w_lo"), sem("unit_done")
        evict_act, evict_dve = sem("evict_act"), sem("evict_dve")
        hist_zero, vch, ach = sem("hist_zero"), sem("vch"), sem("ach")
        qc_done, qt_done, qs_done, sqr_done = sem("qc_done"), sem("qt_done"), sem("qs_done"), sem("sqr_done")
        ssq_done, nrm_root, nrm_inv = sem("ssq_done"), sem("nrm_root"), sem("nrm_inv")
        tails_done = sem("tails_done")
        ab_done, ab_copied, ab_act, ab_dve = sem("ab_done"), sem("ab_copied"), sem("ab_act"), sem("ab_dve")
        glu_done, conv_dve, tap_made, tap_added, z_done, d_made = sem("glu_done"), sem("conv_dve"), sem("tap_made"), sem("tap_added"), sem("z_done"), sem("d_made")
        ln_sum, ln_cent, ln_sq, ln_sqs = sem("ln_sum"), sem("ln_cent"), sem("ln_sq"), sem("ln_sqs")
        ln_std, ln_norm, aff_done, caff_done = sem("ln_std"), sem("ln_norm"), sem("aff_done"), sem("caff_done")
        yp_seen = sem("yp_seen")
        csig, csilu = sem("csig"), sem("csilu")
        split_hi, split_lo = sem("split_hi"), sem("split_lo")
        yp_done, mix_done = sem("yp_done"), sem("mix_done")
        dmm, d_act, d_dve = sem("dmm"), sem("d_act"), sem("d_dve")
        gb_made, dif_made, kdec_made, eg_made = sem("gb_made"), sem("dif_made"), sem("kdec_made"), sem("eg_made")
        arg_made, dec_made, xy0_made = sem("arg_made"), sem("dec_made"), sem("xy0_made")
        s_zero, rms_sq, rms_sum, rms_inv, o_made = sem("s_zero"), sem("rms_sq"), sem("rms_sum"), sem("rms_inv"), sem("o_made")
        vblk_made = sem("vblk_made")
        fraw_in = [sem(f"fraw_in{i}") for i in range(5)]
        f_hi, f_lo, f_done = sem("f_hi"), sem("f_lo"), sem("f_done")
        f_silu, f_uev, f_dev, f_h = sem("f_silu"), sem("f_uev"), sem("f_dev"), sem("f_h")
        f_hhi, f_hlo, acc_init = sem("f_hhi"), sem("f_hlo"), sem("acc_init")
        rt_done, rt_top, rt_exp, gx_made, gb_done, gb_copied = (
            sem("rt_done"), sem("rt_top"), sem("rt_exp"), sem("gx_made"), sem("gb_done"), sem("gb_copied"))
        pos_done, pos_made, flag_made = sem("pos_done"), sem("pos_made"), sem("flag_made")
        xt_mm, xt_act, xt_dve = sem("xt_mm"), sem("xt_act"), sem("xt_dve")
        m_raw = [sem(f"m_raw{i}") for i in range(MRAW)]
        m_hi, m_lop, m_lod, m_done = sem("m_hi"), sem("m_lop"), sem("m_lod"), sem("m_done")
        m_p, m_pt, m_ptc = sem("m_p"), sem("m_pt"), sem("m_ptc")
        m_g, m_xea, m_xev = sem("m_g"), sem("m_xea"), sem("m_xev")
        m_silu, m_h, m_t, m_thi, m_tlo = sem("m_silu"), sem("m_h"), sem("m_t"), sem("m_thi"), sem("m_tlo")
        m_yf, m_yhi, m_ylo, m_sc, m_acc = sem("m_yf"), sem("m_yhi"), sem("m_ylo"), sem("m_sc"), sem("m_acc")
        acc_ready = sem("acc_ready")
        block = ctx.enter_context(nc.Block())

        def rows(t):
            return 128 if t < 2 else 64

        def cols(t):
            return slice(128 * t, 128 * t + rows(t))

        def groups_of(u):
            return ["act"] if u < U_YP else ["act"] * 8 if u < U_YC else ["dve"] * 2 if u < U_WO else ["dve"]

        GROUPS = [k for u in range(NU) for k in groups_of(u)]
        FIRST = [sum(len(groups_of(v)) for v in range(u)) for u in range(NU)]

        def evicted(l, g):
            k = GROUPS[g]
            return (evict_act if k == "act" else evict_dve), l * GROUPS.count(k) + GROUPS[:g + 1].count(k)

        def bank_free(eng, l, g):
            n = l * len(GROUPS) + g - 4
            if n >= 0:
                eng.wait_ge(*evicted(*divmod(n, len(GROUPS))))

        def gbank(l, g):
            return PS[(l * len(GROUPS) + g) % 4]

        def products(t):
            n = [[(f"n{i}", "dve")] if t == 0 else [] for i in range(8)]
            out = n[4] + n[5] + [("gc", "act"), ("R", "dve")] + n[6] + n[7] + [("kt", "dve"), ("vt", "dve"), ("G", "dve"), ("NT", "act")]
            if t == 2:
                out = out[:4] + [("cm", "dve")] + out[4:] + [("cv", "act")]
            top = 5 if t < 2 else 2
            for s in range(1, top + 1):
                out += [(f"t{s}", "dve")] + (n[0] if s == 1 else n[3] if s == 2 else [])
                out += ([(f"x{s}", "dve")] if s < top else []) + (n[1] if s == 1 else [])
                out += [(f"y{s}", "dve")] + (n[2] if s == 1 else [])
                out += [("A", "dve")] if s == 2 else []
            if t < 2:
                out += [("u", "act"), ("w", "act")]
                for c in range(2):
                    out += [(f"p{c}", "dve"), (f"o{c}", "act"), (f"s{c}", "dve")]
            else:
                out += [("u", "act"), ("w", "act"), ("p", "dve"), ("v", "act"), ("o", "dve")]
                out += [("rs", "act")] + [(f"b{h}", "dve") for h in range(H)]
                out += [(f"s{h}{b}", "dve") for h in range(H) for b in range(2)]
            return out

        PROD = [(t, n, e) for t in range(3) for n, e in products(t)]
        KINDS = [e for _, _, e in PROD]

        def number(l, t, name):
            return l * len(PROD) + [(a, b) for a, b, _ in PROD].index((t, name))

        def consumed(j):
            l, i = divmod(j, len(PROD))
            return (d_act if KINDS[i] == "act" else d_dve), l * KINDS.count(KINDS[i]) + KINDS[:i + 1].count(KINDS[i])

        def read(l, t, name):
            return consumed(number(l, t, name))

        def dbank(j):
            return PS[4 + j % 4]

        SPL, NSPL = {"d": 0, "c": 4, "o": 8, "m": 12, "x1": 20, "x2": 28}, 36

        def split(l, name, i):
            return 8 + l * NSPL + SPL[name] + i + 1

        def x_split(l):
            return 8 if l == 0 else split(l - 1, "x2", 7)

        LNT = [4, 8, 8]

        def ln_at(l, w):
            return l * sum(LNT) + sum(LNT[:w])

        def shifts(l, w):
            return 16 * l + 8 * (w - 1)

        def router_next(l, w):
            return (l, w) == (DEPTH - 1, 1)

        def sqs_at(l, w):
            return ln_at(l, w) - l - (w > 0)

        def conved(l, i):
            return (conv_dve, l * PTAP + i + 1) if i < PTAP else (tap_added, tap_at(l, i, CK - 1))

        def tap_at(l, i, k):
            return (l * (4 - PTAP) + i - PTAP) * CK + k + 1

        def e_range(l):
            return (0, 2) if l == 0 else (2, 2 + NE)

        def mwidth(i):
            return FUNIT if i < MG + MU else D

        def m_rest(e, i):
            mine = i in MPOOL
            k = sum((v in MPOOL) == mine for v in range(i + 1))
            n = len(MPOOL) if mine else MN - len(MPOOL)
            return (m_lop if mine else m_lod), e * n + (n + k)

        def m_rest_before(e, i):
            i -= MRAW
            if i >= 0:
                return m_rest(e, i)
            i += MP
            if i == MN:
                i -= MRAW
            mine = i in MPOOL
            return (m_lop if mine else m_lod), e * (len(MPOOL) if mine else MN - len(MPOOL)) + sum(
                (v in MPOOL) == mine for v in range(i + 1))

        def m_before(e, i):
            i -= MS
            if i >= 0:
                return m_done, e * MN + (MN + i + 1)
            i += MP
            if i == MN:
                i -= MS
            return m_done, e * MN + (i + 1)

        def m_loaded(e, i):
            n = len(range(i % MRAW, MN, MRAW))
            return m_raw[i % MRAW], e * (n * 16) + (i // MRAW + 1) * 16

        def overflow(eng):
            eng.wait_ge(flag_made, 1)
            return eng.value_load(flag[0:1, 0:1], min_val=0, max_val=1) > 0

        STEPS = []

        def whole(u):
            return [("part", (u, p)) for p in range(4)] + [("unit", u)]

        for u in range(N_QKV):
            STEPS += whole(u) + [("qconv", u)]
            STEPS += [("qact", u - 1)] if u else []
            STEPS += [("ssq", u - 2)] if 2 <= u < 10 else []
            STEPS += [("ab", 0)] if u == 3 else []
            STEPS += [("root", 0)] if u == 10 else []
        fill = []
        for u in range(U_AB, U_YD - 2):
            if u == U_YP:
                fill += [("dsplit", 0), ("gap", 0), ("gap", 0)]
            if u == U_YC:
                fill += [("csplit", 0), ("gap", 0)]
            fill += whole(u)
            if U_AB <= u < U_POOL and (u - U_AB) % 2:
                fill += [("glu", (u - U_AB) // 2)]
        STEPS += [("qact", 11)] + fill[:8]
        fill = fill[8:]
        taps = [("tap", (i, k)) for i in range(PTAP) for k in range(CK)]
        for i in range(4):
            at = (2 * i + 3) * len(taps) // 11
            taps[at:at] = [("pool", (i, 1)), ("pool", (i, 0))]
        ptaps = [("ptap", (i, k)) for i in range(PTAP, 4) for k in range(CK)]
        WEIGHT = {"t": 2.0, "x": 0.3, "y": 1.5, "u": 0.5, "w": 1.2, "p": 2.0, "k": 0.6, "v": 0.6, "A": 0.5, "n": 0.3, "s": 0.8}

        def weight(n):
            return WEIGHT.get(n[0], 1.0)

        def ready(s):
            if s[0] == "pool":
                return ("unit", U_POOL + s[1][0]) in STEPS
            return s[1][1] > 0 or ("glu", s[1][0]) in STEPS

        CHAIN = [(t, n) for t, n, _ in PROD if n != "rs" and not (t == 2 and n[0] in "bs")]
        total, done = sum(weight(n) for _, n in CHAIN), 0.0
        early = sum(weight(n) for t, n in CHAIN if t < 2)
        queues = [(fill, len(fill), 0.0, total), (taps, len(taps), 5.0, early), (ptaps, len(ptaps), 8.0, early)]
        for t, n in CHAIN:
            STEPS += [("delta", (t, n))]
            if t == 2 and n in ("cv", "t1", "y1", "t2"):
                STEPS += [("cnorm", ("cv", "t1", "y1", "t2").index(n))]
            done += weight(n)
            for todo, count, lo, hi in queues:
                while todo and count - len(todo) < count * (done - lo) / (hi - lo) and (todo is fill or ready(todo[0])):
                    STEPS += [todo.pop(0)]
        assert not fill and not taps and not ptaps
        STEPS += [("delta", (2, "rs"))] + whole(U_YD - 2)
        for i in range(H):
            STEPS += [("delta", (2, f"b{i}")), ("rms", i)]
        STEPS += whole(U_YD - 1)
        for i in range(4):
            STEPS += whole(U_YD + i) + ([("mix", 2 * i - 2), ("mix", 2 * i - 1)] if i else [])
        STEPS += [("mix", 6), ("mix", 7)]
        for i in range(8):
            STEPS += ([("vblk", i // 2)] if i % 2 == 0 else []) + whole(U_WO + i) + [("delta", (2, f"s{i // 2}{i % 2}"))]
        STEPS += [("ln", 1)]

        @block.sync
        def _(sp):
            def load_block(l, b):
                n = l * NB + b
                if n >= 3:
                    m, c = divmod(n - 3, NB)
                    sp.wait_ge(w_lo, m * NU + min(2 * c + 2, NU))
                w = min(2, NU - 2 * b)
                sp.dma_start(raw[:, n % 3, 0:w, :], io["w_mix"][l, :, 2 * b:2 * b + w, :]).then_inc(raw_in[n % 3], 16)

            def load_experts(l):
                lo, hi = e_range(l)
                with sp.Fori(lo, hi) as e:
                    for i in range(FU):
                        sp.wait_ge(f_lo, e * FU + (i + 1))
                        k = KT if i < 2 * FT else FT
                        if l == 0:
                            o = i * UNIT if i < 2 * FT else 2 * FT * UNIT + (i - 2 * FT) * FUNIT
                            src = io["w_ffn"][bass.ds(e, 1), :, o:o + k * 128].rearrange("e p n -> p (e n)")
                            dst = fraw[:, i % 5, 0:k * 128]
                        else:
                            w = io["w_moe"][bass.ds(e - lo, 1)].rearrange("e p n -> p (e n)")
                            if i < 2 * FT:
                                o, n, c = (i % 2) * MG * FUNIT, FUNIT, i // 2
                            else:
                                o, n, c = (MG + MU) * FUNIT, D, i - 2 * FT
                            src = w[:, o:o + k * n].rearrange("p (k n) -> p k n", n=n)[:, :, 128 * c:128 * c + 128]
                            dst = fraw[:, i % 5, 0:k * 128].rearrange("p (k n) -> p k n", n=128)
                        sp.dma_start(dst, src).then_inc(fraw_in[i % 5], 16)

            sp.dma_start(X[:, 0:4, :], io["x"][:, 0:4, :]).then_inc(xa_in, 16)
            for l in range(DEPTH):
                load_block(l, 0)
                if l == 0:
                    sp.dma_start(X[:, 4:8, :], io["x"][:, 4:8, :]).then_inc(xb_in, 16)
                    sp.dma_start(par[:, :, :], io["par"]).then_inc(par_in, 16)
                else:
                    sp.wait_ge(split_lo, x_split(l))
                sp.dma_start(qh[:, :, :, :], io["st_qkv"][l]).then_inc(qh_in, 16)
                load_block(l, 1)
                if l == 0:
                    for dst, src in ((con[:, :], io["con"]), (wrt[:, :, :], io["w_router"]), (brt[:, :], io["b_router"])):
                        sp.dma_start(dst, src).then_inc(con_in, 16)
                for dst, src in ((wab[:, :, :], io["w_ab"][l]), (cxs[:, :, :, :], io["st_conv"][l]),
                                 (pxs[:, :, :, :], io["st_pool"][l])):
                    sp.dma_start(dst, src).then_inc(state_in, 16)
                for b in range(2, NB):
                    load_block(l, b)
                    if b == (U_G + 20) // 2:
                        sp.wait_ge(glu_done, 4 * (l + 1))
                        sp.wait_ge(*evicted(l, U_Z))
                        sp.wait_ge(tails_done, 12 * (l + 1))
                        for dst, src in ((io["o_conv_p"][l], cxp[:, :, SEQ:]), (io["o_conv_s"][l], cxs[:, :, :, :]),
                                         (io["o_pool_p"][l], pxp[:, :, SEQ:]), (io["o_pool_s"][l], pxs[:, :, :, :]),
                                         (io["o_qkv_p"][l], tp[:, :, :]), (io["o_qkv_s"][l], ts[:, :, :, :])):
                            sp.dma_start(dst, src).then_inc(out_done, 16)
                    if b == (U_YP + 2) // 2:
                        sp.wait_ge(d_made, 8 * (l + 1))
                        sp.wait_ge(*conved(l, PTAP - 1))
                        sp.wait_ge(*conved(l, 3))
                        sp.wait_ge(out_done, (l * NOUT + 6) * 16)
                        sp.dma_start(Ss[:, :, :, :], io["st_delta"][l]).then_inc(ss_in, 16)
                sp.wait_ge(*read(l, 1, "s1"))
                sp.dma_start(io["o_delta_p"][l], S[:, :, :]).then_inc(out_done, 16)
                for h in range(H):
                    sp.wait_ge(*read(l, 2, f"s{h}1"))
                    sp.dma_start(io["o_delta_s"][l, :, h], Ss[:, h, :, :]).then_inc(out_done, 16)
                sp.wait_ge(out_done, (l + 1) * NOUT * 16)
                sp.wait_ge(split_lo, split(l, "m", 7))
                if l == 0:
                    load_experts(l)
                else:
                    with sp.Fori(0, NE) as e:
                        for i in range(MN):
                            sp.wait_ge(*m_rest_before(e, i))
                            o = min(i, MG + MU) * FUNIT + max(i - MG - MU, 0) * D
                            sp.dma_start(mraw[:, i % MRAW, 0:mwidth(i)],
                                         io["w_moe"][bass.ds(e, 1), :, o:o + mwidth(i)].rearrange("e p n -> p (e n)"))\
                                .then_inc(m_raw[i % MRAW], 16)
                    with sp.If(overflow(sp)):
                        sp.wait_ge(m_acc, 2 + 8 * (NE + 1))
                        load_experts(l)
            sp.wait_ge(aff_done, shifts(DEPTH, 1))
            sp.dma_start(io["y"], X[:, :, :]).then_inc(out_done, 16)
            sp.wait_ge(out_done, (NOUT * DEPTH + 1) * 16)

        @block.gpsimd
        def _(pool):
            def expert_rests(l):
                with pool.Fori(*e_range(l)) as e:
                    for i in range(FU):
                        w = UNIT if i < 2 * FT else FUNIT
                        pool.wait_ge(f_hi, e * FU + (i + 1))
                        pool.tensor_tensor(fl[:, i % 3, 0:w], fraw[:, i % 5, 0:w],
                                           fh[:, i % 3, 0:w].bitcast(f32), ALU.subtract).then_inc(f_lo, 1)

            def rest(n):
                if n >= DEPTH * NU:
                    return
                l, u = divmod(n, NU)
                b = l * NB + u // 2
                pool.wait_ge(w_hi, n + 1)
                pool.tensor_tensor(Wl[:, n % 3, :], raw[:, b % 3, u % 2, :],
                                   Wh[:, n % 3, :].bitcast(f32), ALU.subtract).then_inc(w_lo, 1)

            def tap(l, i, k):
                if k == 0:
                    return
                n = tap_at(l, i, k)
                pool.wait_ge(tap_made, n)
                pool.wait_ge(tap_added, n - 1)
                pool.tensor_tensor(cacc[:, i, :], cacc[:, i, :], G[:, 20 + n % 4, :], ALU.add).then_inc(tap_added, 1)

            pool.sem_inc(f_lo, 5)
            pool.sem_inc(m_lop, len(MPOOL))
            pool.sem_inc(m_lod, MN - len(MPOOL))
            for l in range(DEPTH):
                if l:
                    pool.wait_ge(split_lo, x_split(l))
                for z in (cxp[:, :, 0:CB], pxp[:, :, 0:PB], qxp[:, :, 0:SB], ab[:, :, :]):
                    pool.memset(z, 0.0).then_inc(hist_zero, 1)
                rest(l * NU)
                rest(l * NU + 1)
                for kind, x in STEPS:
                    if kind == "part":
                        u, p = x
                        if p == 0 and u < U_WO + 6:
                            rest(l * NU + u + 2)
                    elif kind == "ptap":
                        tap(l, *x)
                if l == 0:
                    expert_rests(l)
                else:
                    with pool.Fori(0, NE) as e:
                        for i in MPOOL:
                            w = mwidth(i)
                            pool.wait_ge(m_hi, e * MN + (i + 1))
                            pool.tensor_tensor(ml[:, i % MS, 0:w], mraw[:, i % MRAW, 0:w],
                                               mh[:, i % MS, 0:w].bitcast(f32), ALU.subtract).then_inc(m_lop, 1)
                    with pool.If(overflow(pool)):
                        expert_rests(l)

        @block.scalar
        def _(act):
            steps = [0]

            def link(ins):
                steps[0] += 1
                ins.then_inc(ach, 1)
                act.wait_ge(ach, steps[0])

            def head(n):
                if n >= DEPTH * NU:
                    return
                l, u = divmod(n, NU)
                b = l * NB + u // 2
                act.wait_ge(raw_in[b % 3], (b // 3 + 1) * 16)
                if n >= 3:
                    act.wait_ge(unit_done, n - 2)
                act.activation(Wh[:, n % 3, :], raw[:, b % 3, u % 2, :], ACT.Copy).then_inc(w_hi, 1)

            def unit(l, u):
                if u >= U_YP:
                    return
                act.wait_ge(unit_done, l * NU + u + 1)
                bank = gbank(l, FIRST[u])
                pr, sa = bank[:, 0:SEQ], bank[:, SEQ:T].rearrange("p (b t) -> p b t", b=NSEQ)
                if u < U_AB:
                    if u >= 2:
                        act.wait_ge(qc_done, l * 12 + u - 1)
                    if u == 0:
                        act.wait_ge(hist_zero, 4 * (l + 1))
                        act.wait_ge(qh_in, 16 * (l + 1))
                    if u == 5:
                        act.wait_ge(state_in, 48 * (l + 1))
                        act.wait_ge(par_in, 16)
                        act.wait_ge(con_in, 48)
                    act.activation(qxs[:, u % 2, :, 0:SB], qh[:, u, :, :], ACT.Copy)
                    act.activation(tp[:, u, :], bank[:, SEQ - SB:SEQ], ACT.Copy)
                    act.activation(ts[:, u, :, :], sa[:, :, TS - SB:TS], ACT.Copy).then_inc(tails_done, 1)
                    act.activation(qxp[:, u % 2, SB:], pr, ACT.Copy)
                    act.activation(qxs[:, u % 2, :, SB:], sa, ACT.Copy).then_inc(evict_act, 1)
                elif u < U_POOL:
                    i = (u - U_AB) // 2
                    if (u - U_AB) % 2 == 0:
                        act.activation(cxp[:, i, CB:], pr, ACT.Copy, scale=0.5)
                        act.activation(cxs[:, i, :, CB:], sa, ACT.Copy, scale=0.5).then_inc(evict_act, 1)
                    else:
                        if i:
                            act.wait_ge(glu_done, l * 4 + i)
                        act.activation(std[:, :], bank[:, 0:T], ACT.Tanh, scale=0.5).then_inc(evict_act, 1)
                elif u < U_Z:
                    act.activation(pxp[:, u - U_POOL, PB:], pr, ACT.Copy)
                    act.activation(pxs[:, u - U_POOL, :, PB:], sa, ACT.Copy).then_inc(evict_act, 1)
                elif u < U_G:
                    i = u - U_Z
                    if i >= 2:
                        act.wait_ge(z_done, l * 4 + i - 1)
                    act.activation(Z[:, i, :], bank[:, 0:T], ACT.Copy)
                    act.activation(sq[:, i % 2, :], bank[:, 0:T], ACT.Tanh, scale=0.5).then_inc(evict_act, 1)
                else:
                    act.activation(G[:, u - U_G, :], bank[:, 0:T], ACT.Tanh, scale=0.5).then_inc(evict_act, 1)

            def part(l, u, p):
                if p == 0 and u < U_WO + 6:
                    head(l * NU + u + 2)
                if u != U_YP:
                    return
                if p == 0:
                    act.wait_ge(qs_done, 12 * (l + 1))
                for m in (2 * p, 2 * p + 1):
                    g = FIRST[U_YP] + m
                    act.wait_ge(yp_seen, l * 8 + m + 1)
                    if m >= 2:
                        act.wait_ge(yp_done, l * 8 + m - 1)
                    act.activation(yb[:, m % 2, :], gbank(l, g)[:, 0:T], ACT.Copy, scale=P(l, "pscale", m))\
                        .then_inc(evict_act, 1)

            def tap(l, i, k):
                n = tap_at(l, i, k)
                if k == 0:
                    act.wait_ge(glu_done, l * 4 + i + 1)
                elif n > 4:
                    act.wait_ge(tap_added, n - 4)
                w = P(l, "w_dw", CK * i + k)
                dst = cacc[:, i, :] if k == 0 else G[:, 20 + n % 4, :]
                kw = {"bias": P(l, "b_dw", i)} if k == 0 else {}
                f = ACT.Identity if k == 0 else ACT.Copy
                act.activation(dst[:, 0:SEQ], cxp[:, i, k:k + SEQ], f, scale=w, **kw)
                ins = act.activation(dst[:, SEQ:T].rearrange("p (b t) -> p b t", b=NSEQ), cxs[:, i, :, k:k + TS], f,
                                     scale=w, **kw)
                ins.then_inc(tap_made, 1)
                if k == 0:
                    act.wait_ge(tap_made, n)
                    if n > 1:
                        act.wait_ge(tap_added, n - 1)
                    act.sem_inc(tap_added, 1)

            def qact(l, i):
                dst = (qT, kT, vT)[i // 4][:, i % 4, :]
                act.wait_ge(qc_done, l * 12 + i + 1)
                if i >= 2:
                    act.wait_ge(qs_done, l * 12 + i - 1)
                act.activation(yb[:, i % 2, :], dst, ACT.Tanh, scale=0.5).then_inc(qt_done, 1)
                if i < 8:
                    act.wait_ge(qs_done, l * 12 + i + 1)
                    if i >= 2:
                        act.wait_ge(ssq_done, l * 8 + i - 1)
                    act.activation(sq[:, i % 2, :], dst, ACT.Square).then_inc(sqr_done, 1)

            def root(l):
                act.wait_ge(ssq_done, 8 * (l + 1))
                act.activation(std[0:8, :], PS[4][0:8, 0:T], ACT.Sqrt, bias=4e-6).then_inc(nrm_root, 1)

            def ab_part(l):
                act.wait_ge(ab_done, l + 1)
                for t in range(3):
                    ins = act.activation(ab[0:rows(t), t, :], PS[6][0:rows(t), 8 * t:8 * t + 8], ACT.Copy)
                ins.then_inc(ab_copied, 1)
                act.wait_ge(ab_dve, 2 * l + 1)
                link(act.activation(tmp3[:, 1, :, :], tmp3[:, 0, :, :], ACT.Abs))
                link(act.activation(tmp3[:, 1, :, :], tmp3[:, 1, :, :], ACT.Exp, scale=-1.0))
                act.activation(tmp3[:, 1, :, :], tmp3[:, 1, :, :], ACT.Ln, bias=1.0).then_inc(ab_act, 1)
                act.activation(tmp3[:, 2, 0, :], par[:, l, PAR["a_log"][0]:PAR["a_log"][0] + 4], ACT.Exp).then_inc(ab_act, 1)
                act.activation(sc[:, 1, :, :], ab[:, :, 4:8], ACT.Tanh, scale=0.5).then_inc(ab_act, 1)

            def ln(l, w):
                k, n0 = 8, ln_at(l, w)
                src = (None, X, acc)[w]
                for m in range(k):
                    act.wait_ge(ln_cent, n0 + m + 1)
                    if m >= 2:
                        act.wait_ge(ln_sqs, sqs_at(l, w) + m - 1)
                    act.activation(sq[:, m % 2, :], src[:, m, :], ACT.Square).then_inc(ln_sq, 1)
                act.wait_ge(ln_sqs, sqs_at(l, w) + k)
                act.activation(std[:, :], PS[7][:, 0:T], ACT.Sqrt, scale=1.0 / (128 * k),
                               bias=(4e-5 if w == 1 else 1e-5)).then_inc(ln_std, 1)
                if (l, w) == (DEPTH - 1, 2):
                    return
                for m in range(k):
                    if router_next(l, w):
                        act.wait_ge(aff_done, shifts(l, w) + m + 1)
                        act.activation(Xh[:, m, :], X[:, m, :], ACT.Copy).then_inc(split_hi, 1)
                    else:
                        act.wait_ge(ln_norm, n0 + m + 1)
                        act.activation(Xh[:, m, :], X[:, m, :], ACT.Identity, bias=P(l, ("ln1_b", "ln2_b")[w - 1], m))\
                            .then_inc(split_hi, 1)

            def cnorm(l, stage):
                if stage == 1:
                    for m in range(4):
                        act.wait_ge(ln_norm, ln_at(l, 0) + m + 1)
                        act.activation(cacc[:, m, :], cacc[:, m, :], ACT.Identity, scale=P(l, "cg", m), bias=P(l, "cb", m))\
                            .then_inc(caff_done, 1)
                if stage == 2:
                    for m in range(4):
                        act.wait_ge(caff_done, l * 4 + m + 1)
                        if m < 2:
                            act.activation(sq[:, m, :], cacc[:, m, :], ACT.Tanh, scale=0.5).then_inc(csig, 1)
                if stage == 3:
                    for m in (2, 3):
                        act.wait_ge(csilu, l * 4 + m - 1)
                        act.activation(sq[:, m % 2, :], cacc[:, m, :], ACT.Tanh, scale=0.5).then_inc(csig, 1)

            def dsplit(l):
                act.wait_ge(unit_done, l * NU + U_YP)
                for i in range(4):
                    act.wait_ge(d_made, l * 8 + 2 * i + 2)
                    act.activation(Xh[:, 4 + i, :], dif[:, i, :], ACT.Copy).then_inc(split_hi, 1)

            def csplit(l):
                for m in range(4):
                    act.wait_ge(csilu, l * 4 + m + 1)
                    act.activation(Xh[:, m, :], cacc[:, m, :], ACT.Copy, scale=0.5).then_inc(split_hi, 1)

            def delta(l, t, name):
                j, r = number(l, t, name), rows(t)
                b = dbank(j)
                b4 = b[:, 0:4 * r].rearrange("p (h n) -> p h n", h=H)
                if dict(products(t)).get(name) == "act" or name == "R":
                    act.wait_ge(dmm, j + 1)
                inc = consumed(j)[0]
                if name == "cm":
                    act.wait_ge(z_done, 4 * (l + 1))
                    for m in range(4):
                        act.wait_ge(ln_cent, ln_at(l, 0) + m + 1)
                        if m >= 2:
                            act.wait_ge(ln_sqs, sqs_at(l, 0) + m - 1)
                        act.activation(sq[:, m % 2, :], cacc[:, m, :], ACT.Square).then_inc(ln_sq, 1)
                elif name == "cv":
                    act.activation(std[:, :], b[:, 0:T], ACT.Sqrt, scale=1.0 / 512, bias=1e-5).then_inc(inc, 1)
                elif name == "rs":
                    act.activation(std[0:8, :], b[0:8, 0:T], ACT.Sqrt, scale=1.0 / 128, bias=1e-6).then_inc(inc, 1)
                elif name == "gc":
                    act.activation(sc[0:r, 3:5, t, :], b[0:r, 0:8].rearrange("p (a h) -> p a h", a=2), ACT.Copy)
                    act.activation(sc[0:r, 5, t, :], b[0:r, 0:4], ACT.Exp)
                    act.activation(gs[:, :, :], b[:, 16:48].rearrange("p (h n) -> p h n", h=H), ACT.Exp).then_inc(inc, 1)
                    act.wait_ge(dif_made, l * 3 + t + 1)
                    act.activation(sc[0:r, 7, t, :], sc[0:r, 7, t, :], ACT.Exp).then_inc(kdec_made, 1)
                elif name == "R":
                    act.activation(eg[:, :, 0:r], b4, ACT.Exp).then_inc(eg_made, 1)
                    act.wait_ge(arg_made, l * 3 + t + 1)
                    act.activation(dec[0:r, :, 0:r], dec[0:r, :, 0:r], ACT.Exp, scale=-1.0)
                    act.activation(decT[0:r, :, 0:r], decT[0:r, :, 0:r], ACT.Exp).then_inc(dec_made, 1)
                elif name == "NT":
                    act.activation(NT[0:r, :, 0:r], b4[0:r], ACT.Copy).then_inc(inc, 1)
                elif name == "u":
                    if t < 2:
                        act.activation(uu[:, :, :], b4, ACT.Copy).then_inc(inc, 1)
                    else:
                        act.activation(uu[:, :, 0:r], b4, ACT.Copy).then_inc(inc, 1)
                elif name == "w":
                    act.activation(wT[:, :, 0:r], b4, ACT.Copy).then_inc(inc, 1)
                elif name == "v":
                    act.activation(vn[0:r, :, :], b[0:r, :].rearrange("p (h n) -> p h n", h=H), ACT.Copy).then_inc(inc, 1)
                elif name in ("o0", "o1"):
                    c0 = 128 * t + (64 if name == "o1" else 0)
                    act.activation(oT[:, :, c0:c0 + 64], b[:, 0:256].rearrange("p (h n) -> p h n", h=H), ACT.Copy)\
                        .then_inc(inc, 1)
                elif name == "o":
                    act.wait_ge(*read(l, 2, "o"))
                    act.wait_ge(*read(l, 1, "o1"))
                    act.wait_ge(csilu, 4 * (l + 1))
                    for h in range(H):
                        if h >= 2:
                            act.wait_ge(rms_sum, l * 2 + h - 1)
                        act.activation(sq[:, h % 2, :], oT[:, h, :], ACT.Square).then_inc(rms_sq, 1)

            def rms(l, h):
                act.wait_ge(o_made, l * 4 + h + 1)
                act.activation(Xh[:, 4 + h, :], oT[:, h, :], ACT.Copy).then_inc(split_hi, 1)

            def mix(l, m):
                act.wait_ge(mix_done, l * 8 + m + 1)
                act.activation(Mh[:, m, :], G[:, m, :], ACT.Copy).then_inc(split_hi, 1)

            def ffn(l):
                lo, hi = e_range(l)

                def fhead(e, i):
                    w = UNIT if i < 2 * FT else FUNIT
                    act.wait_ge(fraw_in[i % 5], e * (FU // 5 * 16) + (i // 5 + 1) * 16)
                    act.wait_ge(f_done, e * FU + (i + 1))
                    act.activation(fh[:, i % 3, 0:w], fraw[:, i % 5, 0:w], ACT.Copy).then_inc(f_hi, 1)

                def hhead(e, j):
                    if l == 0:
                        act.wait_ge(f_uev, e * FT + (2 + j + 1))
                    else:
                        act.wait_ge(f_h, (e - lo) * FT + (j + 1))
                    act.activation(Hh[:, j, :], hf[:, j % 2, :], ACT.Copy).then_inc(f_hhi, 1)

                with act.Fori(lo, hi) as e:
                    fhead(e, 0)
                    fhead(e, 1)
                    for j in range(FT):
                        fhead(e, 2 * j + 2)
                        if 2 * j + 3 < 2 * FT:
                            fhead(e, 2 * j + 3)
                        act.wait_ge(f_done, e * FU + (3 + 2 * j + 1))
                        act.wait_ge(f_uev, e * FT + (j + 1))
                        act.activation(sg[:, j % 2, :], PS[2 * j % 6][:, 0:T], ACT.Silu).then_inc(f_silu, 1)
                        if j:
                            hhead(e, j - 1)
                    hhead(e, FT - 1)
                    for i in range(2 * FT + 1, FU):
                        fhead(e, i)

            def router(l):
                act.wait_ge(rt_top, 1)
                act.activation(rk[:, 2], rk[:, 2], ACT.Exp).then_inc(rt_exp, 1)

            def gates_everywhere():
                for t in range(3):
                    for half in range(2):
                        act.wait_ge(gb_done, 2 * t + half + 1)
                        act.activation(gbc[:, 4 * half:4 * half + 4, cols(t)],
                                       PS[6 + half][:, :].rearrange("p (e n) -> p e n", e=4)[:, :, 0:rows(t)], ACT.Copy)\
                            .then_inc(gb_copied, 1)

            def experts():
                for q in range(0, 12, 2):
                    t, half, lo = q // 4, q // 2 % 2, q % 2
                    act.wait_ge(xt_mm, q + 1)
                    act.activation(xth[0:rows(t), t, 512 * half:512 * half + 512], PS[q % 6][0:rows(t), :], ACT.Copy)\
                        .then_inc(xt_act, 1)

                def mhead(e, i):
                    act.wait_ge(*m_loaded(e, i))
                    act.wait_ge(*m_before(e, i))
                    act.activation(mh[:, i % MS, 0:mwidth(i)], mraw[:, i % MRAW, 0:mwidth(i)], ACT.Copy).then_inc(m_hi, 1)

                def gathered(e, n):
                    act.wait_ge(m_g, e * 4 + (n + 1))
                    dst = (xeh if n == 0 else xel)[:, 0:4, :]
                    act.activation(dst, PS[(7, 6, 0, 1)[n]][:, :].rearrange("p (k n) -> p k n", k=4), ACT.Copy)\
                        .then_inc(m_xea, 1)

                def y_head(e):
                    act.wait_ge(m_yf, e + 1)
                    act.activation(yh[:, :], yf[:, :], ACT.Copy).then_inc(m_yhi, 1)

                gathered(0, 0)
                gathered(0, 2)
                with act.Fori(0, NE) as e:
                    mhead(e, 0)
                    mhead(e, 1)
                    mhead(e, 2)
                    y_head(e)
                    for i in range(MN):
                        if i + 3 < MN:
                            mhead(e, i + 3)
                        if i == MG - 1:
                            act.wait_ge(m_done, e * MN + (MN + MG))
                            for c in range(3):
                                n = min(512, FUNIT - 512 * c)
                                act.activation(sg1[:, 512 * c:512 * c + n], PS[c][:, 0:n], ACT.Silu).then_inc(m_silu, 1)
                        if i == 7 + SCAT:
                            act.wait_ge(m_pt, e + 1)
                            act.activation(gslot[:, :], PS[6][:, T:T + 1], ACT.Copy)
                            act.activation(PT[:, :], PS[6][:, 0:T], ACT.Copy).then_inc(m_ptc, 1)
                        if i == MG + MU - 1:
                            gathered(e + 1, 0)
                            gathered(e + 1, 2)
                            for c in range(3):
                                k = min(4, FT - 4 * c)
                                act.wait_ge(m_t, e * 3 + (c + 1))
                                act.activation(hTh[:, 4 * c:4 * c + k, :],
                                               PS[3 + c][:, 0:128 * k].rearrange("p (k n) -> p k n", k=k), ACT.Copy)\
                                    .then_inc(m_thi, 1)
                y_head(NE)

            for m in range(KT):
                if m % 4 == 0:
                    act.wait_ge(xa_in if m < 4 else xb_in, 16)
                act.activation(Xh[:, m, :], X[:, m, :], ACT.Copy).then_inc(split_hi, 1)
                if m % 4 == 3:
                    head(m // 4)
            for l in range(DEPTH):
                for kind, x in STEPS:
                    if kind == "part":
                        part(l, *x)
                    elif kind == "unit":
                        unit(l, x)
                    elif kind == "qact":
                        qact(l, x)
                    elif kind == "root":
                        root(l)
                    elif kind == "ab":
                        ab_part(l)
                    elif kind == "ptap":
                        tap(l, *x)
                    elif kind == "cnorm":
                        cnorm(l, x)
                    elif kind == "dsplit":
                        dsplit(l)
                    elif kind == "csplit":
                        csplit(l)
                    elif kind == "ln":
                        ln(l, x)
                    elif kind == "delta":
                        delta(l, *x)
                    elif kind == "rms":
                        rms(l, x)
                    elif kind == "mix":
                        mix(l, x)
                if l == 0:
                    ffn(l)
                else:
                    router(l)
                    experts()
                    with act.If(overflow(act)):
                        act.wait_ge(m_acc, 2 + 8 * (NE + 1))
                        gates_everywhere()
                        ffn(l)
                ln(l, 2)
                head((l + 1) * NU)
                head((l + 1) * NU + 1)

        @block.tensor
        def _(pe):
            def mm3(out, wh, wl, xh, xl, start, stop):
                pe.matmul(out, wl, xh, start=start, stop=False)
                pe.matmul(out, wh, xl, start=False, stop=False)
                return pe.matmul(out, wh, xh, start=False, stop=stop)

            def part(l, u, p):
                n = l * NU + u
                g = FIRST[u]
                hi, lo = Wh[:, n % 3, :], Wl[:, n % 3, :]
                if p == 0:
                    pe.wait_ge(w_lo, n + 1)
                if u < U_YP or u >= U_WO:
                    xh, xl = (Xh, Xl) if u < U_YP else (Mh, Ml)
                    if p == 0:
                        bank_free(pe, l, g)
                    for k in (2 * p, 2 * p + 1):
                        if u == 0:
                            pe.wait_ge(split_lo, x_split(l) - KT + k + 1)
                        if u == U_WO:
                            pe.wait_ge(split_lo, split(l, "m", k))
                        c = slice(128 * k, 128 * k + 128)
                        ins = mm3(gbank(l, g)[:, 0:T], hi[:, c], lo[:, c], xh[:, k, :], xl[:, k, :], k == 0, k == KT - 1)
                elif u == U_YP:
                    if p == 0:
                        pe.wait_ge(split_lo, split(l, "d", 3))
                    for m in (2 * p, 2 * p + 1):
                        bank_free(pe, l, g + m)
                        c = slice(128 * m, 128 * m + 128)
                        mm3(gbank(l, g + m)[:, 0:T], hi[:, c], lo[:, c], Xh[:, 4 + m // 2, :], Xl[:, 4 + m // 2, :],
                            True, True).then_inc(yp_seen, 1)
                    if p == 3:
                        pe.wait_ge(yp_seen, (l + 1) * 8)
                        pe.sem_inc(unit_done, 1)
                    return
                else:
                    k0 = 0 if u < U_YD else 4
                    m = p // 2
                    if p == 0 and u in (U_YC, U_YD):
                        pe.wait_ge(split_lo, split(l, "c" if u < U_YD else "o", 3))
                    if p % 2 == 0:
                        bank_free(pe, l, g + m)
                    for k in (2 * (p % 2), 2 * (p % 2) + 1):
                        c = slice(512 * m + 128 * k, 512 * m + 128 * k + 128)
                        ins = mm3(gbank(l, g + m)[:, 0:T], hi[:, c], lo[:, c], Xh[:, k0 + k, :], Xl[:, k0 + k, :],
                                  k == 0, k == 3)
                if p == 3:
                    ins.then_inc(unit_done, 1)

            def ssq(l, i):
                if (l, i) == (0, 0):
                    pe.wait_ge(con_in, 48)
                pe.wait_ge(sqr_done, l * 8 + i + 1)
                pe.matmul(PS[4][0:8, 0:T], picked(i), sq[:, i % 2, :], start=(i == 0), stop=(i == 7)).then_inc(ssq_done, 1)

            def ab_part(l):
                for t in range(3):
                    for k in range(KT):
                        ins = pe.matmul(PS[6][0:rows(t), 8 * t:8 * t + 8], X[:, k, cols(t)], wab[:, k, :],
                                        start=(k == 0), stop=(k == KT - 1))
                ins.then_inc(ab_done, 1)

            def ln(l, w):
                k, n0 = 8, ln_at(l, w)
                src = (None, X, acc)[w]
                if w == 1:
                    pe.wait_ge(*read(l, 2, "s31"))
                for m in range(k):
                    if w == 1:
                        pe.wait_ge(*evicted(l, FIRST[U_WO + m]))
                    else:
                        pe.wait_ge(acc_ready, l + 1)
                    ins = pe.matmul(PS[6][:, 0:T], ones(), src[:, m, :], start=(m == 0), stop=(m == k - 1))
                ins.then_inc(ln_sum, 1)
                for m in range(k):
                    pe.wait_ge(ln_sq, n0 + m + 1)
                    pe.matmul(PS[7][:, 0:T], ones(), sq[:, m % 2, :], start=(m == 0), stop=(m == k - 1))\
                        .then_inc(ln_sqs, 1)

            def delta(l, t, name):
                j, r = number(l, t, name), rows(t)
                if j % len(PROD) >= 4:
                    pe.wait_ge(*consumed(j - 4))
                b = dbank(j)
                p = "s" if t == 2 else "p"
                cum = C("cum_" + p, r)
                heads = range(H)
                cs = cols(t)

                def out4(h, m, n):
                    return b[0:m, n * h:n * h + n]

                if name == "cm":
                    for m in range(4):
                        pe.wait_ge(*conved(l, m))
                        ins = pe.matmul(b[:, 0:T], ones(), cacc[:, m, :], start=(m == 0), stop=(m == 3))
                elif name == "cv":
                    for m in range(4):
                        pe.wait_ge(ln_sq, ln_at(l, 0) + m + 1)
                        ins = pe.matmul(b[:, 0:T], ones(), sq[:, m % 2, :], start=(m == 0), stop=(m == 3))
                        if m < 3:
                            ins.then_inc(ln_sqs, 1)
                elif name == "rs":
                    for h in heads:
                        pe.wait_ge(rms_sq, l * 4 + h + 1)
                        ins = pe.matmul(b[0:8, 0:T], picked(h), sq[:, h % 2, :], start=(h == 0), stop=(h == H - 1))
                        if h < 2:
                            ins.then_inc(rms_sum, 1)
                elif name[0] == "n":
                    pe.wait_ge(nrm_inv, l + 1)
                    ins = pe.matmul(b[:, 0:T], spread(int(name[1])), rstd[0:8, :], start=True, stop=True)
                elif name[0] == "b":
                    pe.wait_ge(rms_inv, l + 1)
                    ins = pe.matmul(b[:, 0:T], spread(int(name[1])), rstd[0:8, :], start=True, stop=True)
                elif name == "gc":
                    pe.wait_ge(gb_made, l * 3 + t + 1)
                    pe.matmul(b[0:r, 0:4], cum, sc[0:r, 0, t, :], start=True, stop=True)
                    pe.matmul(b[0:r, 4:8], C("blk_" + p, r), sc[0:r, 0, t, :], start=True, stop=True)
                    ni = 2 if t < 2 else 8
                    for h in heads:
                        ins = pe.matmul(b[:, 16 + 8 * h:24 + 8 * h], gb[0:r, h, :], C("ind_" + p, r), start=True, stop=True)
                elif name == "R":
                    for h in heads:
                        ins = pe.matmul(out4(h, 128, r), gb[0:r, h, :], cum, start=True, stop=True)
                elif name in ("kt", "vt"):
                    if name == "kt":
                        pe.wait_ge(*read(l, 0, "n7"))
                        pe.wait_ge(qs_done, (l + 1) * 12)
                    src = kT if name == "kt" else vT
                    for h in heads:
                        ins = pe.transpose(out4(h, r, 128), src[:, h, cs], C("ident"))
                elif name == "G":
                    for h in heads:
                        ins = pe.matmul(out4(h, r, r), kT[:, h, cs], kT[:, h, cs], start=True, stop=True)
                elif name == "A":
                    pe.wait_ge(*read(l, 0, "n3"))
                    for h in heads:
                        ins = pe.matmul(out4(h, r, r), kT[:, h, cs], qT[:, h, cs], start=True, stop=True)
                elif name == "NT":
                    pe.wait_ge(*read(l, t, "G"))
                    for h in heads:
                        ins = pe.transpose(out4(h, r, r), NN[0:r, h, 0:r], C("ident", r)[:, 0:r])
                elif name[0] == "t" :
                    s = int(name[1])
                    if s == 1:
                        pe.wait_ge(xy0_made, l * 3 + t + 1)
                    else:
                        pe.wait_ge(*read(l, t, f"x{s - 1}"))
                    for h in heads:
                        ins = pe.matmul(out4(h, r, r), NT[0:r, h, 0:r], XX[0:r, h, 0:r], start=True, stop=True)
                elif name[0] in "xy":
                    pe.wait_ge(*read(l, t, "t" + name[1]))
                    for h in heads:
                        a, c = (YY, T1) if name[0] == "x" else (T1, YY)
                        ins = pe.matmul(out4(h, r, r), a[0:r, h, 0:r], c[0:r, h, 0:r], start=True, stop=True)
                elif name == "u":
                    pe.wait_ge(*read(l, t, "y5" if t < 2 else "y2"))
                    for h in heads:
                        if t < 2:
                            ins = pe.matmul(out4(h, r, 128), YY[0:r, h, 0:r], vb[0:r, h, :], start=True, stop=True)
                        else:
                            ins = pe.matmul(out4(h, 128, r), vb[0:r, h, :], YY[0:r, h, 0:r], start=True, stop=True)
                elif name == "w":
                    for h in heads:
                        ins = pe.matmul(out4(h, 128, r), kb[0:r, h, :], YY[0:r, h, 0:r], start=True, stop=True)
                elif name in ("p0", "p1"):
                    c = int(name[1])
                    pe.wait_ge(*read(l, t, "w"))
                    if (t, c) == (0, 0):
                        pe.wait_ge(s_zero, l + 1)
                    else:
                        pe.wait_ge(*(read(l, t, "s0") if c else read(l, t - 1, "s1")))
                    for h in heads:
                        ins = pe.matmul(out4(h, 128, 128), wT[:, h, :], S[:, h, :], start=True, stop=True)
                elif name in ("o0", "o1"):
                    c = int(name[1])
                    q = slice(64 * c, 64 * c + 64)
                    for h in heads:
                        pe.matmul(out4(h, 128, 64), S[:, h, :], eg[:, h, q], start=(h == 0), stop=False, skip_group_check=True)
                    pe.wait_ge(*read(l, t, f"p{c}"))
                    for h in heads:
                        ins = pe.matmul(out4(h, 128, 64), vn[q, h, :], aT[q, h, q], start=False, stop=(h == H - 1),
                                        skip_group_check=True)
                elif name in ("s0", "s1"):
                    q = slice(64 * int(name[1]), 64 * int(name[1]) + 64)
                    for h in heads:
                        ins = pe.matmul(out4(h, 128, 128), kd[q, h, :], vn[q, h, :], start=True, stop=True)
                elif name == "p":
                    pe.wait_ge(*read(l, t, "w"))
                    pe.wait_ge(ss_in, 16 * (l + 1))
                    pe.wait_ge(*read(l, t, "A"))
                    for h in heads:
                        for i in range(NSEQ):
                            ins = pe.matmul(b[:, 16 * (8 * h + i):16 * (8 * h + i) + 16], Ss[:, h, i, :],
                                            wT[:, h, :].rearrange("p (a i n) -> p a i n", a=2, i=NSEQ)[:, :, i, :],
                                            start=True, stop=True)
                elif name == "v":
                    pe.wait_ge(*read(l, t, "p"))
                    for h in heads:
                        ins = pe.transpose(out4(h, r, 128), uu[:, h, 0:r], C("ident"))
                elif name == "o":
                    pe.wait_ge(*read(l, t, "v"))
                    for h in heads:
                        ins = pe.matmul(out4(h, 128, 64), vn[0:64, h, :], aT[0:64, h, 0:64], start=True, stop=True)
                else:
                    h, half = int(name[1]), int(name[2])
                    if half == 0:
                        pe.wait_ge(vblk_made, l * 4 + h + 1)
                    ins = pe.matmul(b[:, :], kd[0:64, h, :], vblk[:, 4 * half:4 * half + 4, :], start=True, stop=True)
                ins.then_inc(dmm, 1)

            def router(l):
                for t in range(3):
                    for k in range(KT):
                        ins = pe.matmul(PS[7][0:rows(t), 8 * t:8 * t + 8], X[:, k, cols(t)], wrt[:, k, :],
                                        start=(k == 0), stop=(k == KT - 1))
                ins.then_inc(rt_done, 1)

            def gates_everywhere():
                for t in range(3):
                    pe.wait_ge(gx_made, t + 2)
                    for e in range(NE):
                        if e % 4 == 0 and t:
                            pe.wait_ge(gb_copied, 2 * t + e // 4 - 1)
                        ins = pe.matmul(PS[6 + e // 4][:, 128 * (e % 4):128 * (e % 4) + rows(t)], gexp[0:rows(t), e, :],
                                        C("ident", rows(t))[:, 0:rows(t)], start=True, stop=True)
                        if e % 4 == 3:
                            ins.then_inc(gb_done, 1)

            def experts():
                for q in range(12):
                    t, half, lo = q // 4, q // 2 % 2, q % 2
                    if q >= 6:
                        pe.wait_ge(*((xt_dve, (q - 6) // 2 + 1) if q % 2 else (xt_act, (q - 6) // 2 + 1)))
                    for k in range(4):
                        ins = pe.transpose(PS[q % 6][0:rows(t), 128 * k:128 * k + 128],
                                           (Xl if lo else Xh)[:, 4 * half + k, cols(t)].bitcast(f32), C("ident"))
                    ins.then_inc(xt_mm, 1)
                pe.wait_ge(gx_made, 1)
                for t in range(3):
                    for s in range(t + 1):
                        pe.matmul(PS[7][0:rows(t), 8 * t:8 * t + 8],
                                  C("upto", rows(s))[:, 0:rows(t)] if s == t else ones(rows(s), rows(t)),
                                  rk[0:rows(s), 3, s, :], start=(s == 0), stop=(s == t))
                for s in range(3):
                    ins = pe.matmul(PS[7][:, 32:40], ones(rows(s)), rk[0:rows(s), 3, s, :], start=(s == 0), stop=(s == 2))
                ins.then_inc(pos_done, 1)

                def gather(e, n):
                    src, half = (xth if n < 2 else xtl), n % 2
                    for k in range(4):
                        f = 512 * half + 128 * k
                        for t in range(3):
                            ins = pe.matmul(PS[(7, 6, 0, 1)[n]][:, 128 * k:128 * k + 128], src[0:rows(t), t, f:f + 128],
                                            Pm[0:rows(t), t, :], start=(t == 0), stop=(t == 2))
                    ins.then_inc(m_g, 1)

                def scatter(e, m):
                    if m == 0:
                        pe.wait_ge(m_ylo, e + 2)
                    pe.wait_ge(m_acc, e * 8 + (m + 1))
                    c = slice(128 * m, 128 * m + 128)
                    pe.matmul(PS[6 + m % 2][:, 0:T], yl[:, c], PT[:, :], start=True, stop=False)
                    pe.matmul(PS[6 + m % 2][:, 0:T], yh[:, c], PT[:, :], start=False, stop=True).then_inc(m_sc, 1)

                def wide(e, i, banks, w, xh, xl, k, last):
                    pe.wait_ge(*m_rest(e, i))
                    for c in range(len(banks)):
                        n = min(512, w - 512 * c)
                        o = banks[c][:, 0:n]
                        s = slice(512 * c, 512 * c + n)
                        pe.matmul(o, xl[:, k, :], mh[:, i % MS, s], start=(k == 0), stop=False)
                        pe.matmul(o, xh[:, k, :], ml[:, i % MS, s], start=False, stop=False)
                        ins = pe.matmul(o, xh[:, k, :], mh[:, i % MS, s], start=False, stop=(k == last))
                    ins.then_inc(m_done, 1)

                pe.wait_ge(m_p, 1)
                pe.wait_ge(xt_act, 6)
                pe.wait_ge(xt_dve, 6)
                for n in range(4):
                    gather(0, n)
                with pe.Fori(0, NE) as e:
                    pe.wait_ge(m_xea, e * 2 + 2)
                    pe.wait_ge(m_xev, e * 2 + 2)
                    for k in range(8 + SCAT):
                        if k < MG:
                            wide(e, k, PS[0:3], FUNIT, xeh, xel, k, MG - 1)
                        else:
                            wide(e, k, PS[3:6], FUNIT, xeh, xel, k - MG, MU - 1)
                        if k >= SCAT:
                            scatter(e, k - SCAT)
                    pe.wait_ge(m_acc, e * 8 + (2 + 7))
                    for t in range(3):
                        pe.transpose(PS[6][:, cols(t)], Pm[0:rows(t), t, :].bitcast(f32), C("ident", rows(t))[:, 0:rows(t)])
                    for t in range(3):
                        ins = pe.matmul(PS[6][:, T:T + 1], Pm[0:rows(t), t, :].bitcast(f32), gcol[0:rows(t), t:t + 1],
                                        start=(t == 0), stop=(t == 2))
                    ins.then_inc(m_pt, 1)
                    for k in range(SCAT, MU):
                        wide(e, MG + k, PS[3:6], FUNIT, xeh, xel, k, MU - 1)
                    pe.wait_ge(m_p, e + 2)
                    pe.wait_ge(m_acc, e * 8 + (2 + 8))
                    gather(e + 1, 0)
                    pe.wait_ge(m_ptc, e + 1)
                    gather(e + 1, 1)
                    pe.wait_ge(m_silu, e * 3 + 3)
                    gather(e + 1, 2)
                    gather(e + 1, 3)
                    for c in range(3):
                        pe.wait_ge(m_h, e * 3 + (c + 1))
                        for k in range(4 * c, min(4 * c + 4, FT)):
                            ins = pe.transpose(PS[3 + c][:, 128 * (k % 4):128 * (k % 4) + 128], sg1[:, 128 * k:128 * k + 128],
                                               C("ident"))
                        ins.then_inc(m_t, 1)
                    pe.wait_ge(m_xea, e * 2 + 3)
                    pe.wait_ge(m_xev, e * 2 + 3)
                    for k in range(MD):
                        if k % 4 == 0:
                            pe.wait_ge(m_tlo, e * 3 + (k // 4 + 1))
                        wide(e, MG + MU + k, PS[6:8], D, hTh, hTl, k, MD - 1)
                for m in range(8):
                    scatter(NE, m)

            def ffn(l):
                lo, hi = e_range(l)
                with pe.Fori(lo, hi) as e:
                    for i in range(FU):
                        p = i - 6
                        if p < 0:
                            pe.wait_ge(f_dev, e * 8 + (i + 3))
                        elif p < 2 * FT and p % 2 == 0:
                            pe.wait_ge(f_silu, e * FT + (p // 2 + 1))
                        elif p < 2 * FT:
                            pe.wait_ge(f_uev, e * FT + (2 + p // 2 + 1))
                        else:
                            pe.wait_ge(f_dev, e * 8 + (8 + p - 2 * FT + 1))
                        pe.wait_ge(f_lo, e * FU + (5 + i + 1))
                        if i == 2 * FT:
                            pe.wait_ge(f_hlo, e * FT + (2 + FT))
                        n, xh, xl = (KT, Xh, Xl) if i < 2 * FT else (FT, Hh, Hl)
                        for k in range(n):
                            if i == 0:
                                pe.wait_ge(split_lo, split(l, "x1", k))
                            c = slice(128 * k, 128 * k + 128)
                            ins = mm3(PS[i % 6][:, 0:T], fh[:, i % 3, c], fl[:, i % 3, c], xh[:, k, :], xl[:, k, :],
                                      k == 0, k == n - 1)
                        ins.then_inc(f_done, 1)

            pe.sem_inc(m_done, MN)
            pe.sem_inc(m_ylo, 1)
            pe.sem_inc(m_acc, 2)
            pe.sem_inc(f_done, 3)
            pe.sem_inc(f_uev, 2)
            pe.sem_inc(f_hlo, 2)
            pe.sem_inc(f_dev, 8)
            for l in range(DEPTH):
                for kind, x in STEPS:
                    if kind == "part":
                        part(l, *x)
                    elif kind == "ssq":
                        ssq(l, x)
                    elif kind == "ab":
                        pe.wait_ge(state_in, 48 * (l + 1))
                        if l:
                            pe.wait_ge(aff_done, shifts(l, 1))
                        ab_part(l)
                    elif kind == "ln":
                        ln(l, x)
                    elif kind == "delta":
                        delta(l, *x)
                if l == 0:
                    ffn(l)
                else:
                    pe.wait_ge(aff_done, shifts(l, 2))
                    router(l)
                    pe.wait_ge(split_lo, split(l, "x1", 7))
                    experts()
                    with pe.If(overflow(pe)):
                        gates_everywhere()
                        ffn(l)
                ln(l, 2)

        @block.vector
        def _(dve):
            steps = [0]

            def step(ins):
                steps[0] += 1
                ins.then_inc(vch, 1)
                return steps[0]

            def link(ins):
                dve.wait_ge(vch, step(ins))

            def seqs(ap):
                return ap.rearrange("p (b t) -> p b t", b=NSEQ)

            def qconv(l, i):
                dst = (qT, kT, vT)[i // 4][:, i % 4, :]
                dve.wait_ge(*evicted(l, i))
                s = i % 2
                last = {}
                for k in range(SK_):
                    w = P(l, "w_short", SK_ * i + k)
                    for part in (0, 1):
                        src = qxp[:, s, k:k + SEQ] if part == 0 else qxs[:, s, :, k:k + TS]
                        out = dst[:, 0:SEQ] if part == 0 else seqs(dst[:, SEQ:T])
                        if k:
                            dve.wait_ge(vch, last[part])
                            ins = dve.scalar_tensor_tensor(out=out, in0=src, scalar=w, in1=out, op0=ALU.mult, op1=ALU.add)
                        else:
                            ins = dve.tensor_scalar(out, src, w, None, ALU.mult)
                        if k == SK_ - 1 and part:
                            ins.then_inc(qc_done, 1)
                        else:
                            last[part] = step(ins)
                dve.wait_ge(vch, last[0])

            def qact(l, i):
                dst = (qT, kT, vT)[i // 4][:, i % 4, :]
                dve.wait_ge(qt_done, l * 12 + i + 1)
                dve.wait_ge(qc_done, l * 12 + i + 1)
                dve.scalar_tensor_tensor(out=dst, in0=yb[:, i % 2, :], scalar=1.0, in1=dst, op0=ALU.add, op1=ALU.mult)\
                    .then_inc(qs_done, 1)

            def glu(l, i):
                dve.wait_ge(*evicted(l, U_AB + 2 * i + 1))
                link(dve.scalar_tensor_tensor(out=cxp[:, i, CB:], in0=std[:, 0:SEQ], scalar=1.0, in1=cxp[:, i, CB:],
                                              op0=ALU.add, op1=ALU.mult))
                dve.scalar_tensor_tensor(out=cxs[:, i, :, CB:], in0=seqs(std[:, SEQ:T]), scalar=1.0,
                                         in1=cxs[:, i, :, CB:], op0=ALU.add, op1=ALU.mult).then_inc(glu_done, 1)

            def z_silu(l, i):
                dve.wait_ge(*evicted(l, U_Z + i))
                dve.scalar_tensor_tensor(out=Z[:, i, :], in0=sq[:, i % 2, :], scalar=1.0, in1=Z[:, i, :],
                                         op0=ALU.add, op1=ALU.mult).then_inc(z_done, 1)

            def ab_part(l):
                a = PAR["dt"][0]
                dve.wait_ge(ab_copied, l + 1)
                dve.tensor_tensor(tmp3[:, 0, :, :], ab[:, :, 0:4], over(par[:, l, a:a + 4], 3), ALU.add).then_inc(ab_dve, 1)
                dve.wait_ge(ab_act, 3 * l + 3)
                dve.wait_ge(ab_dve, 2 * l + 1)
                link(dve.scalar_tensor_tensor(out=tmp3[:, 1, :, :], in0=tmp3[:, 0, :, :], scalar=0.0, in1=tmp3[:, 1, :, :],
                                              op0=ALU.max, op1=ALU.add))
                link(dve.scalar_tensor_tensor(out=sc[:, 0, :, :], in0=tmp3[:, 1, :, :], scalar=-1.0,
                                              in1=over(tmp3[:, 2, 0, :], 3), op0=ALU.mult, op1=ALU.mult))
                link(dve.tensor_scalar(sc[:, 1, :, :], sc[:, 1, :, :], 0.5, 0.5, ALU.mult, ALU.add))
                dve.tensor_scalar(sc[:, 2, :, :], sc[:, 1, :, :], 0.5, None, ALU.mult).then_inc(ab_dve, 1)

            def root(l):
                dve.wait_ge(nrm_root, l + 1)
                dve.reciprocal(rstd[0:8, :], std[0:8, :]).then_inc(nrm_inv, 1)

            def pool(l, i, part):
                w = WINDOWS[i]
                dve.wait_ge(*evicted(l, U_POOL + i))
                d = dif[:, i, :]
                if True:
                    src = pxp[:, i, :] if part == 0 else pxs[:, i, :, :]
                    n = PB + (SEQ if part == 0 else TS)

                    def at(ap, a, b):
                        return ap[:, a:b] if part == 0 else ap[:, :, a:b]

                    bufs = [pw[:, q, :] if part == 0 else pw[:, q, 0:NSEQ * n].rearrange("p (b t) -> p b t", b=NSEQ)
                            for q in (0, 1)]
                    cur, step_, q = src, 1, 0
                    while step_ < w:
                        lo = 2 * step_ - 1
                        link(dve.tensor_tensor(at(bufs[q], lo, n), at(cur, lo, n), at(cur, lo - step_, n - step_), ALU.add))
                        cur, step_, q = bufs[q], 2 * step_, 1 - q
                    out = d[:, 0:SEQ] if part == 0 else seqs(d[:, SEQ:T])
                    ins = dve.scalar_tensor_tensor(out=out, in0=at(cur, PB, n), scalar=1.0 / w, in1=at(src, PB, n),
                                                   op0=ALU.mult, op1=ALU.subtract)
                    if part == 0:
                        link(ins)
                        o = CON["invcnt"][0] + 16 * i
                        link(dve.tensor_tensor(pw[:, q, 0:16], cur[:, PB:PB + 16], con[:, o:o + 16], ALU.mult))
                        ins = dve.tensor_tensor(d[:, 0:16], pw[:, q, 0:16], src[:, PB:PB + 16], ALU.subtract)
                    ins.then_inc(d_made, 1)
                    dve.wait_ge(d_made, l * 8 + 2 * i + (2 if part == 0 else 1))

            last = {}

            def tap(l, i, k):
                w = P(l, "w_dw", CK * i + k)
                for part in (0, 1):
                    src = cxp[:, i, k:k + SEQ] if part == 0 else cxs[:, i, :, k:k + TS]
                    out = cacc[:, i, 0:SEQ] if part == 0 else seqs(cacc[:, i, SEQ:T])
                    if k == 0:
                        if part == 0:
                            dve.wait_ge(glu_done, l * 4 + i + 1)
                        ins = dve.tensor_scalar(out, src, w, P(l, "b_dw", i), ALU.mult, ALU.add)
                    else:
                        dve.wait_ge(vch, last[part])
                        ins = dve.scalar_tensor_tensor(out=out, in0=src, scalar=w, in1=out, op0=ALU.mult, op1=ALU.add)
                    if k == CK - 1 and part:
                        ins.then_inc(conv_dve, 1)
                    else:
                        last[part] = step(ins)

            def ln(l, w):
                k, n0 = 8, ln_at(l, w)
                src = (None, X, acc)[w]
                dve.wait_ge(ln_sum, 2 * l + w)
                for m in range(k):
                    if w == 1:
                        dve.wait_ge(*evicted(l, FIRST[U_WO + m]))
                    else:
                        dve.wait_ge(acc_ready, l + 1)
                    dve.scalar_tensor_tensor(out=src[:, m, :], in0=PS[6][:, 0:T], scalar=-1.0 / (128 * k), in1=src[:, m, :],
                                             op0=ALU.mult, op1=ALU.add).then_inc(ln_cent, 1)
                dve.wait_ge(ln_std, 2 * l + w)
                dve.wait_ge(ln_cent, n0 + k)
                link(dve.reciprocal(rstd[:, :], std[:, :]))
                gain, bias = ("ln1_g", "ln1_b") if w == 1 else ("ln2_g", "ln2_b")

                def scaled(m):
                    dve.scalar_tensor_tensor(out=X[:, m, :], in0=src[:, m, :], scalar=P(l, gain, m), in1=rstd[:, :],
                                             op0=ALU.mult, op1=ALU.mult).then_inc(ln_norm, 1)

                def shifted(m):
                    dve.wait_ge(ln_norm, n0 + m + 1)
                    dve.tensor_scalar(X[:, m, :], X[:, m, :], P(l, bias, m), None, ALU.add).then_inc(aff_done, 1)

                def rest(m):
                    dve.wait_ge(split_hi, split(l, "x1" if w == 1 else "x2", m))
                    dve.scalar_tensor_tensor(out=Xl[:, m, :], in0=X[:, m, :], scalar=P(l, bias, m),
                                             in1=Xh[:, m, :].bitcast(f32), op0=ALU.add, op1=ALU.subtract).then_inc(split_lo, 1)

                if (l, w) == (DEPTH - 1, 2) or router_next(l, w):
                    for m in range(k):
                        scaled(m)
                    for m in range(k):
                        shifted(m)
                    if w == 1:
                        for m in range(k):
                            dve.wait_ge(split_hi, split(l, "x1", m))
                            dve.tensor_tensor(Xl[:, m, :], X[:, m, :], Xh[:, m, :].bitcast(f32), ALU.subtract)\
                                .then_inc(split_lo, 1)
                else:
                    scaled(0)
                    for m in range(1, k):
                        scaled(m)
                        rest(m - 1)
                    rest(k - 1)
                    for m in range(k):
                        shifted(m)

            def acc_start(l):
                dve.wait_ge(aff_done, shifts(l, 2))
                dve.tensor_scalar(acc[:, :, :], X[:, :, :], ALPHA, None, ALU.mult).then_inc(acc_init, 1)

            def cnorm(l, stage):
                n0 = ln_at(l, 0)
                if stage == 0:
                    dve.wait_ge(*read(l, 2, "cv"))
                    dve.wait_ge(ln_cent, n0 + 4)
                    link(dve.reciprocal(rstd[:, :], std[:, :]))
                    for m in range(4):
                        dve.tensor_tensor(cacc[:, m, :], cacc[:, m, :], rstd[:, :], ALU.mult).then_inc(ln_norm, 1)
                if stage == 3:
                    for m in range(4):
                        dve.wait_ge(csig, l * 4 + m + 1)
                        dve.scalar_tensor_tensor(out=cacc[:, m, :], in0=sq[:, m % 2, :], scalar=1.0, in1=cacc[:, m, :],
                                                 op0=ALU.add, op1=ALU.mult).then_inc(csilu, 1)

            def dsplit(l):
                for i in range(4):
                    dve.wait_ge(split_hi, split(l, "d", i))
                    dve.tensor_tensor(Xl[:, 4 + i, :], dif[:, i, :], Xh[:, 4 + i, :].bitcast(f32), ALU.subtract)\
                        .then_inc(split_lo, 1)

            def csplit(l):
                for m in range(4):
                    dve.wait_ge(split_hi, split(l, "c", m))
                    dve.scalar_tensor_tensor(out=Xl[:, m, :], in0=cacc[:, m, :], scalar=0.5,
                                             in1=Xh[:, m, :].bitcast(f32), op0=ALU.mult, op1=ALU.subtract)\
                        .then_inc(split_lo, 1)

            def delta(l, t, name):
                j, r = number(l, t, name), rows(t)
                b = dbank(j)
                n4 = {"kt": 128, "vt": 128, "p0": 128, "p1": 128, "s0": 128, "s1": 128}.get(name, r)
                b4 = b[:, 0:4 * n4].rearrange("p (h n) -> p h n", h=H)
                p = "s" if t == 2 else "p"
                inc = consumed(j)[0]
                if (dict(products(t))[name] == "dve") and not (t == 2 and name[0] == "s"):
                    dve.wait_ge(dmm, j + 1)

                def scal(i):
                    return sc[0:r, i, t, :]

                def lev(s, n="lev"):
                    o = CON[n][0] + 128 * s
                    return over(con[0:r, o:o + r], H)

                if name[0] == "n":
                    i = int(name[1])
                    dst = (qT if i < 4 else kT)[:, i % 4, :]
                    dve.wait_ge(qs_done, l * 12 + i + 1)
                    dve.scalar_tensor_tensor(out=dst, in0=dst, scalar=128 ** -0.5 if i < 4 else 1.0, in1=b[:, 0:T],
                                             op0=ALU.mult, op1=ALU.mult).then_inc(inc, 1)
                elif name == "rs":
                    dve.wait_ge(*read(l, t, "rs"))
                    dve.reciprocal(rstd[0:8, :], std[0:8, :]).then_inc(rms_inv, 1)
                elif name[0] == "b":
                    h = int(name[1])
                    dve.wait_ge(*read(l, 2, "o"))
                    dve.scalar_tensor_tensor(out=oT[:, h, :], in0=oT[:, h, :], scalar=P(l, "dn_g"), in1=b[:, 0:T],
                                             op0=ALU.mult, op1=ALU.mult).then_inc(inc, 1)
                elif name == "cm":
                    for m in range(4):
                        dve.wait_ge(*conved(l, m))
                        ins = dve.scalar_tensor_tensor(out=cacc[:, m, :], in0=b[:, 0:T], scalar=-1.0 / 512,
                                                       in1=cacc[:, m, :], op0=ALU.mult, op1=ALU.add)
                        if m < 3:
                            ins.then_inc(ln_cent, 1)
                    link(ins)
                    dve.sem_inc(ln_cent, 1)
                    dve.sem_inc(inc, 1)
                elif name == "gc":
                    dve.wait_ge(ab_dve, 2 * l + 2)
                    dve.tensor_copy(gb[0:r, :, :], along(scal(0), 128)).then_inc(gb_made, 1)
                    dve.wait_ge(*read(l, t, "gc"))
                    dve.tensor_tensor(scal(7), scal(4), scal(3), ALU.subtract).then_inc(dif_made, 1)
                    link(dve.tensor_tensor(scal(6), scal(1), scal(5), ALU.mult))
                elif name == "R":
                    dve.wait_ge(eg_made, l * 3 + t + 1)
                    link(dve.tensor_tensor(decT[0:r, :, 0:r], b4[0:r], along(scal(3), r), ALU.subtract))
                    dve.tensor_scalar(dec[0:r, :, 0:r], decT[0:r, :, 0:r], 0.0, None, ALU.max).then_inc(inc, 1)
                    dve.tensor_scalar(decT[0:r, :, 0:r], decT[0:r, :, 0:r], 0.0, None, ALU.min).then_inc(arg_made, 1)
                elif name == "kt":
                    dve.wait_ge(kdec_made, l * 3 + t + 1)
                    dve.tensor_tensor(kb[0:r, :, :], b4[0:r], along(scal(6), 128), ALU.mult)
                    dve.tensor_tensor(kd[0:r, :, :], b4[0:r], along(scal(7), 128), ALU.mult).then_inc(inc, 1)
                elif name == "vt":
                    dve.tensor_tensor(vb[0:r, :, :], b4[0:r], along(scal(2), 128), ALU.mult).then_inc(inc, 1)
                elif name == "G":
                    dve.wait_ge(dec_made, l * 3 + t + 1)
                    link(dve.scalar_tensor_tensor(out=dec[0:r, :, 0:r], in0=dec[0:r, :, 0:r], scalar=-1.0,
                                                  in1=over(C("strict_" + p, r), H), op0=ALU.mult, op1=ALU.mult))
                    link(dve.tensor_tensor(dec[0:r, :, 0:r], dec[0:r, :, 0:r], along(scal(1), r), ALU.mult))
                    dve.tensor_tensor(NN[0:r, :, 0:r], b4[0:r], dec[0:r, :, 0:r], ALU.mult).then_inc(inc, 1)
                elif name == "A":
                    link(dve.tensor_tensor(decT[0:r, :, 0:r], decT[0:r, :, 0:r], over(C("cum_" + p, r), H), ALU.mult))
                    dve.wait_ge(*read(l, 0, "n3"))
                    dst = eg[:, :, :] if t < 2 else wT[:, :, 64:128]
                    dve.tensor_tensor(dst, qT[:, :, cols(t)], eg[:, :, 0:r], ALU.mult)
                    dve.tensor_tensor(aT[0:r, :, 0:r], b4[0:r], decT[0:r, :, 0:r], ALU.mult).then_inc(inc, 1)
                elif name == "NT":
                    dve.wait_ge(*read(l, t, "G"))
                    link(dve.tensor_tensor(XX[0:r, :, 0:r], NN[0:r, :, 0:r], lev(0), ALU.mult))
                    link(dve.tensor_tensor(XX[0:r, :, 0:r], XX[0:r, :, 0:r], over(C("ident", r)[:, 0:r], H), ALU.add))
                    dve.wait_ge(*read(l, t, "NT"))
                    link(dve.tensor_tensor(YY[0:r, :, 0:r], NT[0:r, :, 0:r], lev(0, "lev0t"), ALU.mult))
                    dve.tensor_tensor(YY[0:r, :, 0:r], YY[0:r, :, 0:r], over(C("ident", r)[:, 0:r], H), ALU.add)\
                        .then_inc(xy0_made, 1)
                elif name[0] == "t":
                    dve.tensor_tensor(T1[0:r, :, 0:r], b4[0:r], lev(int(name[1])), ALU.mult).then_inc(inc, 1)
                elif name[0] in "xy":
                    m = XX if name[0] == "x" else YY
                    s = int(name[1])
                    if s == 1:
                        dve.wait_ge(xy0_made, l * 3 + t + 1)
                    elif name[0] == "y":
                        dve.wait_ge(*read(l, t, f"y{s - 1}"))
                    dve.tensor_tensor(m[0:r, :, 0:r], m[0:r, :, 0:r], b4[0:r], ALU.add).then_inc(inc, 1)
                elif name in ("p0", "p1"):
                    q = slice(64 * int(name[1]), 64 * int(name[1]) + 64)
                    dve.wait_ge(*read(l, t, "u"))
                    dve.tensor_tensor(vn[q, :, :], uu[q, :, :], b4[q], ALU.subtract).then_inc(inc, 1)
                elif name in ("s0", "s1"):
                    c = int(name[1])
                    for h in range(H):
                        ins = dve.scalar_tensor_tensor(out=S[:, h, :], in0=S[:, h, :], scalar=gs[:, h, c:c + 1],
                                                       in1=b4[:, h, :], op0=ALU.mult, op1=ALU.add)
                    ins.then_inc(inc, 1)
                    dve.wait_ge(*read(l, t, name))
                elif name == "p":
                    dve.wait_ge(*read(l, t, "u"))
                    both = b[:, :].rearrange("p (h i a n) -> p h i a n", h=H, i=NSEQ, a=2)
                    at = [a.rearrange("p h (i n) -> p h i n", i=NSEQ) for a in (uu[:, :, 0:r], oT[:, :, cols(t)])]
                    dve.tensor_copy(at[1], both[:, :, :, 1, :])
                    dve.tensor_tensor(at[0], at[0], both[:, :, :, 0, :], ALU.subtract).then_inc(inc, 1)
                elif name == "o":
                    dve.wait_ge(*read(l, t, "p"))
                    dve.tensor_tensor(oT[:, :, cols(t)], oT[:, :, cols(t)], b4, ALU.add).then_inc(inc, 1)
                elif name == "v":
                    dve.wait_ge(*read(l, t, "v"))
                elif name[0] == "s":
                    h, half = int(name[1]), int(name[2])
                    q = slice(4 * half, 4 * half + 4)
                    dve.wait_ge(dmm, j + 1)
                    dve.tensor_tensor(Ss[:, h, q, :], Ss[:, h, q, :], b[:, :].rearrange("p (n d) -> p n d", n=4), ALU.add)\
                        .then_inc(inc, 1)

            def vblk_of(l, h):
                dve.wait_ge(dmm, number(l, 2, f"s{h}0"))
                dve.tensor_tensor(vblk[:, :, :], over(vn[0:64, h, :], NSEQ), along(C("ind_s", 64), 128), ALU.mult)\
                    .then_inc(vblk_made, 1)
                link(dve.tensor_tensor(Ss[:, h, :, :], Ss[:, h, :, :], along(gs[:, h, :], 128), ALU.mult))

            def rms(l, h):
                dve.wait_ge(*read(l, 2, f"b{h}"))
                dve.scalar_tensor_tensor(out=oT[:, h, :], in0=oT[:, h, :], scalar=0.5, in1=Z[:, h, :],
                                         op0=ALU.mult, op1=ALU.mult).then_inc(o_made, 1)
                dve.wait_ge(split_hi, split(l, "o", h))
                dve.tensor_tensor(Xl[:, 4 + h, :], oT[:, h, :], Xh[:, 4 + h, :].bitcast(f32), ALU.subtract)\
                    .then_inc(split_lo, 1)

            def part(l, u, p):
                if u != U_YP:
                    return
                for m in (2 * p, 2 * p + 1):
                    dve.wait_ge(*evicted(l, FIRST[U_YP] + m))
                    dve.scalar_tensor_tensor(out=G[:, m, :], in0=G[:, m, :], scalar=1.0, in1=yb[:, m % 2, :],
                                             op0=ALU.add, op1=ALU.mult).then_inc(yp_done, 1)

            def branch(l, u, gate0, last_branch):
                dve.wait_ge(unit_done, l * NU + u + 1)
                if u == U_YC:
                    dve.wait_ge(yp_done, 8 * (l + 1))
                for i in range(2):
                    g = FIRST[u] + i
                    m = 2 * (u - (U_YD if last_branch else U_YC)) + i
                    dve.scalar_tensor_tensor(out=tt[:, i, :], in0=G[:, gate0 + m, :], scalar=1.0, in1=gbank(l, g)[:, 0:T],
                                             op0=ALU.add, op1=ALU.mult).then_inc(evict_dve, 1)
                    dve.wait_ge(*evicted(l, g))
                    ins = dve.tensor_tensor(G[:, m, :], G[:, m, :], tt[:, i, :], ALU.add)
                    if last_branch:
                        ins.then_inc(mix_done, 1)
                    else:
                        link(ins)

            def mix(l, m):
                dve.wait_ge(split_hi, split(l, "m", m))
                dve.tensor_tensor(Ml[:, m, :], G[:, m, :], Mh[:, m, :].bitcast(f32), ALU.subtract).then_inc(split_lo, 1)

            def unit(l, u):
                if U_Z <= u < U_G:
                    z_silu(l, u - U_Z)
                elif U_YC <= u < U_YD:
                    branch(l, u, 8, False)
                elif U_YD <= u < U_WO:
                    branch(l, u, 16, True)
                elif u >= U_WO:
                    m = u - U_WO
                    dve.wait_ge(unit_done, l * NU + u + 1)
                    dve.scalar_tensor_tensor(out=X[:, m, :], in0=X[:, m, :], scalar=2 * ALPHA, in1=gbank(l, FIRST[u])[:, 0:T],
                                             op0=ALU.mult, op1=ALU.add).then_inc(evict_dve, 1)

            def ffn(l):
                lo, hi = e_range(l)

                def rest(e, j):
                    dve.wait_ge(f_hhi, e * FT + (j + 1))
                    dve.tensor_tensor(Hl[:, j, :], hf[:, j % 2, :], Hh[:, j, :].bitcast(f32), ALU.subtract).then_inc(f_hlo, 1)

                dve.wait_ge(acc_init, 1 if l == 0 else 3)
                with dve.Fori(lo, hi) as e:
                    for j in range(FT):
                        dve.wait_ge(f_silu, e * FT + (j + 1))
                        dve.wait_ge(f_done, e * FU + (3 + 2 * j + 2))
                        dve.wait_ge(f_hlo, e * FT + (j + 1))
                        dve.tensor_tensor(hf[:, j % 2, :], sg[:, j % 2, :], PS[(2 * j + 1) % 6][:, 0:T], ALU.mult)\
                            .then_inc(f_uev, 1)
                        if l % 2:
                            dve.wait_ge(f_uev, e * FT + (2 + j + 1))
                            dve.tensor_tensor(hf[:, j % 2, :], hf[:, j % 2, :],
                                              gbc[:, bass.ds(e - lo, 1), :].rearrange("p e t -> p (e t)"), ALU.mult)\
                                .then_inc(f_h, 1)
                        if j:
                            rest(e, j - 1)
                    rest(e, FT - 1)
                    for m in range(8):
                        dve.wait_ge(f_done, e * FU + (3 + 2 * FT + m + 1))
                        dve.wait_ge(f_dev, e * 8 + (m + 1))
                        dve.tensor_tensor(acc[:, m, :], acc[:, m, :], PS[(2 * FT + m) % 6][:, 0:T], ALU.add).then_inc(f_dev, 1)
                dve.wait_ge(f_dev, 8 + 8 * hi)

            def router(l):
                lg, mx, ex, cnt, den = rk[:, 0], rk[:, 1, :, 0:1], rk[:, 2], rk[:, 3], rk[:, 4, :, 0:1]
                link(dve.memset(rk[:, :, :, :], 0.0))
                dve.wait_ge(rt_done, 1)
                for t in range(3):
                    ins = dve.tensor_tensor(lg[0:rows(t), t, :], PS[7][0:rows(t), 8 * t:8 * t + 8], brt[0:rows(t), :], ALU.add)
                link(ins)
                for t in range(3):
                    le = along(lg[:, t, :], NE)
                    lj = over(lg[:, t, :], NE)
                    dve.tensor_tensor(rc[:, 0, t], lj, le, ALU.is_gt)
                    link(dve.tensor_tensor(rc[:, 1, t], lj, le, ALU.is_equal))
                    link(dve.tensor_tensor(rc[:, 1, t], rc[:, 1, t],
                                           C("before").rearrange("p (e j) -> p e j", e=NE), ALU.mult))
                    link(dve.tensor_tensor(rc[:, 0, t], rc[:, 0, t], rc[:, 1, t], ALU.add))
                    link(dve.tensor_reduce(cnt[:, t, :], rc[:, 0, t], AX.X, ALU.add))
                dve.tensor_scalar(cnt, cnt, 1.5, None, ALU.is_lt).then_inc(gx_made, 1)
                link(dve.tensor_reduce(mx, lg, AX.X, ALU.max))
                dve.tensor_tensor(ex, lg, mx.broadcast_to([128, 3, NE]), ALU.subtract).then_inc(rt_top, 1)
                dve.wait_ge(rt_exp, 1)
                dve.wait_ge(gx_made, 1)
                link(dve.tensor_tensor(ex, ex, cnt, ALU.mult))
                link(dve.tensor_reduce(den, ex, AX.X, ALU.add))
                link(dve.reciprocal(den, den))
                link(dve.tensor_tensor(gate[:, :, 0:NE], ex, den.broadcast_to([128, 3, NE]), ALU.mult))

            def gates_everywhere():
                for t in range(3):
                    if t:
                        dve.wait_ge(gb_done, 2 * t)
                    dve.tensor_copy(gexp[:, :, :], along(gate[:, t, 0:NE], 128)).then_inc(gx_made, 1)

            def experts():
                for q in range(1, 12, 2):
                    t, half = q // 4, q // 2 % 2
                    dve.wait_ge(xt_mm, q + 1)
                    dve.tensor_copy(xtl[0:rows(t), t, 512 * half:512 * half + 512], PS[q % 6][0:rows(t), :])\
                        .then_inc(xt_dve, 1)
                dve.wait_ge(pos_done, 1)
                dve.memset(gate[:, :, NE:], 0.0)
                link(dve.memset(posm[:, :, :], -1.0))
                for t in range(3):
                    r = rows(t)
                    link(dve.tensor_tensor(posm[0:r, t, 0:NE], PS[7][0:r, 8 * t:8 * t + 8], rk[0:r, 3, t, :], ALU.mult))
                    link(dve.tensor_scalar(posm[0:r, t, 0:NE], posm[0:r, t, 0:NE], 1.0, None, ALU.subtract))
                link(dve.tensor_reduce(rk[:, 1, 0, 0:1], PS[7][:, 32:40], AX.X, ALU.max))
                dve.tensor_scalar(flag[:, :], rk[:, 1, 0, 0:1], CAP + 0.5, None, ALU.is_gt).then_inc(flag_made, 1)

                def places(e, seen):
                    for t in range(3):
                        dve.tensor_scalar(Pm[:, t, :], C("slot"), seen(posm, t), None, ALU.is_equal)
                    dve.tensor_copy(gcol[:, :], seen(gate, None)).then_inc(m_p, 1)

                def column(e):
                    def seen(a, t):
                        ap = a[:, :, bass.ds(e, 1)] if t is None else a[:, t, bass.ds(e, 1)]
                        return ap.rearrange("p t e -> p (t e)") if t is None else ap
                    return seen

                def mlo(e, i):
                    if i in MPOOL:
                        return
                    w = mwidth(i)
                    dve.wait_ge(m_hi, e * MN + (i + 1))
                    dve.tensor_tensor(ml[:, i % MS, 0:w], mraw[:, i % MRAW, 0:w],
                                      mh[:, i % MS, 0:w].bitcast(f32), ALU.subtract).then_inc(m_lod, 1)

                def gathered(e, n):
                    dve.wait_ge(m_g, e * 4 + (n + 1))
                    dst = (xeh if n == 1 else xel)[:, 4:8, :]
                    dve.tensor_copy(dst, PS[(7, 6, 0, 1)[n]][:, :].rearrange("p (k n) -> p k n", k=4)).then_inc(m_xev, 1)

                def y_full(e):
                    dve.wait_ge(m_done, e * MN + MN)
                    dve.wait_ge(m_ylo, e + 1)
                    for c in range(2):
                        ins = dve.tensor_scalar(yf[:, 512 * c:512 * c + 512], PS[6 + c][:, :], gslot[:, 0:1], None, ALU.mult)
                    ins.then_inc(m_yf, 1)

                def y_rest(e):
                    dve.wait_ge(m_yhi, e + 1)
                    dve.wait_ge(m_yf, e + 1)
                    dve.tensor_tensor(yl[:, :], yf[:, :], yh[:, :].bitcast(f32), ALU.subtract).then_inc(m_ylo, 1)

                def add(e, m):
                    dve.wait_ge(m_sc, e * 8 + (m + 1))
                    dve.wait_ge(m_acc, e * 8 + (m + 1))
                    dve.tensor_tensor(acc[:, m, :], acc[:, m, :], PS[6 + m % 2][:, 0:T], ALU.add).then_inc(m_acc, 1)

                link(dve.memset(gslot[:, :], 0.0))
                link(dve.memset(PT[:, :].bitcast(f32), 0.0))
                for t in range(3):
                    dve.tensor_scalar(Pm[:, t, :], C("slot"), posm[:, t, 0:1], None, ALU.is_equal)
                dve.tensor_copy(gcol[:, :], gate[:, :, 0]).then_inc(m_p, 1)
                gathered(0, 1)
                gathered(0, 3)
                dve.wait_ge(m_xea, 2)
                dve.wait_ge(m_xev, 2)
                dve.wait_ge(acc_init, 2)
                with dve.Fori(0, NE) as e:
                    mlo(e, 0)
                    mlo(e, 1)
                    y_full(e)
                    mlo(e, 2)
                    for i in range(MN):
                        if i + 3 < MN:
                            mlo(e, i + 3)
                        if i == 0:
                            y_rest(e)
                        if SCAT <= i < SCAT + 8:
                            add(e, i - SCAT)
                        if i == 7 + SCAT:
                            dve.wait_ge(m_pt, e + 1)
                            places(e, column(e + 1))
                        if i == MG + MU - 1:
                            dve.wait_ge(m_silu, e * 3 + 3)
                            dve.wait_ge(m_done, e * MN + (MN + MG + MU))
                            for c in range(3):
                                n = min(512, FUNIT - 512 * c)
                                s = slice(512 * c, 512 * c + n)
                                dve.tensor_tensor(sg1[:, s], sg1[:, s], PS[3 + c][:, 0:n], ALU.mult).then_inc(m_h, 1)
                            gathered(e + 1, 1)
                            gathered(e + 1, 3)
                            for c in range(3):
                                k = min(4, FT - 4 * c)
                                dve.wait_ge(m_thi, e * 3 + (c + 1))
                                dve.tensor_tensor(hTl[:, 4 * c:4 * c + k, :],
                                                  PS[3 + c][:, 0:128 * k].rearrange("p (k n) -> p k n", k=k),
                                                  hTh[:, 4 * c:4 * c + k, :].bitcast(f32), ALU.subtract).then_inc(m_tlo, 1)
                y_full(NE)
                y_rest(NE)
                for m in range(8):
                    add(NE, m)
                dve.wait_ge(m_acc, 2 + 8 * (NE + 1))

            for m in range(KT):
                dve.wait_ge(split_hi, m + 1)
                dve.tensor_tensor(Xl[:, m, :], X[:, m, :], Xh[:, m, :].bitcast(f32), ALU.subtract).then_inc(split_lo, 1)
            dve.wait_ge(par_in, 16)
            for l in range(DEPTH):
                for kind, x in STEPS:
                    if kind == "part":
                        part(l, *x)
                    elif kind == "unit":
                        unit(l, x)
                    elif kind == "qconv":
                        qconv(l, x)
                    elif kind == "qact":
                        qact(l, x)
                    elif kind == "glu":
                        glu(l, x)
                    elif kind == "ab":
                        ab_part(l)
                    elif kind == "root":
                        root(l)
                    elif kind == "pool":
                        pool(l, *x)
                    elif kind == "tap":
                        tap(l, *x)
                    elif kind == "cnorm":
                        cnorm(l, x)
                    elif kind == "dsplit":
                        dsplit(l)
                    elif kind == "csplit":
                        csplit(l)
                    elif kind == "ln":
                        ln(l, x)
                    elif kind == "delta":
                        if x == (0, "gc"):
                            if l:
                                dve.wait_ge(out_done, l * NOUT * 16)
                            dve.memset(S[:, :, :], 0.0).then_inc(s_zero, 1)
                        delta(l, *x)
                    elif kind == "vblk":
                        vblk_of(l, x)
                    elif kind == "rms":
                        rms(l, x)
                    elif kind == "mix":
                        mix(l, x)
                if l == 0:
                    acc_start(l)
                    ffn(l)
                else:
                    router(l)
                    acc_start(l)
                    experts()
                    with dve.If(overflow(dve)):
                        acc_start(l)
                        gates_everywhere()
                        ffn(l)
                dve.sem_inc(acc_ready, 1)
                ln(l, 2)


def _constants():
    i, j = np.arange(128)[:, None], np.arange(128)[None, :]
    out = np.zeros((128, NCON), np.float32)

    def put(name, a):
        o, w = CON[name]
        out[:a.shape[0], o:o + w] = a.reshape(a.shape[0], w)

    put("ident", (i == j).astype(np.float32))
    put("ones", np.ones((128, 1), np.float32))
    put("pick", np.tile((np.arange(15) == 7).astype(np.float32), (128, 1)))
    for p, n, c in (("p", 128, CHUNK), ("s", 64, TS)):
        a, b = i[:n], j[:, :n]
        same = a // c == b // c
        put("cum_" + p, (same & (a <= b)).astype(np.float32))
        put("blk_" + p, same.astype(np.float32))
        put("strict_" + p, (same & (a > b)).astype(np.float32))
        put("ind_" + p, (a // c == np.arange(8)[None]).astype(np.float32))
    lev = [((i >> (s + 1)) == (j >> (s + 1))) & ((i >> s) & 1 == 1) & ((j >> s) & 1 == 0) for s in range(6)]
    put("lev", np.stack(lev, 1).astype(np.float32))
    put("lev0t", lev[0].T.astype(np.float32))
    put("invcnt", np.tile(np.concatenate([1.0 / np.minimum(np.arange(16) + 1, w) for w in WINDOWS]).astype(np.float32), (128, 1)))
    put("upto", (i <= j).astype(np.float32))
    put("slot", np.tile(np.arange(128, dtype=np.float32), (128, 1)))
    put("before", np.tile((np.arange(NE)[None, :] < np.arange(NE)[:, None]).astype(np.float32).ravel(), (128, 1)))
    return out


def _tiles(a):
    return np.moveaxis(a.reshape(a.shape[:-1] + (-1, 128)), -1, 0)


def kernel(**inputs):
    import concourse.bacc as bacc
    from concourse import mybir
    from concourse.bass_utils import run_bass_kernel_spmd

    a = {k: np.asarray(v) for k, v in inputs.items()}
    L = range(DEPTH)

    def units(w):
        k, n = w.shape[0] // 128, w.shape[1] // 128
        return w.reshape(k, 128, n, 128).transpose(1, 2, 0, 3).reshape(128, n, k * 128)

    x = np.concatenate([a["x_prompt"][0], a["x_sample"].reshape(-1, D)], 0)
    mix, wab = [], []
    for l in L:
        w = a["w_in"][l]
        pool, ca, cb, qkv, z = w[:, 0:512], w[:, 512:1024], w[:, 1024:1536], w[:, 1536:3072], w[:, 3072:3584]
        ab = np.stack([units(ca), units(cb)], 2).reshape(128, 8, UNIT)
        mix.append(np.concatenate([
            units(qkv), ab, units(pool), units(z), units(w[:, GATE_OFF:]),
            a["w_pool"][l].transpose(1, 0, 2).reshape(128, 1, UNIT),
            units(a["w_conv_out"][l]).reshape(128, 4, UNIT), units(a["w_dn_out"][l]).reshape(128, 4, UNIT),
            units(a["w_out"][l])], 1))
        wab.append(w[:, 3584:3592].reshape(KT, 128, 8).transpose(1, 0, 2))

    def expert(wg, wu, wd):
        gu = np.stack([units(wg), units(wu)], 2).reshape(128, 2 * FT * UNIT)
        return np.concatenate([gu, units(wd).reshape(128, 8 * FUNIT)], 1)

    hf = FT * 128
    g, u, d = a["ffn_wg"][0], a["ffn_wu"][0], a["ffn_wd"][0]
    ffn = [expert(g[:, i * hf:(i + 1) * hf], u[:, i * hf:(i + 1) * hf], d[i * hf:(i + 1) * hf]) for i in range(2)]


    def matrix(w):
        e, k, n = w.shape
        return w.reshape(e, k // 128, 128, n).transpose(0, 2, 1, 3).reshape(e, 128, -1)

    moe = np.concatenate([matrix(a[k][0]) for k in ("moe_wg", "moe_wu", "moe_wd")], 2)

    par = np.zeros((128, DEPTH, NPAR), np.float32)
    for l in L:
        for name, v in (("w_dw", _tiles(a["w_dw"][l]).transpose(0, 2, 1)), ("b_dw", _tiles(a["b_dw"][l])),
                        ("cg", _tiles(a["conv_ln_g"][l])), ("cb", _tiles(a["conv_ln_b"][l])),
                        ("w_short", _tiles(a["w_short"][l]).transpose(0, 2, 1)), ("pscale", _tiles(a["pool_scale"][l])),
                        ("dn_g", _tiles(a["dn_norm_g"][l])), ("ln1_g", _tiles(a["ln1_g"][l])), ("ln1_b", _tiles(a["ln1_b"][l])),
                        ("ln2_g", _tiles(a["ln2_g"][l])), ("ln2_b", _tiles(a["ln2_b"][l])),
                        ("a_log", np.tile(a["a_log"][l], (128, 1))), ("dt", np.tile(a["dt_bias"][l], (128, 1)))):
            o, w = PAR[name]
            par[:, l, o:o + w] = v.reshape(128, w)

    def history(s, room):
        n, b, r, c = s.shape
        s = s.reshape(n, b, r, c // 128, 128).transpose(0, 4, 3, 1, 2)
        return np.pad(s, [(0, 0)] * 4 + [(0, room)])

    arrays = {
        "x": x.reshape(T, KT, 128).transpose(2, 1, 0), "con": _constants(), "par": par,
        "w_router": a["w_router"][0].reshape(KT, 128, NE).transpose(1, 0, 2), "b_router": np.tile(a["b_router"][0], (128, 1)),
        "w_mix": np.stack(mix), "w_ab": np.stack(wab), "w_ffn": np.stack(ffn), "w_moe": moe,
        "st_qkv": history(a["state_qkv_conv"], 0), "st_conv": history(a["state_conv"], TS),
        "st_pool": history(a["state_pool"], TS), "st_delta": a["state_delta"].transpose(0, 3, 2, 1, 4),
    }
    arrays = {k: np.ascontiguousarray(v) for k, v in arrays.items()}
    outs = {
        "y": (128, KT, T), "o_conv_p": (DEPTH, 128, H, CB), "o_conv_s": (DEPTH, 128, H, NSEQ, CB + TS),
        "o_pool_p": (DEPTH, 128, H, PB), "o_pool_s": (DEPTH, 128, H, NSEQ, PB + TS),
        "o_qkv_p": (DEPTH, 128, 12, SB), "o_qkv_s": (DEPTH, 128, 12, NSEQ, SB),
        "o_delta_p": (DEPTH, 128, H, 128), "o_delta_s": (DEPTH, 128, H, NSEQ, 128),
    }
    nc = bacc.Bacc("TRN2", target_bir_lowering=False, num_devices=1)
    io = {k: nc.dram_tensor(k, v.shape, mybir.dt.from_np(v.dtype), kind="ExternalInput").ap() for k, v in arrays.items()}
    io |= {k: nc.dram_tensor(k, s, mybir.dt.float32, kind="ExternalOutput").ap() for k, s in outs.items()}
    build(nc, io)
    r = run_bass_kernel_spmd(nc, [arrays], core_ids=[0]).results[0]

    y = r["y"].transpose(2, 1, 0).reshape(T, D)

    def rows_p(s):
        return s.transpose(0, 3, 2, 1).reshape(DEPTH, 1, s.shape[3], -1)

    def rows_s(s, keep):
        return s[..., -keep:].transpose(0, 3, 4, 2, 1).reshape(DEPTH, NSEQ, keep, -1)

    return (y[:SEQ].reshape(1, SEQ, D), y[SEQ:].reshape(NSEQ, TS, D),
            rows_p(r["o_pool_p"]), rows_p(r["o_conv_p"]), rows_p(r["o_qkv_p"]),
            r["o_delta_p"].transpose(0, 2, 1, 3)[:, None],
            rows_s(r["o_pool_s"], PB), rows_s(r["o_conv_s"], CB), rows_s(r["o_qkv_s"], SB),
            r["o_delta_s"].transpose(0, 3, 2, 1, 4))
```
